# Optimizing a Trainium2 kernel written in Bass

```python
import math
import jax
import jax.numpy as jnp
from jax import lax
import numpy as np

D_MODEL = 1024
BATCH = 1
SEQ = 512
DEPTH = 2
DEC_BATCH = 8
DEC_SEQ = 4
PAST_LEN = 256
PAGE_SIZE = 128

N_A = DEPTH // 2
N_B = DEPTH - N_A
D_FF = ((8 * D_MODEL // 3 + 255) // 256) * 256
SSD_EXPAND = 2
D_INNER = SSD_EXPAND * D_MODEL
SSD_HEADDIM = 64
SSD_HEADS = D_INNER // SSD_HEADDIM
SSD_GROUPS = 8
SSD_RPG = SSD_HEADS // SSD_GROUPS
SSD_STATE = 128
CONV_W = 4
CONV_DIM = D_INNER + 2 * SSD_GROUPS * SSD_STATE
SSD_CHUNK = 128
DIL_CONFIGS = ((128, 1), (512, 4), (2048, 16))
N_DIL = 3
DIL_QH = 4
DIL_KVH = 2
DIL_QPK = DIL_QH // DIL_KVH
DIL_HD = 128
ALIBI_MAX = 8.0
N_MEM = 256
MEM_HEADS = 4
MEM_HD = 256
MEM_Q = MEM_HEADS * MEM_HD
EPS = 1e-6
SSD_IN = 2 * D_INNER + 2 * SSD_GROUPS * SSD_STATE + SSD_HEADS
IN_A = SSD_IN + MEM_Q
IN_B = N_DIL * DIL_QH * DIL_HD + MEM_Q
OUT_A = D_INNER + MEM_Q
OUT_B = DIL_QH * DIL_HD + MEM_Q
KV_SHARED = N_DIL * 2 * DIL_KVH * DIL_HD

kernel_name = 'yoco_ssd_dilated_macaron_decoder_step'

def rmsnorm(x, g):
    xf = x.astype(jnp.float32)
    y = xf * lax.rsqrt(jnp.mean(xf * xf, axis=-1, keepdims=True) + EPS)
    return (y * g.astype(jnp.float32)).astype(x.dtype)

def swiglu(h, w_gu, w_down):
    gu = h @ w_gu
    return (jax.nn.silu(gu[..., :D_FF]) * gu[..., D_FF:]) @ w_down

def alibi_slopes():
    n = N_DIL * DIL_QH
    i = jnp.arange(1, n + 1, dtype=jnp.float32)
    return jnp.exp2(-ALIBI_MAX * i / n).reshape(N_DIL, DIL_QH)

def causal_conv(xbc, conv_prev, w, b):
    L = xbc.shape[1]
    seq = jnp.concatenate([conv_prev.astype(xbc.dtype), xbc], axis=1)
    out = b + seq[:, 0:L] * w[0]
    for k in range(1, CONV_W):
        out = out + seq[:, k:k + L] * w[k]
    return jax.nn.silu(out), seq[:, L:]

def ssd_scan(x, dt, A, Bm, Cm, init, chunk):
    b, L = x.shape[:2]
    c = L // chunk
    xc = x.reshape(b, c, chunk, SSD_GROUPS, SSD_RPG, SSD_HEADDIM)
    dtc = dt.reshape(b, c, chunk, SSD_GROUPS, SSD_RPG)
    Bc = Bm.reshape(b, c, chunk, SSD_GROUPS, SSD_STATE)
    Cc = Cm.reshape(b, c, chunk, SSD_GROUPS, SSD_STATE)
    acum = jnp.cumsum(dtc * A, axis=2)
    xd = xc * dtc[..., None]
    at = jnp.moveaxis(acum, 2, -1)
    causal = jnp.tril(jnp.ones((chunk, chunk), dtype=bool))
    seg = at[..., :, None] - at[..., None, :]
    decay_ls = jnp.exp(jnp.where(causal, seg, -jnp.inf))
    cb = jnp.einsum('bclgn,bcsgn->bcgls', Cc, Bc)
    y_diag = jnp.einsum('bcgrls,bcsgrp->bclgrp', cb[:, :, :, None] * decay_ls, xd)
    decay_end = jnp.exp(acum[:, :, -1:] - acum)
    states = jnp.einsum('bclgn,bclgrp->bcgrpn', Bc, xd * decay_end[..., None]).astype(jnp.float32)
    chunk_decay = jnp.exp(acum[:, :, -1])

    def step(s, inp):
        dec, st = inp
        return s * dec[..., None, None] + st, s

    final, prev = lax.scan(step, init.astype(jnp.float32),
                           (jnp.moveaxis(chunk_decay, 1, 0), jnp.moveaxis(states, 1, 0)))
    prev = jnp.moveaxis(prev, 0, 1)
    y_off = jnp.einsum('bclgn,bcgrpn->bclgrp', Cc, prev) * jnp.exp(acum)[..., None]
    y = (y_diag + y_off).reshape(b, L, SSD_GROUPS, SSD_RPG, SSD_HEADDIM)
    return y, final

def mamba2_mix(u, conv_prev, ssm_prev, conv_w, conv_b, dt_bias, a_log, d_skip, gnorm_g, chunk):
    b, L = u.shape[:2]
    z = u[..., :D_INNER]
    xbc, conv_new = causal_conv(u[..., D_INNER:D_INNER + CONV_DIM], conv_prev, conv_w, conv_b)
    dt_raw = u[..., D_INNER + CONV_DIM:]
    xs = xbc[..., :D_INNER].reshape(b, L, SSD_GROUPS, SSD_RPG, SSD_HEADDIM)
    Bm = xbc[..., D_INNER:D_INNER + SSD_GROUPS * SSD_STATE].reshape(b, L, SSD_GROUPS, SSD_STATE)
    Cm = xbc[..., D_INNER + SSD_GROUPS * SSD_STATE:].reshape(b, L, SSD_GROUPS, SSD_STATE)
    dt = jax.nn.softplus((dt_raw + dt_bias).astype(jnp.float32)).reshape(b, L, SSD_GROUPS, SSD_RPG)
    A = -jnp.exp(a_log.astype(jnp.float32)).reshape(SSD_GROUPS, SSD_RPG)
    init = ssm_prev.reshape(b, SSD_GROUPS, SSD_RPG, SSD_HEADDIM, SSD_STATE)
    y, final = ssd_scan(xs, dt, A, Bm, Cm, init, chunk)
    y = y + d_skip.reshape(SSD_GROUPS, SSD_RPG)[..., None] * xs
    y = y.reshape(b, L, D_INNER).astype(u.dtype)
    y = rmsnorm(y * jax.nn.silu(z), gnorm_g)
    return y, conv_new, final.reshape(b, SSD_HEADS, SSD_HEADDIM, SSD_STATE).astype(ssm_prev.dtype)

def mem_kv_from(mem, g, w):
    kv = rmsnorm(mem, g) @ w
    return kv.reshape(mem.shape[0], mem.shape[1], 2, MEM_HEADS, MEM_HD)

def mem_attention(q, mem_kv):
    b, L = q.shape[:2]
    qh = q.reshape(b, L, MEM_HEADS, MEM_HD)
    s = jnp.einsum('blhd,bmhd->bhlm', qh, mem_kv[:, :, 0]).astype(jnp.float32) * (MEM_HD ** -0.5)
    p = jax.nn.softmax(s, axis=-1)
    o = jnp.einsum('bhlm,bmhd->blhd', p, mem_kv[:, :, 1].astype(jnp.float32))
    return o.reshape(b, L, MEM_Q).astype(q.dtype)

def dilated_prompt(q, kv, slopes, window, dil):
    b, S = q.shape[:2]
    nk = window // dil
    span = dil * nk
    Lp = -(-S // span) * span
    q = jnp.pad(q, ((0, 0), (0, Lp - S), (0, 0), (0, 0)))
    kv = jnp.pad(kv, ((0, 0), (0, Lp - S), (0, 0), (0, 0), (0, 0)))
    n = Lp // dil
    nb = n // nk

    def split_res(t):
        t = t.reshape((b, n, dil) + t.shape[2:])
        t = jnp.moveaxis(t, 2, 1)
        return t.reshape((b, dil, nb, nk) + t.shape[3:])

    def merge_res(t):
        rest = t.shape[4:]
        t = jnp.moveaxis(t.reshape((b, dil, n) + rest), 1, 2)
        return t.reshape((b, Lp) + rest)[:, :S]

    qr = split_res(q).reshape(b, dil, nb, nk, DIL_KVH, DIL_QPK, DIL_HD)
    kvr = split_res(kv)
    kv_prev = jnp.pad(kvr[:, :, :-1], ((0, 0), (0, 0), (1, 0), (0, 0), (0, 0), (0, 0), (0, 0)))
    kvb = jnp.concatenate([kv_prev, kvr], axis=3)
    s = jnp.einsum('bdnqkgh,bdnskh->bdnkgqs', qr, kvb[:, :, :, :, 0]).astype(jnp.float32) * (DIL_HD ** -0.5)
    du = nk + jnp.arange(nk)[:, None] - jnp.arange(2 * nk)[None, :]
    first = (jnp.arange(nb) == 0)[:, None, None] & (jnp.arange(2 * nk) < nk)[None, None, :]
    valid = (du >= 0)[None] & (du <= nk)[None] & ~first
    bias = -slopes.reshape(DIL_KVH, DIL_QPK)[:, :, None, None] * (dil * du).astype(jnp.float32)
    s = jnp.where(valid[:, None, None], s + bias, -jnp.inf)
    lse = jax.nn.logsumexp(s, axis=-1)
    p = jnp.exp(s - lse[..., None])
    o = jnp.einsum('bdnkgqs,bdnskh->bdnqkgh', p, kvb[:, :, :, :, 1].astype(jnp.float32))
    o = merge_res(o.reshape(b, dil, nb, nk, DIL_QH, DIL_HD))
    lse = merge_res(jnp.moveaxis(lse, -1, 3).reshape(b, dil, nb, nk, DIL_QH))
    return o, lse

def dilated_sample(q, kv_ext, slopes, window, dil):
    b, T = q.shape[:2]
    Lb = kv_ext.shape[1] - T
    nk = window // dil
    j = jnp.arange(nk + 1)
    idx = Lb + jnp.arange(T)[:, None] - dil * j[None, :]
    valid = idx >= 0
    kvg = kv_ext[:, jnp.maximum(idx, 0)]
    qg = q.reshape(b, T, DIL_KVH, DIL_QPK, DIL_HD)
    s = jnp.einsum('btkgh,btjkh->btkgj', qg, kvg[:, :, :, 0]).astype(jnp.float32) * (DIL_HD ** -0.5)
    bias = -slopes.reshape(DIL_KVH, DIL_QPK)[:, :, None] * (dil * j).astype(jnp.float32)
    s = jnp.where(valid[:, None, None, :], s + bias, -jnp.inf)
    lse = jax.nn.logsumexp(s, axis=-1)
    p = jnp.exp(s - lse[..., None])
    o = jnp.einsum('btkgj,btjkh->btkgh', p, kvg[:, :, :, 1].astype(jnp.float32))
    return o.reshape(b, T, DIL_QH, DIL_HD), lse.reshape(b, T, DIL_QH)

def dilated_mix(q, kv_shared, win_bufs, slopes):
    b, L = q.shape[:2]
    outs, lses = [], []
    for gi in range(N_DIL):
        window, dil = DIL_CONFIGS[gi]
        kv_g = kv_shared[:, :, gi]
        if win_bufs is None:
            o, lse = dilated_prompt(q[:, :, gi], kv_g, slopes[gi], window, dil)
        else:
            kv_ext = jnp.concatenate([win_bufs[gi].astype(kv_g.dtype), kv_g], axis=1)
            o, lse = dilated_sample(q[:, :, gi], kv_ext, slopes[gi], window, dil)
        outs.append(o)
        lses.append(lse)
    o = jnp.stack(outs, axis=2)
    alpha = jax.nn.softmax(jnp.stack(lses, axis=2), axis=2)
    y = jnp.sum(alpha[..., None] * o, axis=2)
    return y.reshape(b, L, DIL_QH * DIL_HD).astype(q.dtype)

def trunk(x, mem_kv, conv_prev, ssm_prev, win_bufs, ssd_chunk, norm_g, w_ffn_gu, w_ffn_down,
          w_in_a, conv_w, conv_b, dt_bias, a_log, d_skip, ssd_norm_g, w_out_a, w_in_b, w_out_b,
          kv_norm_g, w_kv_shared, final_norm_g):
    b, L = x.shape[:2]
    slopes = alibi_slopes()
    conv_new, ssm_new = [], []
    kv_shared = None
    for l in range(DEPTH):
        g = norm_g[l]
        x = x + 0.5 * rmsnorm(swiglu(rmsnorm(x, g[0]), w_ffn_gu[l, 0], w_ffn_down[l, 0]), g[1])
        h = rmsnorm(x, g[2])
        if l < N_A:
            u = h @ w_in_a[l]
            y_mix, cn, sn = mamba2_mix(u[..., :SSD_IN], conv_prev[l], ssm_prev[l], conv_w[l], conv_b[l],
                                       dt_bias[l], a_log[l], d_skip[l], ssd_norm_g[l], ssd_chunk)
            conv_new.append(cn)
            ssm_new.append(sn)
            q_mem = u[..., SSD_IN:]
            w_out = w_out_a[l]
        else:
            i = l - N_A
            u = h @ w_in_b[i]
            q_dil = u[..., :N_DIL * DIL_QH * DIL_HD].reshape(b, L, N_DIL, DIL_QH, DIL_HD)
            y_mix = dilated_mix(q_dil, kv_shared, win_bufs, slopes)
            q_mem = u[..., N_DIL * DIL_QH * DIL_HD:]
            w_out = w_out_b[i]
        y = jnp.concatenate([y_mix, mem_attention(q_mem, mem_kv[l])], axis=-1) @ w_out
        x = x + rmsnorm(y, g[3])
        x = x + 0.5 * rmsnorm(swiglu(rmsnorm(x, g[4]), w_ffn_gu[l, 1], w_ffn_down[l, 1]), g[5])
        if l == N_A - 1:
            kv_shared = (rmsnorm(x, kv_norm_g) @ w_kv_shared).reshape(b, L, N_DIL, 2, DIL_KVH, DIL_HD)
    return rmsnorm(x, final_norm_g), jnp.stack(conv_new), jnp.stack(ssm_new), kv_shared

def setup_inputs(seed: int = 0) -> dict:
    key = jax.random.key(seed)
    ks = jax.random.split(key, 32)
    f32 = jnp.float32

    def nrm(k, shape, scale):
        return jax.random.normal(k, shape, f32) * scale

    def gain(k, shape):
        return 1.0 + 0.05 * jax.random.normal(k, shape, f32)

    wl = [min(w, PAST_LEN) for w, _ in DIL_CONFIGS]
    dt0 = jnp.exp(jax.random.uniform(ks[10], (N_A, SSD_HEADS), f32, math.log(1e-3), math.log(1e-1)))
    return {
        'x_prompt': nrm(ks[0], (BATCH, SEQ, D_MODEL), 1.0),
        'x_sample': nrm(ks[1], (DEC_BATCH, DEC_SEQ, D_MODEL), 1.0),
        'mem_prompt': nrm(ks[2], (BATCH, N_MEM, D_MODEL), 1.0),
        'cache_mem_kv': nrm(ks[3], (DEPTH, DEC_BATCH, N_MEM, 2, MEM_HEADS, MEM_HD), 1.0),
        'state_ssm': nrm(ks[4], (N_A, DEC_BATCH, SSD_HEADS, SSD_HEADDIM, SSD_STATE), 0.1),
        'state_conv': nrm(ks[5], (N_A, DEC_BATCH, CONV_W - 1, CONV_DIM), 1.0),
        'cache_win_g1': nrm(ks[6], (DEC_BATCH, wl[0], 2, DIL_KVH, DIL_HD), 1.0),
        'cache_win_g2': nrm(ks[7], (DEC_BATCH, wl[1], 2, DIL_KVH, DIL_HD), 1.0),
        'cache_win_g3': nrm(ks[8], (DEC_BATCH, wl[2], 2, DIL_KVH, DIL_HD), 1.0),
        'norm_g': gain(ks[9], (DEPTH, 6, D_MODEL)),
        'w_ffn_gu': nrm(ks[11], (DEPTH, 2, D_MODEL, 2 * D_FF), D_MODEL ** -0.5),
        'w_ffn_down': nrm(ks[12], (DEPTH, 2, D_FF, D_MODEL), D_FF ** -0.5),
        'w_in_a': nrm(ks[13], (N_A, D_MODEL, IN_A), D_MODEL ** -0.5),
        'conv_w': nrm(ks[14], (N_A, CONV_W, CONV_DIM), CONV_W ** -0.5),
        'conv_b': nrm(ks[15], (N_A, CONV_DIM), 0.01),
        'dt_bias': dt0 + jnp.log(-jnp.expm1(-dt0)),
        'a_log': jnp.log(jax.random.uniform(ks[16], (N_A, SSD_HEADS), f32, 1.0, 16.0)),
        'd_skip': gain(ks[17], (N_A, SSD_HEADS)),
        'ssd_norm_g': gain(ks[18], (N_A, D_INNER)),
        'w_out_a': nrm(ks[19], (N_A, OUT_A, D_MODEL), OUT_A ** -0.5),
        'w_in_b': nrm(ks[20], (N_B, D_MODEL, IN_B), D_MODEL ** -0.5),
        'w_out_b': nrm(ks[21], (N_B, OUT_B, D_MODEL), OUT_B ** -0.5),
        'kv_norm_g': gain(ks[22], (D_MODEL,)),
        'w_kv_shared': nrm(ks[23], (D_MODEL, KV_SHARED), D_MODEL ** -0.5),
        'mem_norm_g': gain(ks[24], (DEPTH, D_MODEL)),
        'w_mem_kv': nrm(ks[25], (DEPTH, D_MODEL, 2 * MEM_Q), D_MODEL ** -0.5),
        'final_norm_g': gain(ks[26], (D_MODEL,)),
    }

def reference(x_prompt, x_sample, mem_prompt, cache_mem_kv, state_ssm, state_conv, cache_win_g1,
              cache_win_g2, cache_win_g3, norm_g, w_ffn_gu, w_ffn_down, w_in_a, conv_w, conv_b,
              dt_bias, a_log, d_skip, ssd_norm_g, w_out_a, w_in_b, w_out_b, kv_norm_g, w_kv_shared,
              mem_norm_g, w_mem_kv, final_norm_g):
    bp, S = x_prompt.shape[:2]
    mem_kv_p = jnp.stack([mem_kv_from(mem_prompt, mem_norm_g[l], w_mem_kv[l]) for l in range(DEPTH)])
    conv0 = jnp.zeros((N_A, bp, CONV_W - 1, CONV_DIM), x_prompt.dtype)
    ssm0 = jnp.zeros((N_A, bp, SSD_HEADS, SSD_HEADDIM, SSD_STATE), x_prompt.dtype)
    y_prompt, conv_p, ssm_p, kv_p = trunk(
        x_prompt, mem_kv_p, conv0, ssm0, None, min(SSD_CHUNK, S), norm_g, w_ffn_gu, w_ffn_down,
        w_in_a, conv_w, conv_b, dt_bias, a_log, d_skip, ssd_norm_g, w_out_a, w_in_b, w_out_b,
        kv_norm_g, w_kv_shared, final_norm_g)
    win_p = [kv_p[:, S - min(w, S):, gi] for gi, (w, _) in enumerate(DIL_CONFIGS)]
    y_sample, conv_s, ssm_s, kv_s = trunk(
        x_sample, cache_mem_kv, state_conv, state_ssm, (cache_win_g1, cache_win_g2, cache_win_g3),
        x_sample.shape[1], norm_g, w_ffn_gu, w_ffn_down, w_in_a, conv_w, conv_b, dt_bias, a_log,
        d_skip, ssd_norm_g, w_out_a, w_in_b, w_out_b, kv_norm_g, w_kv_shared, final_norm_g)
    return (y_prompt, y_sample, mem_kv_p, ssm_p, conv_p, win_p[0], win_p[1], win_p[2],
            ssm_s, conv_s, kv_s[:, :, 0], kv_s[:, :, 1], kv_s[:, :, 2])


_drawn_inputs = setup_inputs


def setup_inputs(seed=0):
    import zlib

    import numpy as np

    out = dict(_drawn_inputs(seed))
    spreads = {}
    factors = {'conv_b': 3.524, 'd_skip': 2.669}
    for name, (base, spread) in spreads.items():
        noise = np.random.default_rng([zlib.crc32(name.encode()), seed]).standard_normal(out[name].shape)
        drawn = base * np.exp(spread * noise) if base else spread * noise
        out[name] = jnp.asarray(drawn.astype(out[name].dtype))
    for name, factor in factors.items():
        out[name] = (out[name] * factor).astype(out[name].dtype)
    return out
```

```python
from contextlib import ExitStack

import numpy as np

import concourse.bass as bass
from concourse import mybir

F32 = mybir.dt.float32
F32R = mybir.dt.float32r
ACT = mybir.ActivationFunctionType
ALU = mybir.AluOpType
AX_X = mybir.AxisListType.X

P = 128
D = 1024
KD = D // P
SEQ, NB, NT = 512, 8, 4
NS = NB * NT
T = SEQ + NS
HT = T // 2
HP = SEQ - HT
FF = 2816
KF = FF // P
DEPTH = 2
DI = 2048
KI = DI // P
NH, NG, RPG, PD = 32, 8, 4, 64
NCH = SEQ // P
CONV_DIM = 4096
CW = 4
XBC0 = DI
DT0 = DI + CONV_DIM
QM0 = DT0 + NH
NM, MH, MD = 256, 4, 256
GD = 3
QH, KVH, HD = 4, 2, 128
DILS = ((128, 1), (512, 4), (2048, 16))
WINS = (128, 256, 256)
EPS = 1e-6
BIG = 1e30
NEW0 = 448
U = 8 * P


def constants():
    p = np.arange(P)
    ident = np.eye(P, dtype=np.float32)
    ones = np.ones((P, P), np.float32)
    causal = (p[:, None] <= p[None, :]).astype(np.float32)
    s = np.arange(NS)
    small = np.zeros((P, NS), np.float32)
    small[:NS] = (s[:, None] <= s[None, :]) & (s[:, None] // NT == s[None, :] // NT)
    own = np.zeros((P, NB), np.float32)
    own[:NS] = s[:, None] // NT == np.arange(NB)[None, :]
    eps = np.full((P, 1), EPS, np.float32)
    slope = 2.0 ** (-8.0 * np.arange(1, GD * QH + 1) / (GD * QH)).reshape(GD, QH)
    neg = -slope[:, (p // NT) % QH].T.astype(np.float32)
    base = np.concatenate([ident, ones, causal, small, own, eps, neg], 1).astype(np.float32)
    dist = 384 + p[:, None] - np.arange(SEQ)[None, :]
    tabs = []
    for w, dil in DILS:
        ok = (dist >= 0) & (dist <= w) & (dist % dil == 0)
        tabs.append(np.where(ok, dist, BIG))
    t, b = (p % NT)[:, None], (p // (NT * QH))[:, None]
    e = np.arange(P)[None, :]
    c1 = np.where(e >= t, 128 + t - e, BIG)
    e = np.arange(256)[None, :]
    c2 = np.where((e - t) % 4 == 0, 256 + t - e, BIG)
    r, a = np.arange(64)[None, :] // 16, np.arange(64)[None, :] % 16
    c3 = np.where(r == t, 256 + t - 16 * a - r, BIG)
    bb, tt = s[None, :] // NT, s[None, :] % NT
    new = [np.where((bb == b) & (tt <= t) & ((t - tt) % dil == 0), t - tt, BIG) for _, dil in DILS]
    dilc = np.concatenate(tabs + [c1, c2, c3] + new, 1).astype(np.float32)
    reset = np.ones((NH, T), np.float32)
    reset[:, 0:SEQ:P] = 0
    reset[:, SEQ::NT] = 0
    return base, dilc, reset


NBASE = 3 * P + NS + NB + 1 + GD
NDIL = GD * SEQ + NEW0 + GD * NS
SLOPES = [[2.0 ** (-8.0 * (g * QH + h + 1) / (GD * QH)) for h in range(QH)] for g in range(GD)]


class Dense:

    def __init__(self, plan, n, tiles, nks, xk=1):
        self.n, self.tiles, self.nks = n, tiles, nks
        self.k0 = [sum(nks[:q]) for q in range(len(nks))]
        self.ub = tiles * len(nks)
        self.u0 = plan["units"]
        plan["units"] += n * self.ub
        assert n == 1 or self.ub % 2 == 0


class Tally:

    def __init__(self):
        self.sq = self.norm = self.t = self.res = 0
        self.unscaled = 0


def step_loop(eng, n, body):
    with eng.Fori(0, n) as i:
        body(i)


CREDITS = (("group_end", 1), ("taps", 2), ("cvn_done", 2), ("nst_free", 1))

SEMS = """const_in x_in row_in cols_out x_tr mem_in mem_sq mem_rt mem_rb mem_sc mem_tr mem_ev
 w_hi w_lo w_mm evac0 evac1 evac2 evac3 mid_hi mid_lo sq_ready sq_used rt_ready rb_ready
 t_ready hi_ready lo_ready pn_t x_done blk_evac blk_out stage_free w_in0 w_in1 f_tr f_ev y_out
 conv_in hist_tr dt_ab dt_e dt_u dt_ln dt_v scan_done dtt_tr alb_sub de_done na_ready
 col_g hist_g tap0 taps conv_done cvn_done tok_ready cb_ready cvt_ready small_read btok_ready
 xd_ready xdd_ready cbm_ready bcs_ready bcs_read st_ready st_done bc_ready bc_read seg_ready lexp m_ready
 c_ready s0_in s0t_ready s0t_evac yoff_ready yos_ready news_ready news_read news_out cds_exp final_ready
 final_read y_ready cz_ready bz_ready cvo_done group_end ve rest_out qm0 pz hist_copied y_used nst_free group_out passed
 kv_in0 kv_in1 kv_in2 att_go kt_tr kt_ev sc_ready mx_ready p_exp p_rcp p_ready ptr_ready pt_evac pv_ready pv_evac
 q_ready ks_tr ks_ev ss_ready smx s_exp s_rcp s_p s_tr pz_ready vb_done so_ev so_tr att_done qz_zero
 dil_in dkt_tr dkt_ev ds_ready ds_ev dmx dexp drcp dp_ready dptr dpt_ev do_ready do_ev
 dks_in dv_in dks_tr dks_ev dss_ready qn_zero qn_done qd_zero qd_done dil_done
""".split()


def build_trunk(nc, A, O):
    with ExitStack() as ctx:
        s = {n: ctx.enter_context(nc.semaphore(n)) for n in SEMS}
        evac = [s[f"evac{j}"] for j in range(4)]
        w_in = [s["w_in0"], s["w_in1"]]

        top = [16512]

        def keep(name, shape, dt=F32):
            t = nc.alloc_sbuf_tensor_at(name, shape, dt, offset=top[0])
            size = 4
            for d in shape[1:]:
                size *= d
            top[0] += (size + 31) // 32 * 32
            return t

        con = keep("con", [P, NBASE])
        G = keep("G", [P, P])
        GH = keep("GH", [P, P])
        CWT = keep("CWT", [P, P])
        CB = keep("CB", [P, 48])
        DC = keep("DC", [P, KI])
        dtb = keep("dtb", [NH, 1])
        alog = keep("alog", [NH, 1])
        rb = keep("rb", [P, T])
        xT = keep("xT", [P, KD, T])
        raw = keep("raw", [P, 2, U])
        whi = keep("whi", [P, 2, U], F32R)
        wlo = keep("wlo", [P, 2, U], F32R)
        H0 = top[0]
        hH = keep("hH", [P, KD, T], F32R)
        hL = keep("hL", [P, KD, T], F32R)
        Y0 = top[0]
        yT = keep("yT", [P, KD, T])
        M10 = top[0]
        L24 = keep("L24", [P, 24, T], F32R)
        M20 = top[0]
        H24 = keep("H24", [P, 24, T], F32R)
        E0 = top[0]
        tile_b = T * 4

        def at(name, shape, offset, dt=F32):
            return nc.alloc_sbuf_tensor_at(name, shape, dt, offset=offset)

        M1 = at("M1", [P, 24, T], M10)
        sqb = at("sqb", [P, 2, T], H0 + 8 * tile_b)
        rt = at("rt", [P, T], H0 + 10 * tile_b)
        sg = at("sg", [P, 2, T], Y0)
        prod = at("prod", [P, 2, T], Y0 + 2 * tile_b)
        rows = at("rows", [P, 3, P], Y0)
        xnat = at("xnat", [P, NCH + 1, D], M10)
        memnat = at("memnat", [P, 2, D], M20)
        memT = at("memT", [P, KD, NM], M20 + 8192)
        memsq = at("memsq", [P, D], M20 + 16384)
        mst = at("mst", [P, 8], M20 + 20480)
        stage = at("stage", [P, NCH + 1, 512], M10 + 20480)

        ident, ones = con[:, 0:P], con[:, P:2 * P]
        causal = con[:, 2 * P:3 * P]
        small = con[0:NS, 3 * P:3 * P + NS]
        own = con[0:NS, 3 * P + NS:3 * P + NS + NB]
        epsc = con[:, 3 * P + NS + NB:3 * P + NS + NB + 1]
        negc = con[:, 3 * P + NS + NB + 1:NBASE]

        PS = ctx.enter_context(nc.psum_tensor("PS", [P, 8, 512], F32))
        kvs = nc.dram_tensor("kvs", (T, GD * 512), F32).ap()

        plan = {"units": 0}
        ph = {}
        for l in range(DEPTH):
            ph["mem", l] = Dense(plan, 4, 1, (2, 2, 2, 2))
        for l in range(DEPTH):
            ph["gu", l, 0] = Dense(plan, 11, 4, (8,))
            ph["down", l, 0] = Dense(plan, 4, 2, (8, 7, 7))
            if l == 0:
                ph["dt"] = Dense(plan, 1, 1, (8,))
                ph["ssd"] = Dense(plan, NG, 6, (8,))
                ph["qm", 0] = Dense(plan, 4, 2, (8,))
                ph["out", 0] = Dense(plan, 4, 2, (8, 8, 8))
            else:
                ph["in_b"] = Dense(plan, 6, 2, (8,))
                ph["qm", 1] = Dense(plan, 4, 2, (8,))
                ph["out", 1] = Dense(plan, 4, 2, (6, 6))
            ph["gu", l, 1] = Dense(plan, 11, 4, (8,))
            ph["down", l, 1] = Dense(plan, 4, 2, (8, 7, 7))
            if l == 0:
                ph["kv"] = Dense(plan, 3, 1, (2, 2, 2, 2))
        last_unit = plan["units"] - 1

        def gain(l, i):
            return lambda k: G[:, (6 * l + i) * KD + k:(6 * l + i) * KD + k + 1]

        def half_gain(l, i):
            return lambda k: GH[:, (6 * l + i) * KD + k:(6 * l + i) * KD + k + 1]

        def col(c):
            return lambda k: G[:, c + k:c + k + 1]

        x_of = lambda k: xT[:, k, :]
        y_of = lambda k: yT[:, k, :]
        hH_of = lambda k: hH[:, k, :]
        hL_of = lambda k: hL[:, k, :]

        class Place(Tally):
            def __init__(self):
                super().__init__()
                self.ev = [0, 0, 0, 0]
                self.mid = self.blk = self.out = 0
                self.a = 0

        class Arena:
            def __init__(self, *regions):
                self.regions = [list(r) for r in regions]

            def __call__(self, name, shape, dt=F32):
                size = 4
                for d in shape[1:]:
                    size *= d
                size = (size + 31) // 32 * 32
                for r in self.regions:
                    if r[1] - r[0] >= size:
                        r[0] += size
                        return at(name, shape, r[0] - size, dt)
                raise ValueError(name)

        A1 = Arena([M20, E0], [Y0, M10], [M10 + 16 * tile_b, M20], [E0, 229344])
        xbc = A1("xbc", [P, 4, T])
        S0 = A1("S0", [P, 2, NB, P])
        S0T = A1("S0T", [P, NB, 256])
        xd = A1("xd", [P, NCH + 1, 256])
        xdd = A1("xdd", [P, NCH + 1, 256])
        sz = A1("sz", [P, 2, T])
        Lh = A1("Lh", [P, 2, T])
        ST = A1("ST", [P, NCH, 256])
        BZ = A1("BZ", [NS, NB, P])
        nst = A1("nst", [P, NB, P])
        pre = A1("pre", [P, 2, SEQ + CW - 1])
        pres = A1("pres", [P, 2, NB, NT + CW - 1])
        bcS = A1("bcS", [P, 2, SEQ])
        Eh = A1("Eh", [P, 2, SEQ])
        hist = A1("hist", [P, 32, NB * 3])
        btok = A1("btok", [P, NCH + 1, P])
        cbm = A1("cbm", [P, T])
        cvo = A1("cvo", [27, 4, P])
        CZ = A1("CZ", [P, NB, NS])
        tmpS = A1("tmpS", [P, 256])
        cvn = A1("cvn", [P, 4, 32])
        yos = A1("yos", [NS, 256])
        sso = A1("sso", [P, 2, P])
        bcsS = A1("bcsS", [NS, QH, NS])
        cds = A1("cds", [P, 2 * NB])
        acum = A1("acum", [NH, T])
        dtx = A1("dtx", [NH, T])
        selp = A1("selp", [NH, 4, PD])
        selg = A1("selg", [NH, 4])
        aT = A1("aT", [P, NCH + 1, NH])
        dT = A1("dT", [P, NCH + 1, NH])
        DE = A1("DE", [P, NCH + 1, NH])
        CD = A1("CD", [P, NCH + 1, NH])
        EAS = A1("EAS", [NS, NH])
        aTg = A1("aTg", [P, NCH + 1, 4])
        dTg = A1("dTg", [P, NCH + 1, 4])
        DEg = A1("DEg", [P, NCH + 1, 4])
        CDg = A1("CDg", [P, NCH + 1, 4])
        EASg = A1("EASg", [NS, 4])
        DCg = A1("DCg", [P, 2])
        cwg = A1("cwg", [P, 4, 8])
        nA = A1("nA", [NH, 1])
        tmpL = A1("tmpL", [NH, NS])
        cvin = at("cvin", [NB * 3, CONV_DIM], M20 + 4 * tile_b)
        dts = at("dts", [NH, 6, T], M20 + 4 * tile_b + 16384 + 4096)
        reset = at("reset", [NH, T], M20 + 4 * tile_b + 16384 + 4096 + 6 * tile_b)
        A2 = Arena([M20, E0], [H0, Y0], [E0, 229344])
        QZ = A2("QZ", [P, 8, NB, P])
        PZ = A2("PZ", [P, 2, NB, P])
        Pb = A2("Pb", [P, NCH, NM])
        Ob = at("Ob", [P, NCH * NM], M20 + 32768 + 8192)
        PT = A2("PT", [P, 2, SEQ])
        kvr = A2("kvr", [P, 3, 2, D])
        KT = [A2(f"KT{j}", [P, 4, NM]) for j in range(4)]
        am = A2("am", [P, 2, NCH])
        ar = A2("ar", [P, 2, NCH])
        ai = A2("ai", [P, 2, NCH])
        A3 = Arena([M20, 229344])
        A4 = Arena([H0, M10])
        kvd = A3("kvd", [P, NCH, GD * 512])
        Kc = A3("Kc", [P, NB, 4, 256])
        KTd = A4("KTd", [P, 2 * GD, SEQ])
        tab = A4("tab", [P, NDIL])
        SS = A4("SS", [P, 2, 10 * P])
        PTd = A4("PTd", [P, 2, 10 * P])
        kvn = A4("kvn", [NS, GD * 512])
        KTn = A4("KTn", [P, 2 * GD, NS])
        QN = A4("QN", [P, 2 * GD, P])
        dm = A4("dm", [P, 2])
        dr = A4("dr", [P, 2])
        di = A4("di", [P, 2])
        ss_at = H0 + 2 * GD * SEQ * 4 + NDIL * 4
        QZD = at("QZD", [P, 2 * GD, NB, P], M20)
        PTn = at("PTn", [NS, GD, P], ss_at + 5120)
        Od = at("Od", [P, 256], ss_at + 5120 + 1536)
        KTb = at("KTb", [P, 4, NEW0], ss_at + 2 * 5120)
        OLD = ((0, 0, P), (1, P, 3 * P), (2, 3 * P, NEW0))

        def spans(i):
            return [(g, f, (i + 1 - f) * P) for g, f in ((0, max(0, i - 1)), (1, 0), (2, 0))]
        CT = lambda g: (16 + g, 24 + g, 2 * g, 2 * g + 1)
        POS = (0, 1, 2, 3, 0, 1)
        VE = 39

        class Steps:

            def __init__(self, eng, sem, base):
                self.eng, self.sem, self.base, self.n = eng, sem, base, 0

            def __call__(self, ins):
                ins.then_inc(self.sem, 1)
                self.n += 1

            def wait(self):
                self.eng.wait_ge(self.sem, self.base + self.n)

        block = ctx.enter_context(nc.Block())

        @block.sync
        def _(sp):
            sp.dma_start(con[:, :], A["c_base"]).then_inc(s["const_in"], 16)
            ng = A["norm_g"].rearrange("l i (k p) -> (l i k) p", p=P)
            for r0, src in ((0, ng), (96, A["kv_norm_g"].rearrange("(k p) -> k p", p=P)),
                            (104, A["mem_norm_g"].rearrange("l (k p) -> (l k) p", p=P)),
                            (120, A["final_norm_g"].rearrange("(k p) -> k p", p=P))):
                sp.dma_start(rows[r0:r0 + src.shape[0], 0, :], src).then_inc(s["const_in"], 16)
            sp.dma_start(rows[:, 1, :], A["conv_w"].rearrange("a w (k p) -> (a w k) p", p=P)).then_inc(s["const_in"], 16)
            sp.dma_start(rows[0:32, 2, :], A["conv_b"].rearrange("a (k p) -> (a k) p", p=P)).then_inc(s["const_in"], 16)
            sp.dma_start(rows[32:48, 2, :], A["ssd_norm_g"].rearrange("a (k p) -> (a k) p", p=P)).then_inc(s["const_in"], 16)
            sp.dma_start(memnat[:, :, :], A["mem_prompt"].rearrange("a (t p) d -> p (a t) d", p=P)).then_inc(s["mem_in"], 16)

            def load(u, slot, src, nk, cols=P, passed=False):
                sp.wait_ge(s["w_lo"], u + 1)
                if passed:
                    sp.sem_inc(s["passed"], 1)
                sp.dma_start(raw[:, slot, 0:nk * cols].rearrange("p (k n) -> p k n", k=nk), src).then_inc(w_in[slot], 16)

            def kview(w):
                return w.rearrange("(k p) n -> p k n", p=P)

            def wide(d, w):
                def body(i):
                    for q in range(4):
                        load(d.u0 + i * 4 + q, (d.u0 + q) % 2, kview(w)[:, 2 * q:2 * q + 2, bass.ds(i * 512, 512)], 2, 512)
                step_loop(sp, d.n, body)

            for l in range(DEPTH):
                wide(ph["mem", l], A["w_mem_kv"][l])

            def narrow(d, w):
                def body(i):
                    for j in range(2):
                        for q, nk in enumerate(d.nks):
                            u = j * len(d.nks) + q
                            load(d.u0 + i * d.ub + u, (d.u0 + u) % 2, w[:, d.k0[q]:d.k0[q] + nk, bass.ds(i * 256 + j * P, P)], nk)
                step_loop(sp, d.n, body)

            def ffn(l, f):
                d = ph["gu", l, f]
                wg = kview(A["w_ffn_gu"][l, f])

                def gu(i):
                    for j in range(4):
                        c = i * 256 + (j // 2) * P + (j % 2) * FF
                        load(d.u0 + i * 4 + j, (d.u0 + j) % 2, wg[:, :, bass.ds(c, P)], KD)
                step_loop(sp, d.n, gu)
                dn = ph["down", l, f]
                wd = kview(A["w_ffn_down"][l, f])

                def down(i):
                    for j in range(2):
                        for q in range(3):
                            u = 3 * j + q
                            load(dn.u0 + i * 6 + u, (dn.u0 + u) % 2, wd[:, dn.k0[q]:dn.k0[q] + dn.nks[q], bass.ds(i * 256 + j * P, P)], dn.nks[q])
                step_loop(sp, dn.n, down)

            for l in range(DEPTH):
                ffn(l, 0)
                if l == 0:
                    wa = kview(A["w_in_a"][0])
                    u0 = ph["dt"].u0
                    load(u0, u0 % 2, wa[:, :, DT0:DT0 + P], KD)
                    sp.wait_ge(s["qm0"], 1)
                    sp.dma_start(cvin[:, :], A["state_conv"].rearrange("a b r c -> (a b r) c")).then_inc(s["conv_in"], 16)
                    sp.dma_start(reset[:, :], A["c_reset"]).then_inc(s["conv_in"], 16)
                    d = ph["ssd"]
                    s0v = A["state_ssm"].rearrange("a b (g q r) p n -> g q (r p) (a b) n", g=NG, q=2)

                    def group(g):
                        for j, c in enumerate((XBC0 + DI + g * P, XBC0 + DI + D + g * P, XBC0 + g * 256, XBC0 + g * 256 + P, g * 256, g * 256 + P)):
                            load(d.u0 + g * 6 + j, (d.u0 + j) % 2, wa[:, :, bass.ds(c, P)], KD, passed=True)
                            if j == 2:
                                sp.wait_ge(s["hist_copied"], 1)
                                sp.wait_ge(s["group_end"], g + 1)
                                sp.sem_inc(s["passed"], 1)
                                for q in range(2):
                                    sp.dma_start(S0[:, q], s0v[bass.ds(g, 1), q].rearrange("o p b n -> p (o b) n")).then_inc(s["s0_in"], 16)
                    step_loop(sp, NG, group)
                    d1 = ph["qm", 0]

                    def queries(i):
                        for j in range(2):
                            load(d1.u0 + i * 2 + j, (d1.u0 + j) % 2, wa[:, :, bass.ds(i * 256 + (QM0 + j * P), P)], KD)
                    step_loop(sp, d1.n, queries)
                    narrow(ph["out", 0], kview(A["w_out_a"][0]))
                else:
                    wb = kview(A["w_in_b"][0])
                    for d, c0 in ((ph["in_b"], 0), (ph["qm", 1], GD * QH * HD)):
                        def queries(i, d=d, c0=c0):
                            for j in range(2):
                                load(d.u0 + i * 2 + j, (d.u0 + j) % 2, wb[:, :, bass.ds(i * 256 + (c0 + j * P), P)], KD)
                        step_loop(sp, d.n, queries)
                    narrow(ph["out", 1], kview(A["w_out_b"][0]))
                ffn(l, 1)
                if l == 0:
                    wide(ph["kv"], A["w_kv_shared"])
            sp.wait_ge(s["y_out"], 32)

        @block.scalar
        def _(act):
            n = Place()

            def split(u, slot, nk=8):
                act.wait_ge(w_in[slot], (u // 2 + 1) * 16 if isinstance(u, int) else u * 8 + (16 if slot == 0 else 8))
                act.wait_ge(s["w_mm"], u + 1)
                act.activation(whi[:, slot, 0:nk * P], raw[:, slot, 0:nk * P], ACT.Copy).then_inc(s["w_hi"], 1)

            def stats(src, ready, nk, dm):
                for k in range(nk):
                    ready(k)
                    act.wait_ge(s["sq_used"], n.sq + k + 1)
                    act.activation(sqb[:, k % 2, :], src(k), ACT.Square).then_inc(s["sq_ready"], 1)
                n.sq += nk
                act.wait_ge(s["sq_used"], n.sq + 2)
                act.activation(rt[:, :].rearrange("p (h t) -> p h t", h=2), PS[:, 4:6, 0:HT], ACT.Sqrt,
                               bias=epsc, scale=1.0 / dm).then_inc(s["rt_ready"], 1)
                n.norm += 1

            def highs(tmp, hi, nk):
                for k in range(nk):
                    act.wait_ge(s["t_ready"], n.t + k + 1)
                    act.activation(hi(k), tmp(k), ACT.Copy).then_inc(s["hi_ready"], 1)
                n.t += nk

            def x_ready(k):
                act.wait_ge(s["x_done"], n.res + k + 1)

            act.nop().then_inc(s["w_mm"], 2)
            act.nop().then_inc(s["w_lo"], 2)
            act.nop().then_inc(s["sq_used"], 2)
            act.nop().then_inc(s["mid_lo"], 2)
            act.nop().then_inc(s["blk_evac"], 1)
            act.nop().then_inc(s["stage_free"], 1)
            for j in range(4):
                act.nop().then_inc(evac[j], 1)
            for name, k in CREDITS:
                act.nop().then_inc(s[name], k)
            act.dma_start(xnat[:, 0:NCH, :], A["x_prompt"].rearrange("a (t p) d -> p (a t) d", p=P)).then_inc(s["x_in"], 16)
            act.dma_start(xnat[0:NS, NCH, :], A["x_sample"].rearrange("b t d -> (b t) d")).then_inc(s["x_in"], 16)
            act.dma_start(dtb[:, :], A["dt_bias"].rearrange("a (h o) -> (a h) o", o=1)).then_inc(s["const_in"], 16)
            act.dma_start(alog[:, :], A["a_log"].rearrange("a (h o) -> (a h) o", o=1)).then_inc(s["const_in"], 16)
            for r in range(2):
                src = A["d_skip"]
                src = bass.AP(src.tensor, src.offset + r, [[0, PD], [2, KI]])
                act.dma_start(DC[r * PD:(r + 1) * PD, :], src, allow_slow_non_contiguous=True).then_inc(s["const_in"], 16)

            act.wait_ge(s["mem_in"], 16)
            act.wait_ge(s["const_in"], 12 * 16)
            for t in range(2):
                if t:
                    act.wait_ge(s["mem_sq"], 1)
                act.activation(memsq[:, :], memnat[:, t, :], ACT.Square, accum_out=mst[:, t:t + 1]).then_inc(s["mem_sq"], 1)
            act.wait_ge(s["mem_sq"], 2)
            act.activation(mst[:, 2:4], mst[:, 0:2], ACT.Sqrt, bias=epsc, scale=1.0 / D).then_inc(s["mem_rt"], 1)
            split(0, 0)
            for k in range(KD):
                act.wait_ge(s["mem_tr"], k + 1)
                act.activation(memT[:, k, :], PS[:, k % 2, 0:NM], ACT.Copy).then_inc(s["mem_ev"], 1)

            def wide(d):
                def body(i):
                    for q in range(4):
                        split(d.u0 + i * 4 + q + 1, (d.u0 + q + 1) % 2)
                step_loop(act, d.n, body)

            for l in range(DEPTH):
                if l:
                    act.wait_ge(s["w_mm"], ph["mem", l].u0 + 2)
                highs(lambda k: yT[:, k, 0:NM], lambda k: hH[:, k, 0:NM], KD)
                wide(ph["mem", l])
            for k in range(KD):
                act.wait_ge(s["x_tr"], k + 1)
                b = 2 * (k % 3) + 2
                act.activation(xT[:, k, 0:SEQ], PS[:, b, :], ACT.Copy)
                act.activation(xT[:, k, SEQ:T], PS[:, b + 1, 0:NS], ACT.Copy).then_inc(s["x_done"], 1)

            def to_h():
                stats(x_of, x_ready, KD, D)
                highs(y_of, hH_of, KD)

            def narrow(d):
                def body(i):
                    for u in range(d.ub):
                        split(d.u0 + i * d.ub + u + 1, (d.u0 + u + 1) % 2, (d.nks * 2 + (8,))[u + 1])
                step_loop(act, d.n, body)

            def out_stats(d):
                stats(y_of, lambda k: act.wait_ge(evac[k % 2], n.ev[k % 2] + k // 2 + 2), KD, D)
                for j in range(2):
                    n.ev[j] += d.n
                n.res += KD

            def attention(l):
                act.wait_ge(s["kt_tr"], l + 1)
                for k in range(2):
                    act.activation(KT[k][:, :, :], PS[:, 2 * k:2 * k + 2, :].rearrange("p a (j m) -> p (a j) m", j=2), ACT.Copy).then_inc(s["kt_ev"], 1)
                for h in range(MH):
                    act.wait_ge(s["mx_ready"], MH * l + h + 1)
                    if h:
                        act.wait_ge(s["ptr_ready"], MH * l + h)
                    for r in range(NCH):
                        ins = act.activation(Pb[:, r, :], PS[:, 4 + 2 * (h % 2) + r // 2, (r % 2) * NM:(r % 2 + 1) * NM], ACT.Exp, bias=am[:, h % 2, r:r + 1], accum_out=ar[:, h % 2, r:r + 1])
                    ins.then_inc(s["p_exp"], 1)
                    act.wait_ge(s["ptr_ready"], MH * l + h + 1)
                    if h:
                        act.wait_ge(s["pv_ready"], MH * l + h)
                    act.activation(PT[:, :, :], PS[:, 0:2, :], ACT.Copy).then_inc(s["pt_evac"], 1)
                for st in range(16):
                    act.wait_ge(s["ks_tr"], 16 * l + st + 1)
                    if st >= 4:
                        act.wait_ge(s["ss_ready"], 16 * l + st - 3)
                    b = (0, 2, 6)[st % 3]
                    act.activation(KT[st % 4][:, :, :], PS[:, b:b + 2, :].rearrange("p a (j m) -> p (a j) m", j=2), ACT.Copy).then_inc(s["ks_ev"], 1)
                act.wait_ge(s["smx"], l + 1)
                act.activation(Pb[:, 0, :], PS[:, 4, 0:NM], ACT.Exp, bias=am[:, 0, 0:1], accum_out=ar[:, 0, 0:1]).then_inc(s["s_exp"], 1)
                act.wait_ge(s["vb_done"], NB * l + NB)
                act.activation(Ob[:, :].rearrange("p (a n) -> p a n", a=2), PS[:, 6:8, :], ACT.Copy).then_inc(s["so_ev"], 1)
                act.wait_ge(s["att_done"], l + 1)

            def ffn(l, f):
                to_h()
                d = ph["gu", l, f]
                e0 = list(n.ev)

                def gu(i):
                    for b in range(2):
                        u = d.u0 + i * 4 + 2 * b
                        split(u + 1, (d.u0 + 1) % 2)
                        act.wait_ge(s["w_mm"], u + 3)
                        act.wait_ge(evac[2 * b + 1], i + e0[2 * b + 1] + 1)
                        act.activation(sg[:, b, :].rearrange("p (h t) -> p h t", h=2), PS[:, 4 * b:4 * b + 2, 0:HT], ACT.Silu).then_inc(evac[2 * b], 1)
                        split(u + 2, d.u0 % 2)
                        act.wait_ge(evac[2 * b + 1], i + e0[2 * b + 1] + 2)
                        act.activation(H24[:, bass.ds(2 * i + b, 1), :], prod[:, b:b + 1, :], ACT.Copy).then_inc(s["mid_hi"], 1)
                step_loop(act, d.n, gu)
                for j in range(4):
                    n.ev[j] += d.n
                n.mid += 2 * d.n
                dn = ph["down", l, f]
                e1 = list(n.ev)

                def down(i, final=False):
                    for u in range(6):
                        if final and u == 5:
                            break
                        split(dn.u0 + i * 6 + u + 1, (dn.u0 + u + 1) % 2, (dn.nks * 2 + (8,))[u + 1])
                if (l, f) == (DEPTH - 1, 1):
                    step_loop(act, dn.n - 1, down)
                    down(dn.n - 1, True)
                else:
                    step_loop(act, dn.n, down)

                def y_ready(k):
                    act.wait_ge(evac[k % 2], e1[k % 2] + k // 2 + 2)
                stats(y_of, y_ready, KD, D)
                for j in range(2):
                    n.ev[j] += dn.n
                n.res += KD

            for l in range(DEPTH):
                ffn(l, 0)
                if l == 0:
                    act.wait_ge(s["x_done"], n.res + KD)
                    act.nop().then_inc(s["qm0"], 1)
                    to_h()
                    u0 = ph["dt"].u0
                    split(u0 + 1, (u0 + 1) % 2)
                    act.wait_ge(s["w_mm"], u0 + 3)
                    act.activation(dts[:, 0, :].rearrange("p (h t) -> p h t", h=2), PS[0:NH, 0:2, 0:HT], ACT.Identity, bias=dtb[:, :]).then_inc(evac[0], 1)
                    n.ev[0] += 1
                    act.wait_ge(evac[0], n.ev[0] + 1)
                    act.activation(dts[:, 1, :], dts[:, 0, :], ACT.Abs).then_inc(s["dt_ab"], 1)
                    act.wait_ge(s["dt_ab"], 1)
                    act.activation(dts[:, 2, :], dts[:, 1, :], ACT.Exp, scale=-1.0).then_inc(s["dt_e"], 1)
                    act.activation(nA[:, :], alog[:, :], ACT.Exp).then_inc(s["na_ready"], 1)
                    act.wait_ge(s["dt_u"], 1)
                    act.activation(dts[:, 4, :], dts[:, 3, :], ACT.Ln).then_inc(s["dt_ln"], 1)
                    act.wait_ge(s["alb_sub"], 1)
                    act.activation(DE[:, :, :], DE[:, :, :], ACT.Exp)
                    act.activation(CD[:, :, :], CD[:, :, :], ACT.Exp)
                    act.activation(EAS[:, :], aT[0:NS, NCH, :], ACT.Exp).then_inc(s["de_done"], 1)
                    act.wait_ge(s["pz"], 2)
                    act.wait_ge(s["de_done"], 1)
                    d = ph["ssd"]
                    e0 = list(n.ev)

                    def group(g):
                        def conv_in(ti):
                            act.wait_ge(s["w_mm"], d.u0 + g * 6 + ti + 3)
                            act.wait_ge(s["taps"], g * 4 + ti + 3 - 2)
                            act.wait_ge(s["cvn_done"], g * 4 + ti + 3 - 2)
                            b, bank = ti % 2, 2 * POS[ti]
                            act.activation(pre[:, b, CW - 1:CW - 1 + HT], PS[:, bank, 0:HT], ACT.Copy)
                            act.activation(pre[:, b, CW - 1 + HT:], PS[:, bank + 1, 0:HP], ACT.Copy)
                            act.activation(pres[:, b, :, CW - 1:], PS[:, bank + 1, HP:HT].rearrange("p (b t) -> p b t", b=NB), ACT.Copy).then_inc(evac[POS[ti]], 1)
                            rep = 2 if POS[ti] < 2 else 1
                            act.wait_ge(evac[POS[ti]], g * rep + e0[POS[ti]] + 2)
                            act.wait_ge(s["hist_g"], g * 4 + ti + 1)
                            act.activation(xbc[:, ti, 0:SEQ], pre[:, b, 0:SEQ], ACT.Identity, bias=cwg[:, ti, 4:5], scale=cwg[:, ti, 0:1])
                            act.activation(xbc[:, ti, SEQ:T].rearrange("p (b t) -> p b t", b=NB), pres[:, b, :, 0:NT], ACT.Identity, bias=cwg[:, ti, 4:5], scale=cwg[:, ti, 0:1]).then_inc(s["tap0"], 1)

                        def conv_silu(ti):
                            act.wait_ge(s["taps"], g * 4 + ti + 1 + 2)
                            act.activation(xbc[:, ti, :], xbc[:, ti, :], ACT.Silu).then_inc(s["conv_done"], 1)

                        act.wait_ge(s["group_end"], g + 1)
                        for j in range(6):
                            split(d.u0 + g * 6 + j + 1, (d.u0 + j + 1) % 2)
                            if j < 4:
                                conv_in(j)
                                if j:
                                    conv_silu(j - 1)
                            else:
                                act.wait_ge(s["w_mm"], d.u0 + g * 6 + j + 3)
                                act.activation(sz[:, j - 4, :].rearrange("p (h t) -> p h t", h=2), PS[:, 2 * (j - 4):2 * (j - 4) + 2, 0:HT], ACT.Silu).then_inc(evac[j - 4], 1)
                                if j == 4:
                                    conv_silu(3)
                        act.wait_ge(s["tok_ready"], g + 1)
                        act.activation(btok[:, 0:NCH, :], PS[:, 4, :].rearrange("p (c n) -> p c n", c=NCH), ACT.Copy).then_inc(s["btok_ready"], 1)
                        act.wait_ge(s["cvt_ready"], g + 1)
                        act.activation(cvo[:, :, :], PS[0:27, 1, :].rearrange("p (c n) -> p c n", c=4), ACT.Copy).then_inc(s["cvo_done"], 1)
                        act.wait_ge(s["small_read"], g + 1)
                        act.activation(cds[:, :], cds[:, :], ACT.Exp).then_inc(s["cds_exp"], 1)

                        def decay(h):
                            act.wait_ge(s["bc_ready"], g * 4 + h + 1)
                            if h >= 2:
                                act.wait_ge(s["seg_ready"], g * 4 + h - 1)
                            act.activation(bcS[:, h % 2, :], PS[:, h % 2, :], ACT.Copy)
                            if h >= 2:
                                act.wait_ge(s["y_used"], g * 4 + h - 1)
                            act.activation(Eh[:, h % 2, :], PS[:, h % 2, :], ACT.Exp).then_inc(s["bc_read"], 1)

                        def pair_decay(h):
                            act.wait_ge(s["seg_ready"], g * 4 + h + 1)
                            act.activation(Lh[0:NS, h % 2, SEQ:T], Lh[0:NS, h % 2, SEQ:T], ACT.Exp)
                            act.activation(Lh[:, h % 2, 0:SEQ], Lh[:, h % 2, 0:SEQ], ACT.Exp).then_inc(s["lexp"], 1)

                        def state_rows(q):
                            act.wait_ge(s["s0t_ready"], g * 2 + q + 1)
                            act.activation(S0T[:, :, q * P:(q + 1) * P], PS[:, 6:8, :].rearrange("p a (b n) -> p (a b) n", b=4), ACT.Copy).then_inc(s["s0t_evac"], 1)

                        decay(0)
                        decay(1)
                        pair_decay(0)
                        state_rows(0)
                        decay(2)
                        pair_decay(1)
                        state_rows(1)
                        decay(3)
                        pair_decay(2)
                        pair_decay(3)
                        act.wait_ge(s["final_ready"], g + 1)
                        act.activation(sso[:, :, :], PS[:, 4, 0:256].rearrange("p (q n) -> p q n", q=2), ACT.Copy).then_inc(s["final_read"], 1)
                        act.wait_ge(s["final_read"], g + 1)
                    step_loop(act, NG, group)
                    n.ev = [n.ev[0] + 2 * NG, n.ev[1] + 2 * NG, n.ev[2] + NG, n.ev[3] + NG]

                    def queries(d, dst, first=0, scale=MD ** -0.5):
                        e = list(n.ev)

                        def body(i):
                            for j in range(2):
                                split(d.u0 + i * 2 + j + 1, (d.u0 + j + 1) % 2)
                            for j in range(2):
                                act.wait_ge(s["w_mm"], d.u0 + i * 2 + j + 3)
                                act.activation(dst[:, bass.ds(2 * i + (j + first), 1), :].rearrange("p o (h t) -> p (o h) t", h=2), PS[:, 2 * j:2 * j + 2, 0:HT], ACT.Copy, scale=scale).then_inc(evac[j], 1)
                        step_loop(act, d.n, body)
                        for j in range(2):
                            n.ev[j] += d.n

                    act.wait_ge(s["group_end"], NG + 1)
                    queries(ph["qm", 0], yT)
                    stats(lambda k: M1[:, k, :], lambda k: None, KI, DI)
                    attention(0)
                    for k in range(24):
                        if k < KI:
                            act.wait_ge(s["t_ready"], n.t + k + 1)
                        act.activation(H24[:, k, :], M1[:, k, :], ACT.Copy).then_inc(s["hi_ready"], 1)
                    n.t += KI
                    narrow(ph["out", 0])
                    out_stats(ph["out", 0])
                else:
                    to_h()
                    queries(ph["in_b"], M1, 12, HD ** -0.5)
                    queries(ph["qm", 1], yT)
                    attention(1)
                    act.wait_ge(s["dkt_tr"], 1)
                    for k in range(3):
                        act.activation(KTd[:, 2 * k:2 * k + 2, :], PS[:, 2 * k:2 * k + 2, :], ACT.Copy)
                    act.activation(KTn[:, :, :].rearrange("p j n -> p (j n)"), PS[:, 6, 0:2 * GD * NS], ACT.Copy).then_inc(s["dkt_ev"], 1)

                    def expo(t):
                        n_ = sum(n for _, _, n in spans(t % NCH)) if t < 16 else NEW0 + GD * NS
                        act.wait_ge(s["dmx"], t + 1)
                        b = t % 2
                        act.activation(SS[:, b, 0:n_], SS[:, b, 0:n_], ACT.Exp, bias=dm[:, b:b + 1], accum_out=dr[:, b:b + 1]).then_inc(s["dexp"], 1)

                    def head_out(t):
                        act.wait_ge(s["do_ready"], t + 1)
                        act.activation(M1[:, t // NCH, (t % NCH) * P:(t % NCH + 1) * P], PS[:, 6 + t % 2, 0:P], ACT.Copy).then_inc(s["do_ev"], 1)

                    expo(0)
                    for t in range(16):
                        if t + 1 < 16:
                            expo(t + 1)
                        act.wait_ge(s["dptr"], t + 1)
                        if t >= 2:
                            act.wait_ge(s["do_ready"], t - 1)
                        n_ = sum(n for _, _, n in spans(t % NCH))
                        act.activation(PTd[:, t % 2, 0:n_], PS[:, 3:6, :].rearrange("p a n -> p (a n)")[:, 0:n_], ACT.Copy).then_inc(s["dpt_ev"], 1)
                        if t:
                            head_out(t - 1)
                    head_out(15)
                    for st in range(16):
                        act.wait_ge(s["dks_tr"], st + 1)
                        if st >= 4:
                            act.wait_ge(s["dss_ready"], st - 3)
                        act.activation(KTb[:, st % 4, :], PS[:, st % 3, 0:NEW0], ACT.Copy).then_inc(s["dks_ev"], 1)
                    expo(16)
                    act.wait_ge(s["do_ready"], 17)
                    act.activation(Od[:, :], PS[:, 2, 0:256], ACT.Copy).then_inc(s["do_ev"], 1)
                    act.wait_ge(s["dil_done"], 1)
                    for k in range(12):
                        act.activation(H24[:, k, :], M1[:, k, :], ACT.Copy).then_inc(s["hi_ready"], 1)
                    narrow(ph["out", 1])
                    out_stats(ph["out", 1])
                ffn(l, 1)
                if l == 0:
                    to_h()
                    wide(ph["kv"])
            stats(x_of, x_ready, KD, D)

            for t in range(NCH + 1):
                rows_ = P if t < NCH else NS
                for h in range(2):
                    act.wait_ge(s["f_tr"], 2 * t + h + 1)
                    act.activation(xnat[0:rows_, t, h * 512:(h + 1) * 512], PS[0:rows_, (2 * t + h) % 4, :], ACT.Copy).then_inc(s["f_ev"], 1)
            act.wait_ge(s["f_ev"], 2 * NCH + 2)
            act.dma_start(O["y_prompt"].rearrange("a (t p) d -> p (a t) d", p=P), xnat[:, 0:NCH, :]).then_inc(s["y_out"], 16)
            act.dma_start(O["y_sample"].rearrange("b t d -> (b t) d"), xnat[0:NS, NCH, :]).then_inc(s["y_out"], 16)
            act.wait_ge(s["y_out"], 32)

        @block.tensor
        def _(pe):
            n = Place()

            def products(slot, nk, k0, hi, lo, bank, first, final):
                for k in range(nk):
                    for w, x in ((whi, hi), (whi, lo), (wlo, hi)):
                        for h in range(2):
                            mm = pe.matmul(PS[:, bank + h, 0:HT], w[:, slot, k * P:(k + 1) * P],
                                           x(k0 + k)[:, h * HT:(h + 1) * HT],
                                           start=first and k == 0 and w is whi and x is hi,
                                           stop=final and k == nk - 1 and w is wlo)
                return mm

            def dense(d, hi, lo, pos=lambda j: j):
                e = list(n.ev)

                def body(i):
                    seen = [0] * 4
                    for j in range(d.tiles):
                        b = pos(j)
                        reps = sum(pos(jj) == b for jj in range(d.tiles))
                        pe.wait_ge(evac[b], i * reps + e[b] + seen[b] + 1)
                        seen[b] += 1
                        for q, nk in enumerate(d.nks):
                            u = j * len(d.nks) + q
                            pe.wait_ge(s["w_lo"], i * d.ub + d.u0 + u + 3)
                            products((d.u0 + u) % 2, nk, d.k0[q], hi, lo, 2 * b, q == 0, q == len(d.nks) - 1).then_inc(s["w_mm"], 1)
                step_loop(pe, d.n, body)
                for j in range(d.tiles):
                    n.ev[pos(j)] += d.n

            def wide(d, windows):
                def body(i):
                    pe.wait_ge(s["blk_evac"], n.blk + i * len(windows) + 1)
                    for q in range(4):
                        pe.wait_ge(s["w_lo"], d.u0 + i * 4 + q + 3)
                        for kk in range(2):
                            for b, t0 in enumerate(windows):
                                for x, w in ((hH, whi), (hL, whi), (hH, wlo)):
                                    mm = pe.matmul(PS[:, b, :], x[:, 2 * q + kk, t0:t0 + P], w[:, (d.u0 + q) % 2, kk * 512:(kk + 1) * 512],
                                                   start=q == 0 and kk == 0 and x is hH and w is whi,
                                                   stop=q == 3 and kk == 1 and w is wlo)
                        mm.then_inc(s["w_mm"], 1)
                step_loop(pe, d.n, body)
                n.blk += d.n * len(windows)

            def stats(nk):
                for k in range(nk):
                    pe.wait_ge(s["sq_ready"], n.sq + k + 1)
                    for h in range(2):
                        mm = pe.matmul(PS[:, 4 + h, 0:HT], ones, sqb[:, k % 2, h * HT:(h + 1) * HT], start=k == 0, stop=k == nk - 1)
                    mm.then_inc(s["sq_used"], 1)
                n.sq += nk

            pe.wait_ge(s["const_in"], 12 * 16)
            for j, m in ((0, P), (1, P), (2, 48)):
                tr = pe.transpose(PS[:, 0, j * P:j * P + m], rows[0:m, j, :], ident[0:m, 0:m])
            tr.then_inc(s["row_in"], 1)
            pe.wait_ge(s["cols_out"], 1)
            for k in range(KD):
                pe.wait_ge(s["mem_sc"], 2)
                if k >= 2:
                    pe.wait_ge(s["mem_ev"], k - 1)
                for t in range(2):
                    tr = pe.transpose(PS[:, k % 2, t * P:(t + 1) * P], memnat[:, t, k * P:(k + 1) * P], ident)
                tr.then_inc(s["mem_tr"], 1)
            for l in range(DEPTH):
                n.t += KD
                pe.wait_ge(s["lo_ready"], n.t)
                wide(ph["mem", l], (0, P))
            pe.wait_ge(s["x_in"], 32)
            for k in range(KD):
                if k >= 3:
                    pe.wait_ge(s["x_done"], k - 2)
                b = 2 * (k % 3) + 2
                for t in range(NCH):
                    pe.transpose(PS[:, b, t * P:(t + 1) * P], xnat[:, t, k * P:(k + 1) * P], ident)
                pe.transpose(PS[:, b + 1, 0:NS], xnat[0:NS, NCH, k * P:(k + 1) * P], ident[0:NS, 0:NS]).then_inc(s["x_tr"], 1)

            def to_h():
                stats(KD)
                n.t += KD
                pe.wait_ge(s["lo_ready"], n.t)

            kv_in = [s["kv_in0"], s["kv_in1"], s["kv_in2"]]

            def attention(l, q=None):
                q = yT
                land = lambda idx: pe.wait_ge(kv_in[idx % 3], 16 * (6 * l + idx // 3 + 1))
                pe.wait_ge(s["att_go"], l + 1)
                land(0)
                for hk in range(8):
                    for t in range(2):
                        tr = pe.transpose(PS[:, hk // 2, (hk % 2) * 256 + t * P:(hk % 2) * 256 + (t + 1) * P], kvr[:, 0, t, hk * P:(hk + 1) * P], ident)
                tr.then_inc(s["kt_tr"], 1)

                def scores(h):
                    for r in range(NCH):
                        for k in range(2):
                            mm = pe.matmul(PS[:, 4 + 2 * (h % 2) + r // 2, (r % 2) * NM:(r % 2 + 1) * NM], q[:, 2 * h + k, r * P:(r + 1) * P], KT[(2 * h + k) // 4][:, (2 * h + k) % 4, :], start=k == 0, stop=k == 1)
                    mm.then_inc(s["sc_ready"], 1)

                pe.wait_ge(s["kt_ev"], 2 * l + 2)
                scores(0)
                scores(1)
                land(1)
                for h in range(MH):
                    pe.wait_ge(s["p_ready"], MH * l + h + 1)
                    if h:
                        pe.wait_ge(s["pt_evac"], MH * l + h)
                    for t in range(2):
                        for r in range(NCH):
                            tr = pe.transpose(PS[:, t, r * P:(r + 1) * P], Pb[:, r, t * P:(t + 1) * P], ident)
                    tr.then_inc(s["ptr_ready"], 1)
                    if h + 2 < MH:
                        scores(h + 2)
                    pe.wait_ge(s["pt_evac"], MH * l + h + 1)
                    if h:
                        pe.wait_ge(s["pv_evac"], MH * l + h)
                    for k in range(2):
                        for t in range(2):
                            mm = pe.matmul(PS[:, 2 + k, :], kvr[:, 1, t, (2 * h + k) * P:(2 * h + k + 1) * P], PT[:, t, :], start=t == 0, stop=t == 1)
                    mm.then_inc(s["pv_ready"], 1)
                pe.wait_ge(s["q_ready"], 8 * l + 8)
                pe.wait_ge(s["pt_evac"], MH * l + MH)
                pe.wait_ge(s["pv_evac"], MH * l + MH)
                pairs = (0, 2, 6)

                def rows_of(st):
                    b, half = st // 2, st % 2
                    idx = 2 + b
                    if half == 0:
                        land(idx)
                    if st >= 3:
                        pe.wait_ge(s["ks_ev"], 16 * l + st - 2)
                    for j in range(4):
                        for t in range(2):
                            tr = pe.transpose(PS[:, pairs[st % 3] + j // 2, (j % 2) * 256 + t * P:(j % 2) * 256 + (t + 1) * P], kvr[:, idx % 3, t, (4 * half + j) * P:(4 * half + j + 1) * P], ident)
                    tr.then_inc(s["ks_tr"], 1)

                rows_of(0)
                rows_of(1)
                for st in range(16):
                    if st + 2 < 16:
                        rows_of(st + 2)
                    pe.wait_ge(s["ks_ev"], 16 * l + st + 1)
                    for j in range(4):
                        mm = pe.matmul(PS[:, 4, 0:NM], QZ[:, 4 * (st % 2) + j, st // 2, :], KT[st % 4][:, j, :], start=st == 0 and j == 0, stop=st == 15 and j == 3)
                    mm.then_inc(s["ss_ready"], 1)
                pe.wait_ge(s["s_p"], l + 1)
                for t in range(2):
                    tr = pe.transpose(PS[:, 5, t * P:(t + 1) * P], Pb[:, 0, t * P:(t + 1) * P], ident)
                tr.then_inc(s["s_tr"], 1)
                pe.wait_ge(s["pz_ready"], l + 1)
                pe.wait_ge(s["ks_ev"], 16 * l + 16)
                for b in range(NB):
                    land(10 + b)
                    for t in range(2):
                        for k in range(2):
                            mm = pe.matmul(PS[:, 6 + k, :], PZ[:, t, b, :], kvr[:, (10 + b) % 3, t, k * 512:(k + 1) * 512], start=b == 0 and t == 0, stop=b == NB - 1 and t == 1)
                    mm.then_inc(s["vb_done"], 1)
                pe.wait_ge(s["so_ev"], l + 1)
                for hk in range(8):
                    tr = pe.transpose(PS[:, hk // 4, (hk % 4) * P:(hk % 4 + 1) * P], Ob[:, hk * P:(hk + 1) * P], ident)
                tr.then_inc(s["so_tr"], 1)
                pe.wait_ge(s["att_done"], l + 1)

            def ffn(l, f):
                to_h()
                dense(ph["gu", l, f], hH_of, hL_of)
                n.mid += KF
                pe.wait_ge(s["mid_lo"], n.mid + 2)
                dense(ph["down", l, f], lambda k: H24[:, k, :], lambda k: L24[:, k, :])
                stats(KD)

            for l in range(DEPTH):
                ffn(l, 0)
                if l == 0:
                    to_h()
                    dense(ph["dt"], hH_of, hL_of)
                    pe.wait_ge(s["scan_done"], 1)
                    for c in range(NCH + 1):
                        m = P if c < NCH else NS
                        last = acum[:, c * P + P - 1:c * P + P].to_broadcast([NH, P]) if c < NCH else None
                        pe.transpose(PS[0:m, 0, c * NH:(c + 1) * NH], acum[:, c * P:c * P + m], ident[0:NH, 0:NH])
                        pe.transpose(PS[0:m, 0, 160 + c * NH:160 + (c + 1) * NH], dtx[:, c * P:c * P + m], ident[0:NH, 0:NH])
                        if c < NCH:
                            pe.matmul(PS[:, 0, 320 + c * NH:320 + (c + 1) * NH], last, ident[0:NH, 0:NH], start=True, stop=True)
                        else:
                            pe.matmul(PS[0:NS, 0, 320 + c * NH:320 + (c + 1) * NH], tmpL[:, :], ident[0:NH, 0:NH], start=True, stop=True).then_inc(s["dtt_tr"], 1)
                    pe.wait_ge(s["conv_in"], 32)
                    for c in range(32):
                        tr = pe.transpose(PS[:, 2 + c // 16, (c % 16) * 24:(c % 16 + 1) * 24], cvin[:, c * P:(c + 1) * P], ident[0:24, 0:24])
                    tr.then_inc(s["hist_tr"], 1)
                    pe.wait_ge(s["hist_copied"], 1)
                    d = ph["ssd"]
                    e0 = list(n.ev)

                    def group(g):
                        pe.wait_ge(s["group_end"], g + 1)
                        for j in range(6):
                            rep = 2 if POS[j] < 2 else 1
                            pe.wait_ge(evac[POS[j]], g * rep + e0[POS[j]] + 1 + (j >= 4))
                            pe.wait_ge(s["w_lo"], g * 6 + d.u0 + j + 3)
                            products((d.u0 + j) % 2, KD, 0, hH_of, hL_of, 2 * POS[j], True, True).then_inc(s["w_mm"], 1)
                        pe.wait_ge(s["conv_done"], g * 4 + 4)
                        pe.wait_ge(s["col_g"], g + 1)
                        for c in range(NCH):
                            pe.transpose(PS[:, 4, c * P:(c + 1) * P], xbc[:, 0, c * P:(c + 1) * P], ident)
                            for q in range(2):
                                pe.transpose(PS[:, 6 + c // 2, (c % 2) * 256 + q * P:(c % 2) * 256 + (q + 1) * P], xbc[:, 2 + q, c * P:(c + 1) * P], ident)
                        for q, t in enumerate((0, 2, 3)):
                            pe.transpose(PS[0:NS, 5, q * P:(q + 1) * P], xbc[:, t, SEQ:T], ident)
                        pe.matmul(PS[0:NS, 5, 384:384 + NS], xbc[:, 0, SEQ:T], xbc[:, 1, SEQ:T], start=True, stop=True)
                        for q in range(2):
                            mm = pe.matmul(PS[:, 5, 416 + q * NB:416 + (q + 1) * NB], selp[:, 2 * q:2 * q + 2, :].rearrange("p a b -> p (a b)"), acum[:, SEQ + NT - 1:T:NT], start=True, stop=True)
                        mm.then_inc(s["tok_ready"], 1)
                        pe.wait_ge(evac[0], 2 * g + e0[0] + 3)
                        for c in range(NCH):
                            mm = pe.matmul(PS[:, 0, c * P:(c + 1) * P], xbc[:, 0, c * P:(c + 1) * P], xbc[:, 1, c * P:(c + 1) * P], start=True, stop=True)
                        mm.then_inc(s["cb_ready"], 1)
                        pe.wait_ge(s["cvn_done"], g * 4 + 4 + 2)
                        for q in range(4):
                            tr = pe.transpose(PS[0:27, 1, q * P:(q + 1) * P], cvn[:, q, 0:27], ident)
                        tr.then_inc(s["cvt_ready"], 1)
                        pe.wait_ge(evac[1], 2 * g + e0[1] + 3)
                        pe.wait_ge(s["xdd_ready"], g + 1)
                        pe.wait_ge(s["btok_ready"], g + 1)
                        for c in range(NCH):
                            mm = pe.matmul(PS[:, 2 + c // 2, (c % 2) * 256:(c % 2 + 1) * 256], btok[:, c, :], xdd[:, c, :], start=True, stop=True)
                        mm.then_inc(s["st_ready"], 1)
                        pe.wait_ge(s["small_read"], g + 1)
                        for h in range(4):
                            mm = pe.matmul(PS[:, 5, h * NS:(h + 1) * NS], selg[:, h:h + 1].to_broadcast([NH, P]), acum[:, SEQ:T], start=True, stop=True)
                        mm.then_inc(s["bcs_ready"], 1)

                        def spread(h):
                            if h == 0:
                                pe.wait_ge(s["cbm_ready"], g + 1)
                            elif h == 1:
                                pe.wait_ge(s["cvo_done"], g + 1)
                            else:
                                pe.wait_ge(s["bc_read"], g * 4 + h - 1)
                            pe.matmul(PS[:, h % 2, :], selg[:, h:h + 1].to_broadcast([NH, P]), acum[:, 0:SEQ], start=True, stop=True).then_inc(s["bc_ready"], 1)

                        def head(h):
                            pe.wait_ge(s["m_ready"], g * 4 + h + 1)
                            pe.wait_ge(s["c_ready"], g * 4 + h + 1)
                            if h == 0:
                                pe.wait_ge(s["st_done"], g + 1)
                                pe.wait_ge(s["bcs_read"], g + 1)
                            r, w = (h % 2) * PD, slice(h * PD, (h + 1) * PD)
                            for c in range(NCH):
                                pe.matmul(PS[r:r + PD, 2 + h // 2, c * P:(c + 1) * P], xd[:, c, w], Lh[:, h % 2, c * P:(c + 1) * P], start=True, stop=c == 0)
                                if c:
                                    pe.matmul(PS[r:r + PD, 2 + h // 2, c * P:(c + 1) * P], ST[:, c - 1, w], Eh[:, h % 2, c * P:(c + 1) * P], start=False, stop=True)
                            pe.matmul(PS[r:r + PD, 5, 128 + (h // 2) * NS:128 + (h // 2 + 1) * NS], xd[0:NS, NCH, w], Lh[0:NS, h % 2, SEQ:T], start=True, stop=True).then_inc(s["y_used"], 1)

                        def state_rows(q):
                            if q == 0:
                                pe.wait_ge(s["s0_in"], g * 32 + 32)
                                pe.wait_ge(s["xd_ready"], g + 1)
                            else:
                                pe.wait_ge(s["s0t_evac"], g * 2 + 1)
                            for b in range(NB):
                                tr = pe.transpose(PS[:, 6 + b // 4, (b % 4) * P:(b % 4 + 1) * P], S0[:, q, b, :], ident)
                            tr.then_inc(s["s0t_ready"], 1)

                        def new_states(q):
                            if q == 0:
                                pe.wait_ge(s["s0t_evac"], g * 2 + 2)
                                pe.wait_ge(s["bz_ready"], g + 1)
                            else:
                                pe.wait_ge(s["news_read"], g * 2 + 1)
                            for k in range(2):
                                mm = pe.matmul(PS[:, 6 + k, :], xdd[0:NS, NCH, q * P:(q + 1) * P], BZ[:, 4 * k:4 * k + 4, :].rearrange("p b n -> p (b n)"), start=True, stop=True)
                            mm.then_inc(s["news_ready"], 1)

                        spread(0)
                        spread(1)
                        state_rows(0)
                        head(0)
                        spread(2)
                        state_rows(1)
                        head(1)
                        spread(3)
                        pe.wait_ge(s["s0t_evac"], g * 2 + 2)
                        pe.wait_ge(s["cz_ready"], g + 1)
                        for b in range(NB):
                            mm = pe.matmul(PS[0:NS, 4, 0:256], CZ[:, b, :], S0T[:, b, :], start=b == 0, stop=b == NB - 1)
                        mm.then_inc(s["yoff_ready"], 1)
                        new_states(0)
                        head(2)
                        new_states(1)
                        head(3)
                        pe.wait_ge(s["yos_ready"], g + 1)
                        for q in range(2):
                            tr = pe.transpose(PS[:, 4, q * P:(q + 1) * P], ST[:, NCH - 1, q * P:(q + 1) * P], ident)
                        tr.then_inc(s["final_ready"], 1)
                        for q in range(2):
                            tr = pe.transpose(PS[:, 5, 192 + q * NS:192 + (q + 1) * NS], yos[:, q * P:(q + 1) * P], ident[0:NS, 0:NS])
                        tr.then_inc(s["y_ready"], 1)
                    step_loop(pe, NG, group)
                    n.ev = [n.ev[0] + 2 * NG, n.ev[1] + 2 * NG, n.ev[2] + NG, n.ev[3] + NG]
                    pe.wait_ge(s["group_end"], NG + 1)
                    dense(ph["qm", 0], hH_of, hL_of)
                    stats(KI)
                    attention(0)
                    n.t += 24
                    n.unscaled += 8
                    pe.wait_ge(s["lo_ready"], n.t)
                    dense(ph["out", 0], lambda k: H24[:, k, :], lambda k: L24[:, k, :])
                    stats(KD)
                else:
                    to_h()
                    dense(ph["in_b"], hH_of, hL_of)
                    dense(ph["qm", 1], hH_of, hL_of)
                    attention(1)
                    pe.wait_ge(s["dil_in"], 48)
                    for j in range(2 * GD):
                        for t in range(NCH):
                            pe.transpose(PS[:, j, t * P:(t + 1) * P], kvd[:, t, (j // 2) * 512 + (j % 2) * P:(j // 2) * 512 + (j % 2 + 1) * P], ident)
                    for j in range(2 * GD):
                        tr = pe.transpose(PS[:, 6, j * NS:(j + 1) * NS], kvn[:, (j // 2) * 512 + (j % 2) * P:(j // 2) * 512 + (j % 2 + 1) * P], ident[0:NS, 0:NS])
                    tr.then_inc(s["dkt_tr"], 1)

                    def scores(t):
                        h, i = t // NCH, t % NCH
                        if t:
                            pe.wait_ge(s["ds_ev"], t)
                        for g, first, n_ in spans(i):
                            mm = pe.matmul(PS[:, g, 0:n_], M1[:, 12 + g * QH + h, i * P:(i + 1) * P], KTd[:, 2 * g + h // 2, first * P:(i + 1) * P], start=True, stop=True)
                        mm.then_inc(s["ds_ready"], 1)

                    def values(t):
                        h, i = t // NCH, t % NCH
                        if t >= 2:
                            pe.wait_ge(s["do_ev"], t - 1)
                        tiles = [(g, kt) for g, first, _ in spans(i) for kt in range(first, i + 1)]
                        for x, (g, kt) in enumerate(tiles):
                            c = g * 512 + 256 + (h // 2) * P
                            mm = pe.matmul(PS[:, 6 + t % 2, 0:P], kvd[:, kt, c:c + P], PTd[:, t % 2, x * P:(x + 1) * P], start=x == 0, stop=x == len(tiles) - 1)
                        mm.then_inc(s["do_ready"], 1)

                    pe.wait_ge(s["dkt_ev"], 1)
                    scores(0)
                    for t in range(16):
                        if t + 1 < 16:
                            scores(t + 1)
                        pe.wait_ge(s["dp_ready"], t + 1)
                        if t:
                            pe.wait_ge(s["dpt_ev"], t)
                        for x in range(sum(n for _, _, n in spans(t % NCH)) // P):
                            tr = pe.transpose(PS[:, 3 + x // 4, (x % 4) * P:(x % 4 + 1) * P], SS[:, t % 2, x * P:(x + 1) * P], ident)
                        tr.then_inc(s["dptr"], 1)
                        if t:
                            values(t - 1)
                    pe.wait_ge(s["dpt_ev"], 16)
                    values(15)
                    pe.wait_ge(s["dks_in"], 7 * 16)
                    pe.wait_ge(s["ds_ev"], 16)

                    def rows_of(st):
                        b, kv = st // 2, st % 2
                        if st >= 3:
                            pe.wait_ge(s["dks_ev"], st - 2)
                        for sl in range(4):
                            m = P if sl < 3 else 64
                            tr = pe.transpose(PS[:, st % 3, sl * P:sl * P + m], Kc[0:m, b, sl, kv * P:(kv + 1) * P], ident[0:m, 0:m])
                        tr.then_inc(s["dks_tr"], 1)

                    rows_of(0)
                    rows_of(1)
                    pe.wait_ge(s["qd_done"], 1)
                    for st in range(16):
                        if st + 2 < 16:
                            rows_of(st + 2)
                        pe.wait_ge(s["dks_ev"], st + 1)
                        for g, c0, c1 in OLD:
                            mm = pe.matmul(PS[:, 3 + g, 0:c1 - c0], QZD[:, 2 * g + st % 2, st // 2, :], KTb[:, st % 4, c0:c1], start=st == 0, stop=st == 15)
                        mm.then_inc(s["dss_ready"], 1)
                    pe.wait_ge(s["do_ev"], 16)
                    pe.wait_ge(s["qn_done"], 1)
                    for g in range(GD):
                        for kv in range(KVH):
                            mm = pe.matmul(PS[:, 6, g * NS:(g + 1) * NS], QN[:, 2 * g + kv, :], KTn[:, 2 * g + kv, :], start=kv == 0, stop=kv == 1)
                    mm.then_inc(s["ds_ready"], 1)
                    pe.wait_ge(s["dp_ready"], 17)
                    for sl in range(4):
                        m = P if sl < 3 else 64
                        pe.transpose(PS[0:m, 0, sl * P:(sl + 1) * P], SS[:, 0, sl * P:sl * P + m], ident)
                    for g in range(GD):
                        tr = pe.transpose(PS[0:NS, 1, g * P:(g + 1) * P], SS[:, 0, NEW0 + g * NS:NEW0 + (g + 1) * NS], ident)
                    tr.then_inc(s["dptr"], 1)
                    pe.wait_ge(s["dpt_ev"], 17)
                    pe.wait_ge(s["dv_in"], (2 * NB + NT) * 16)
                    for b in range(NB):
                        for sl in range(4):
                            m = P if sl < 3 else 64
                            pe.matmul(PS[:, 2, 0:256], QZD[0:m, sl, b, :], Kc[0:m, b, sl, :], start=b == 0 and sl == 0, stop=False)
                    for g in range(GD):
                        mm = pe.matmul(PS[:, 2, 0:256], PTn[:, g, :], kvn[:, g * 512 + 256:(g + 1) * 512], start=False, stop=g == GD - 1)
                    mm.then_inc(s["do_ready"], 1)
                    pe.wait_ge(s["do_ev"], 17)
                    for kv in range(KVH):
                        tr = pe.transpose(PS[:, 3, kv * P:(kv + 1) * P], Od[:, kv * P:(kv + 1) * P], ident)
                    tr.then_inc(s["dptr"], 1)
                    pe.wait_ge(s["dil_done"], 1)
                    n.t += 12
                    n.unscaled += 12
                    pe.wait_ge(s["lo_ready"], n.t)
                    dense(ph["out", 1], lambda k: H24[:, k, :], lambda k: L24[:, k, :])
                    stats(KD)
                ffn(l, 1)
                if l == 0:
                    to_h()
                    wide(ph["kv"], (0, P, 2 * P, 3 * P, T - P))
                    pe.wait_ge(s["blk_evac"], n.blk + 1)
            stats(KD)
            pe.wait_ge(s["t_ready"], n.t - n.unscaled + KD)
            for t in range(NCH + 1):
                rows_ = P if t < NCH else NS
                for h in range(2):
                    m = 2 * t + h
                    if m >= 4:
                        pe.wait_ge(s["f_ev"], m - 3)
                    for k in range(4):
                        tr = pe.transpose(PS[0:rows_, m % 4, k * P:(k + 1) * P], yT[:, 4 * h + k, t * P:t * P + rows_], ident)
                    tr.then_inc(s["f_tr"], 1)

        @block.vector
        def _(dve):
            n = Place()

            def split(u, slot, nk=8):
                dve.wait_ge(s["w_hi"], u + 1)
                dve.tensor_tensor(wlo[:, slot, 0:nk * P], raw[:, slot, 0:nk * P], whi[:, slot, 0:nk * P].bitcast(F32), ALU.subtract).then_inc(s["w_lo"], 1)

            def inverse():
                dve.wait_ge(s["rt_ready"], n.norm + 1)
                dve.reciprocal(rb[:, :], rt[:, :]).then_inc(s["rb_ready"], 1)
                n.norm += 1
                dve.wait_ge(s["rb_ready"], n.norm)

            def lows(tmp, hi, lo, nk, make):
                for k in range(nk + 2):
                    if k < nk:
                        make(k).then_inc(s["t_ready"], 1)
                    if k >= 2:
                        dve.wait_ge(s["hi_ready"], n.t + k - 1)
                        dve.tensor_tensor(lo(k - 2), tmp(k - 2), hi(k - 2).bitcast(F32), ALU.subtract).then_inc(s["lo_ready"], 1)
                n.t += nk

            def scaled(out, src, g):
                return lambda k: dve.scalar_tensor_tensor(out=out(k), in0=src(k), scalar=g(k), in1=rb[:, :], op0=ALU.mult, op1=ALU.mult)

            def residual(g):
                inverse()
                for k in range(KD + 1):
                    if k < KD:
                        scaled(y_of, y_of, g)(k).then_inc(s["pn_t"], 1)
                    if k:
                        dve.wait_ge(s["pn_t"], n.res + k)
                        dve.tensor_tensor(xT[:, k - 1, :], xT[:, k - 1, :], yT[:, k - 1, :], ALU.add).then_inc(s["x_done"], 1)
                n.res += KD

            dve.wait_ge(s["row_in"], 1)
            dve.tensor_copy(G[:, :], PS[:, 0, 0:P])
            dve.tensor_scalar(GH[:, :], PS[:, 0, 0:P], 0.5, None, ALU.mult)
            dve.tensor_copy(CWT[:, :], PS[:, 0, P:2 * P])
            dve.tensor_copy(CB[:, :], PS[:, 0, 2 * P:2 * P + 48]).then_inc(s["cols_out"], 1)
            dve.wait_ge(s["mem_rt"], 1)
            dve.reciprocal(mst[:, 4:6], mst[:, 2:4]).then_inc(s["mem_rb"], 1)
            dve.wait_ge(s["mem_rb"], 1)
            for t in range(2):
                dve.tensor_scalar(memnat[:, t, :], memnat[:, t, :], mst[:, 4 + t:5 + t], None, ALU.mult).then_inc(s["mem_sc"], 1)
            split(0, 0)
            dve.wait_ge(s["mem_ev"], KD)
            dve.wait_ge(s["cols_out"], 1)

            def wide(d, nt):
                def body(i):
                    for q in range(4):
                        split(d.u0 + i * 4 + q + 1, (d.u0 + q + 1) % 2)
                    dve.wait_ge(s["w_mm"], d.u0 + i * 4 + 6)
                    dve.wait_ge(s["stage_free"], i + n.out + 1)
                    for b in range(nt):
                        dve.tensor_copy(stage[:, b, :], PS[:, b, :]).then_inc(s["blk_evac"], 1)
                return body

            for l in range(DEPTH):
                if l:
                    dve.wait_ge(s["w_mm"], ph["mem", l].u0 + 2)
                g = col(104 + KD * l)
                lows(lambda k: yT[:, k, 0:NM], lambda k: hH[:, k, 0:NM], lambda k: hL[:, k, 0:NM], KD,
                     lambda k: dve.tensor_scalar(yT[:, k, 0:NM], memT[:, k, :], g(k), None, ALU.mult))
                step_loop(dve, 4, wide(ph["mem", l], 2))
                n.out += 4

            def to_h(g):
                inverse()
                lows(y_of, hH_of, hL_of, KD, scaled(y_of, x_of, g))

            def narrow(d):
                def body(i):
                    for j in range(2):
                        for q in range(len(d.nks)):
                            u = j * len(d.nks) + q
                            split(d.u0 + i * d.ub + u + 1, (d.u0 + u + 1) % 2, (d.nks * 2 + (8,))[u + 1])
                        dve.wait_ge(s["w_mm"], d.u0 + i * d.ub + (j + 1) * len(d.nks) + 2)
                        dve.tensor_copy(yT[:, bass.ds(2 * i + j, 1), :].rearrange("p o (h t) -> p (o h) t", h=2), PS[:, 2 * j:2 * j + 2, 0:HT]).then_inc(evac[j], 1)
                step_loop(dve, d.n, body)
                for j in range(2):
                    n.ev[j] += d.n

            def attention(l):
                o0 = (16, 4)[l]

                def maxima(h):
                    dve.wait_ge(s["sc_ready"], MH * l + h + 1)
                    b = 4 + 2 * (h % 2)
                    dve.tensor_reduce(am[:, h % 2, :], PS[:, b:b + 2, :].rearrange("p a (r m) -> p (a r) m", r=2), AX_X, ALU.max, negate=True).then_inc(s["mx_ready"], 1)

                maxima(0)
                for h in range(MH):
                    if h + 1 < MH:
                        maxima(h + 1)
                    dve.wait_ge(s["p_exp"], MH * l + h + 1)
                    dve.reciprocal(ai[:, 0, :], ar[:, h % 2, :]).then_inc(s["p_rcp"], 1)
                    dve.wait_ge(s["p_rcp"], MH * l + h + 1)
                    dve.tensor_tensor(Pb[:, :, :], Pb[:, :, :], ai[:, 0, :].unsqueeze(2).to_broadcast([P, NCH, NM]), ALU.mult).then_inc(s["p_ready"], 1)
                    dve.wait_ge(s["pv_ready"], MH * l + h + 1)
                    dve.tensor_copy(M1[:, o0 + 2 * h:o0 + 2 * h + 2, 0:SEQ], PS[:, 2:4, :]).then_inc(s["pv_evac"], 1)
                dve.wait_ge(s["ss_ready"], 16 * l + 16)
                dve.tensor_reduce(am[:, 0, 0:1], PS[:, 4, 0:NM], AX_X, ALU.max, negate=True).then_inc(s["smx"], 1)
                dve.wait_ge(s["s_exp"], l + 1)
                dve.reciprocal(ai[:, 1, 0:1], ar[:, 0, 0:1]).then_inc(s["s_rcp"], 1)
                dve.wait_ge(s["s_rcp"], l + 1)
                dve.tensor_scalar(Pb[:, 0, :], Pb[:, 0, :], ai[:, 1, 0:1], None, ALU.mult).then_inc(s["s_p"], 1)
                dve.wait_ge(s["s_tr"], l + 1)
                dve.wait_ge(s["qz_zero"], 2 * l + 2)
                for t in range(2):
                    z = PZ[:, t, :, :]
                    ins = dve.tensor_copy(bass.AP(z.tensor, z.offset, [list(z.ap[0]), [P + 16, NB], [1, 16]]), PS[:, 5, t * P:(t + 1) * P].rearrange("p (b r) -> p b r", b=NB))
                ins.then_inc(s["pz_ready"], 1)
                dve.wait_ge(s["so_tr"], l + 1)
                for hk in range(8):
                    src = PS[:, hk // 4, (hk % 4) * P:(hk % 4 + 1) * P].rearrange("p (b h t) -> p b h t", b=NB, h=MH)[:, :, hk // 2, :]
                    ins = dve.tensor_copy(M1[:, o0 + hk, SEQ:T].rearrange("p (b t) -> p b t", b=NB), src)
                ins.then_inc(s["att_done"], 1)

            n.res = 0

            def ffn(l, f):
                to_h(gain(l, 4 * f))
                if f == 0:
                    dve.wait_ge(s["stage_free"], 2 * 4 + GD * l + 1)
                d = ph["gu", l, f]
                e0 = list(n.ev)

                def gu(i):
                    for b in range(2):
                        u = d.u0 + i * 4 + 2 * b
                        split(u + 1, (d.u0 + 1) % 2)
                        split(u + 2, d.u0 % 2)
                        dve.wait_ge(s["w_mm"], u + 4)
                        dve.wait_ge(evac[2 * b], i + e0[2 * b] + 2)
                        dve.wait_ge(s["mid_lo"], 2 * i + b + n.mid + 1)
                        dve.tensor_tensor(prod[:, b, :].rearrange("p (h t) -> p h t", h=2), sg[:, b, :].rearrange("p (h t) -> p h t", h=2),
                                          PS[:, 4 * b + 2:4 * b + 4, 0:HT], ALU.mult).then_inc(evac[2 * b + 1], 1)
                        dve.wait_ge(s["mid_hi"], 2 * i + b + n.mid + 1)
                        dve.tensor_tensor(L24[:, bass.ds(2 * i + b, 1), :], prod[:, b:b + 1, :], H24[:, bass.ds(2 * i + b, 1), :].bitcast(F32), ALU.subtract).then_inc(s["mid_lo"], 1)
                step_loop(dve, d.n, gu)
                for j in range(4):
                    n.ev[j] += d.n
                n.mid += 2 * d.n
                dn = ph["down", l, f]
                dve.wait_ge(s["mid_lo"], n.mid + 2)

                def down(i, final=False):
                    for j in range(2):
                        for q in range(3):
                            u = 3 * j + q
                            if not (final and u == 5):
                                split(dn.u0 + i * 6 + u + 1, (dn.u0 + u + 1) % 2, (dn.nks * 2 + (8,))[u + 1])
                        dve.wait_ge(s["w_mm"], dn.u0 + i * 6 + 3 * j + 5)
                        dve.tensor_copy(yT[:, bass.ds(2 * i + j, 1), :].rearrange("p o (h t) -> p (o h) t", h=2), PS[:, 2 * j:2 * j + 2, 0:HT]).then_inc(evac[j], 1)
                if (l, f) == (DEPTH - 1, 1):
                    step_loop(dve, dn.n - 1, down)
                    down(dn.n - 1, True)
                else:
                    step_loop(dve, dn.n, down)
                for j in range(2):
                    n.ev[j] += dn.n
                residual(half_gain(l, 4 * f + 1))

            for l in range(DEPTH):
                ffn(l, 0)
                if l == 0:
                    to_h(gain(0, 2))
                    u0 = ph["dt"].u0
                    split(u0 + 1, (u0 + 1) % 2)
                    n.ev[0] += 1
                    st = Steps(dve, s["dt_v"], 0)
                    dve.wait_ge(s["dt_e"], 1)
                    dve.tensor_scalar(dts[:, 3, :], dts[:, 2, :], 1.0, None, ALU.add).then_inc(s["dt_u"], 1)
                    dve.wait_ge(s["dt_u"], 1)
                    st(dve.tensor_scalar(dts[:, 1, :], dts[:, 3, :], -1.0, None, ALU.add))
                    st(dve.reciprocal(dts[:, 5, :], dts[:, 3, :]))
                    st.wait()
                    st(dve.tensor_tensor(dts[:, 1, :], dts[:, 2, :], dts[:, 1, :], ALU.subtract))
                    st.wait()
                    st(dve.tensor_tensor(dts[:, 1, :], dts[:, 1, :], dts[:, 5, :], ALU.mult))
                    dve.wait_ge(s["dt_ln"], 1)
                    st.wait()
                    st(dve.tensor_tensor(dts[:, 1, :], dts[:, 1, :], dts[:, 4, :], ALU.add))
                    st.wait()
                    st(dve.scalar_tensor_tensor(out=dtx[:, :], in0=dts[:, 0, :], scalar=0.0, in1=dts[:, 1, :], op0=ALU.max, op1=ALU.add))
                    dve.wait_ge(s["na_ready"], 1)
                    st(dve.tensor_scalar(nA[:, :], nA[:, :], -1.0, None, ALU.mult))
                    st.wait()
                    st(dve.tensor_scalar(dts[:, 2, :], dtx[:, :], nA[:, 0:1], None, ALU.mult))
                    st.wait()
                    dve.wait_ge(s["conv_in"], 32)
                    st(dve.tensor_tensor_scan(acum[:, :], reset[:, :], dts[:, 2, :], 0.0, ALU.mult, ALU.add))
                    st.wait()
                    dve.tensor_copy(tmpL[:, :].rearrange("p (b t) -> p b t", b=NB), acum[:, SEQ + NT - 1:T:NT].unsqueeze(2).to_broadcast([NH, NB, NT])).then_inc(s["scan_done"], 1)
                    for t in (aT, dT, CD):
                        st(dve.memset(t[:, NCH, :], 0.0))
                    dve.wait_ge(s["dtt_tr"], 1)
                    st.wait()
                    for m, c0, c1 in ((P, 0, NCH), (NS, NCH, NCH + 1)):
                        w = slice(c0 * NH, c1 * NH)
                        for q, dst in enumerate((aT, dT, CD)):
                            st(dve.tensor_copy(dst[0:m, c0:c1, :].rearrange("p c h -> p (c h)"), PS[0:m, 0, q * 160 + w.start:q * 160 + w.stop]))
                    st.wait()
                    dve.tensor_tensor(DE[:, :, :], CD[:, :, :], aT[:, :, :], ALU.subtract).then_inc(s["alb_sub"], 1)
                    dve.wait_ge(s["hist_tr"], 1)
                    dve.tensor_copy(hist[:, :, :].rearrange("p (a c) k -> p a (c k)", a=2), PS[:, 2:4, 0:16 * 24]).then_inc(s["hist_copied"], 1)
                    dve.wait_ge(s["hist_copied"], 1)
                    dve.wait_ge(s["de_done"], 1)
                    d = ph["ssd"]
                    cw3 = CWT[:, :].rearrange("p (w c) -> p w c", w=CW)

                    def group(g):
                        st = Steps(dve, s["ve"], g * VE)
                        dve.wait_ge(s["group_end"], g + 1)
                        for ti, ct in enumerate(CT(g)):
                            dve.tensor_copy(cwg[:, ti, 0:CW], cw3[:, :, bass.ds(ct, 1)].rearrange("p w o -> p (w o)"))
                            dve.tensor_copy(cwg[:, ti, 4:5], CB[:, bass.ds(ct, 1)])
                        hs = bass.ds(g * 4, 4)
                        for dst, src in ((aTg, aT), (dTg, dT), (DEg, DE), (CDg, CD)):
                            dve.tensor_copy(dst[:, :, :], src[:, :, hs])
                        dve.tensor_copy(EASg[:, :], EAS[:, hs])
                        dve.tensor_copy(DCg[:, :], DC[:, bass.ds(g * 2, 2)])
                        dve.tensor_copy(selg[:, :], con[0:NH, hs])
                        dve.tensor_copy(selp[:, :, :], con[0:NH, hs].unsqueeze(2).to_broadcast([NH, 4, PD])).then_inc(s["col_g"], 1)
                        dve.wait_ge(s["col_g"], g + 1)

                        def history(ti, ct):
                            if ti >= 2:
                                dve.wait_ge(s["taps"], g * 4 + ti - 2 + 1 + 2)
                                dve.wait_ge(s["cvn_done"], g * 4 + ti - 2 + 1 + 2)
                            dve.tensor_copy(pres[:, ti % 2, :, 0:CW - 1], hist[:, bass.ds(ct, 1), :].rearrange("p o (b r) -> p (o b) r", b=NB)).then_inc(s["hist_g"], 1)

                        cts = CT(g)
                        history(0, cts[0])
                        history(1, cts[1])
                        for j in range(6):
                            split(d.u0 + g * 6 + j + 1, (d.u0 + j + 1) % 2)
                            if j >= 4:
                                continue
                            b = j % 2
                            dve.wait_ge(s["tap0"], g * 4 + j + 1)
                            for w in range(1, CW):
                                st(dve.scalar_tensor_tensor(out=xbc[:, j, 0:SEQ], in0=pre[:, b, w:w + SEQ], scalar=cwg[:, j, w:w + 1], in1=xbc[:, j, 0:SEQ], op0=ALU.mult, op1=ALU.add))
                                xs = xbc[:, j, SEQ:T].rearrange("p (b t) -> p b t", b=NB)
                                ins = dve.scalar_tensor_tensor(out=xs, in0=pres[:, b, :, w:w + NT], scalar=cwg[:, j, w:w + 1], in1=xs, op0=ALU.mult, op1=ALU.add)
                                if w < CW - 1:
                                    st(ins)
                                    st.wait()
                                else:
                                    ins.then_inc(s["taps"], 1)
                            if j < 2:
                                history(j + 2, cts[j + 2])
                        dve.wait_ge(s["tok_ready"], g + 1)
                        st(dve.tensor_copy(btok[0:NS, NCH, :], PS[0:NS, 5, 0:P]))
                        heads = lambda t, m, c0, c1: t[0:m, c0:c1, :].unsqueeze(3).to_broadcast([m, c1 - c0, 4, PD])
                        four = lambda ap: ap.rearrange("p c (h w) -> p c h w", h=4)
                        st(dve.tensor_tensor(xd[0:NS, NCH, :].rearrange("p (h w) -> p h w", h=4), PS[0:NS, 5, P:P + 256].rearrange("p (h w) -> p h w", h=4), dTg[0:NS, NCH, :].unsqueeze(2).to_broadcast([NS, 4, PD]), ALU.mult))
                        st(dve.tensor_tensor(cbm[0:NS, SEQ:T], PS[0:NS, 5, 384:384 + NS], small, ALU.mult))
                        dve.tensor_copy(cds[:, :], PS[:, 5, 416:432]).then_inc(s["small_read"], 1)
                        for k in range(2):
                            ins = dve.tensor_tensor(four(xd[:, 2 * k:2 * k + 2, :]), PS[:, 6 + k, :].rearrange("p (c h w) -> p c h w", c=2, h=4), heads(dTg, P, 2 * k, 2 * k + 2), ALU.mult)
                        ins.then_inc(s["xd_ready"], 1)
                        dve.wait_ge(s["xd_ready"], g + 1)
                        st.wait()
                        dve.tensor_tensor(xdd[0:NS, NCH, :].rearrange("p (h w) -> p h w", h=4), xd[0:NS, NCH, :].rearrange("p (h w) -> p h w", h=4), DEg[0:NS, NCH, :].unsqueeze(2).to_broadcast([NS, 4, PD]), ALU.mult)
                        dve.tensor_tensor(four(xdd[:, 0:NCH, :]), four(xd[:, 0:NCH, :]), heads(DEg, P, 0, NCH), ALU.mult).then_inc(s["xdd_ready"], 1)
                        dve.wait_ge(s["cb_ready"], g + 1)
                        dve.tensor_tensor(cbm[:, 0:SEQ].rearrange("p (c t) -> p c t", c=NCH), PS[:, 0, :].rearrange("p (c t) -> p c t", c=NCH), causal.unsqueeze(1).to_broadcast([P, NCH, P]), ALU.mult).then_inc(s["cbm_ready"], 1)
                        dve.wait_ge(s["bcs_ready"], g + 1)
                        dve.tensor_copy(bcsS[:, :, :].rearrange("p h t -> p (h t)"), PS[0:NS, 5, 0:QH * NS]).then_inc(s["bcs_read"], 1)
                        dve.wait_ge(s["bcs_read"], g + 1)

                        def seg(h):
                            dve.wait_ge(s["bc_read"], g * 4 + h + 1)
                            if h >= 2:
                                dve.wait_ge(s["y_used"], g * 4 + h - 1)
                            dve.tensor_scalar(Lh[0:NS, h % 2, SEQ:T], bcsS[:, h, :], aTg[0:NS, NCH, h:h + 1], 0.0, ALU.subtract, ALU.min)
                            for c in range(NCH):
                                ins = dve.tensor_scalar(Lh[:, h % 2, c * P:(c + 1) * P], bcS[:, h % 2, c * P:(c + 1) * P], aTg[:, c, h:h + 1], 0.0, ALU.subtract, ALU.min)
                            ins.then_inc(s["seg_ready"], 1)

                        def masked(h):
                            dve.wait_ge(s["lexp"], g * 4 + h + 1)
                            dve.tensor_tensor(Lh[0:NS, h % 2, SEQ:T], Lh[0:NS, h % 2, SEQ:T], cbm[0:NS, SEQ:T], ALU.mult)
                            dve.tensor_tensor(Lh[:, h % 2, 0:SEQ], Lh[:, h % 2, 0:SEQ], cbm[:, 0:SEQ], ALU.mult).then_inc(s["m_ready"], 1)

                        seg(0)
                        dve.wait_ge(s["st_ready"], g + 1)
                        st(dve.tensor_copy(ST[:, 0, :], PS[:, 2, 0:256]))
                        st.wait()
                        for c in range(1, NCH):
                            st(dve.tensor_tensor(tmpS[:, :].rearrange("p (h w) -> p h w", h=4), ST[:, c - 1, :].rearrange("p (h w) -> p h w", h=4), CDg[:, c, :].unsqueeze(2).to_broadcast([P, 4, PD]), ALU.mult))
                            st.wait()
                            ins = dve.tensor_tensor(ST[:, c, :], tmpS[:, :], PS[:, 2 + c // 2, (c % 2) * 256:(c % 2 + 1) * 256], ALU.add)
                            if c < NCH - 1:
                                st(ins)
                                st.wait()
                            else:
                                ins.then_inc(s["st_done"], 1)
                        seg(1)
                        masked(0)
                        masked(1)
                        seg(2)
                        masked(2)
                        dve.wait_ge(s["yoff_ready"], g + 1)
                        dve.tensor_tensor(yos[:, :].rearrange("p (h w) -> p h w", h=4), PS[0:NS, 4, 0:256].rearrange("p (h w) -> p h w", h=4), EASg[:, :].unsqueeze(2).to_broadcast([NS, 4, PD]), ALU.mult).then_inc(s["yos_ready"], 1)

                        def new_states(q):
                            if q == 0:
                                dve.wait_ge(s["cds_exp"], g + 1)
                            dve.wait_ge(s["nst_free"], g * 2 + q + 1)
                            st(dve.tensor_tensor(nst[:, :, :], S0[:, q], cds[:, q * NB:(q + 1) * NB].unsqueeze(2).to_broadcast([P, NB, P]), ALU.mult))
                            st.wait()
                            dve.wait_ge(s["news_ready"], g * 2 + q + 1)
                            flat = nst[:, :, :].rearrange("p (a b) n -> p a (b n)", a=2)
                            dve.tensor_tensor(flat, flat, PS[:, 6:8, :], ALU.add).then_inc(s["news_read"], 1)

                        new_states(0)
                        seg(3)
                        masked(3)
                        new_states(1)
                        dve.wait_ge(s["y_ready"], g + 1)
                        for q in range(2):
                            dve.wait_ge(s["y_used"], g * 4 + 4)
                            y = M1[:, bass.ds(g * 2 + q, 1), :].rearrange("p o t -> p (o t)")
                            st(dve.scalar_tensor_tensor(out=xbc[:, 2 + q, 0:SEQ], in0=xbc[:, 2 + q, 0:SEQ], scalar=DCg[:, q:q + 1], in1=PS[:, 2 + q, :], op0=ALU.mult, op1=ALU.add))
                            st(dve.scalar_tensor_tensor(out=xbc[:, 2 + q, SEQ:T], in0=xbc[:, 2 + q, SEQ:T], scalar=DCg[:, q:q + 1], in1=PS[:, 5, 128 + q * NS:128 + (q + 1) * NS], op0=ALU.mult, op1=ALU.add))
                            st.wait()
                            st(dve.tensor_tensor(xbc[:, 2 + q, SEQ:T], xbc[:, 2 + q, SEQ:T], PS[:, 5, 192 + q * NS:192 + (q + 1) * NS], ALU.add))
                            st.wait()
                            st(dve.tensor_tensor(y, xbc[:, 2 + q, :], sz[:, q, :], ALU.mult))
                        st.wait()
                        dve.wait_ge(s["rest_out"], g + 1)
                        dve.sem_inc(s["group_end"], 1)
                        assert st.n == VE, st.n
                    step_loop(dve, NG, group)
                    n.ev = [n.ev[0] + 2 * NG, n.ev[1] + 2 * NG, n.ev[2] + NG, n.ev[3] + NG]
                    d = ph["qm", 0]

                    def queries(d):
                        def body(i):
                            for j in range(2):
                                split(d.u0 + i * 2 + j + 1, (d.u0 + j + 1) % 2)
                        step_loop(dve, d.n, body)
                        for j in range(2):
                            n.ev[j] += d.n
                    queries(d)
                    inverse()
                    dve.sem_inc(s["att_go"], 1)
                    attention(0)
                    for k in range(24 + 2):
                        if k < KI:
                            dve.scalar_tensor_tensor(out=M1[:, k, :], in0=M1[:, k, :], scalar=CB[:, 32 + k:33 + k], in1=rb[:, :], op0=ALU.mult, op1=ALU.mult).then_inc(s["t_ready"], 1)
                        if k >= 2:
                            dve.wait_ge(s["hi_ready"], n.t + k - 1)
                            dve.tensor_tensor(L24[:, k - 2, :], M1[:, k - 2, :], H24[:, k - 2, :].bitcast(F32), ALU.subtract).then_inc(s["lo_ready"], 1)
                    n.t += 24
                    narrow(ph["out", 0])
                    residual(gain(0, 3))
                else:
                    to_h(gain(1, 2))
                    queries(ph["in_b"])
                    queries(ph["qm", 1])
                    for j in range(2):
                        dve.wait_ge(evac[j], n.ev[j] + 1)
                    dve.sem_inc(s["att_go"], 1)
                    attention(1)

                    def soften(t):
                        dve.wait_ge(s["ds_ev"], t + 1)
                        n_ = sum(n for _, _, n in spans(t % NCH)) if t < 16 else NEW0 + GD * NS
                        dve.tensor_reduce(dm[:, t % 2:t % 2 + 1], SS[:, t % 2, 0:n_], AX_X, ALU.max, negate=True).then_inc(s["dmx"], 1)

                    def biased(t):
                        h, i = t // NCH, t % NCH
                        dve.wait_ge(s["ds_ready"], t + 1)
                        if t >= 2:
                            dve.wait_ge(s["dptr"], t - 1)
                        c = 0
                        for g, first, n_ in spans(i):
                            ins = dve.scalar_tensor_tensor(out=SS[:, t % 2, c:c + n_], in0=tab[:, (g + 1) * SEQ - n_:(g + 1) * SEQ], scalar=-SLOPES[g][h], in1=PS[:, g, 0:n_], op0=ALU.mult, op1=ALU.add)
                            c += n_
                        ins.then_inc(s["ds_ev"], 1)
                        soften(t)

                    def divided(t):
                        n_ = sum(n for _, _, n in spans(t % NCH)) if t < 16 else NEW0 + GD * NS
                        b = t % 2
                        dve.wait_ge(s["dexp"], t + 1)
                        dve.reciprocal(di[:, b:b + 1], dr[:, b:b + 1]).then_inc(s["drcp"], 1)
                        dve.wait_ge(s["drcp"], t + 1)
                        dve.tensor_scalar(SS[:, b, 0:n_], SS[:, b, 0:n_], di[:, b:b + 1], None, ALU.mult).then_inc(s["dp_ready"], 1)

                    biased(0)
                    for t in range(16):
                        if t + 1 < 16:
                            biased(t + 1)
                        divided(t)
                    dve.wait_ge(s["ds_ready"], 17)
                    dve.wait_ge(s["dptr"], 16)
                    for g, c0, c1 in OLD:
                        dve.scalar_tensor_tensor(out=SS[:, 0, c0:c1], in0=tab[:, GD * SEQ + c0:GD * SEQ + c1], scalar=negc[:, g:g + 1], in1=PS[:, 3 + g, 0:c1 - c0], op0=ALU.mult, op1=ALU.add)
                    for g in range(GD):
                        c0 = NEW0 + g * NS
                        ins = dve.scalar_tensor_tensor(out=SS[:, 0, c0:c0 + NS], in0=tab[:, GD * SEQ + c0:GD * SEQ + c0 + NS], scalar=negc[:, g:g + 1], in1=PS[:, 6, g * NS:(g + 1) * NS], op0=ALU.mult, op1=ALU.add)
                    ins.then_inc(s["ds_ev"], 1)
                    soften(16)
                    divided(16)
                    dve.wait_ge(s["dptr"], 17)
                    for sl in range(4):
                        m = P if sl < 3 else 64
                        z = QZD[0:m, sl]
                        dve.tensor_copy(bass.AP(z.tensor, z.offset, [list(z.ap[0]), [P + 16, NB], [1, 16]]), PS[0:m, 0, sl * P:(sl + 1) * P].rearrange("p (b r) -> p b r", b=NB))
                    dve.tensor_copy(PTn[:, :, :].rearrange("p g r -> p (g r)"), PS[0:NS, 1, 0:GD * P]).then_inc(s["dpt_ev"], 1)
                    dve.wait_ge(s["dptr"], 18)
                    for h in range(QH):
                        src = PS[:, 3, (h // 2) * P:(h // 2 + 1) * P].rearrange("p (b h t) -> p b h t", b=NB, h=QH)[:, :, h, :]
                        ins = dve.tensor_copy(M1[:, h, SEQ:T].rearrange("p (b t) -> p b t", b=NB), src)
                    ins.then_inc(s["dil_done"], 1)
                    for k in range(12):
                        dve.wait_ge(s["hi_ready"], n.t + k + 1)
                        dve.tensor_tensor(L24[:, k, :], M1[:, k, :], H24[:, k, :].bitcast(F32), ALU.subtract).then_inc(s["lo_ready"], 1)
                    n.t += 12
                    narrow(ph["out", 1])
                    residual(gain(1, 3))
                ffn(l, 1)
                if l == 0:
                    to_h(col(96))
                    body = wide(ph["kv"], NCH + 1)
                    for i in range(GD):
                        n.out = 8
                        body(i)
            inverse()
            for k in range(KD):
                scaled(y_of, x_of, col(120))(k).then_inc(s["t_ready"], 1)

        @block.gpsimd
        def _(pool):
            n = Place()
            mk = O["mem_kv"].rearrange("l a (t p) c h d -> l p (a t) (c h d)", p=P)
            blocks = stores = 0

            def stored(k):
                nonlocal stores
                stores += k
                pool.wait_ge(s["blk_out"], 16 * stores)
                pool.nop().then_inc(s["stage_free"], 1)

            for l in range(DEPTH):
                for i in range(4):
                    blocks += 2
                    pool.wait_ge(s["blk_evac"], blocks + 1)
                    pool.dma_start(mk[l, :, :, i * 512:(i + 1) * 512], stage[:, 0:2, :]).then_inc(s["blk_out"], 16)
                    stored(1)

            def kv_out():
                nonlocal blocks
                for g in range(GD):
                    blocks += NCH + 1
                    pool.wait_ge(s["blk_evac"], blocks + 1)
                    c = slice(g * 512, (g + 1) * 512)
                    w = O[f"win_p{g}"].rearrange("a r c h d -> (a r) (c h d)")
                    pool.dma_start(kvs[0:SEQ, c].rearrange("(t p) c -> p t c", p=P), stage[:, 0:NCH, :]).then_inc(s["blk_out"], 16)
                    pool.dma_start(kvs[SEQ:T, c], stage[P - NS:P, NCH, :]).then_inc(s["blk_out"], 16)
                    pool.dma_start(O[f"win_s{g}"].rearrange("b t c h d -> (b t) (c h d)"), stage[P - NS:P, NCH, :]).then_inc(s["blk_out"], 16)
                    if g == 0:
                        pool.dma_start(w, stage[:, NCH - 1, :]).then_inc(s["blk_out"], 16)
                    else:
                        pool.dma_start(w.rearrange("(t p) c -> p t c", p=P), stage[:, 0:NCH, :]).then_inc(s["blk_out"], 16)
                    stored(4)
            mkc = A["cache_mem_kv"].rearrange("l b (t p) c h d -> l b p t c (h d)", p=P)
            kv_in = [s["kv_in0"], s["kv_in1"], s["kv_in2"]]

            def attention_loads(l, q):
                pool.wait_ge(s["att_go"], l + 1)
                pool.memset(QZ[:, :, :, :], 0.0).then_inc(s["qz_zero"], 1)
                pool.memset(PZ[:, :, :, :], 0.0).then_inc(s["qz_zero"], 1)
                order = [(None, 0), (None, 1)] + [(b, c) for c in range(2) for b in range(NB)]
                for idx, (b, c) in enumerate(order):
                    if idx >= 3:
                        what, last = [("kt_tr", l + 1), ("pv_ready", MH * (l + 1))][idx - 3] if idx < 5 else \
                            ("ks_tr", 16 * l + 2 * (idx - 4)) if idx < 13 else ("vb_done", NB * l + idx - 12)
                        pool.wait_ge(s[what], last)
                    src = mk[l].rearrange("p t (c n) -> p t c n", c=2)[:, :, c, :] if b is None else mkc[l, b][:, :, c, :]
                    pool.dma_start(kvr[:, idx % 3], src).then_inc(kv_in[idx % 3], 16)
                    if idx == 2:
                        pool.wait_ge(s["qz_zero"], 2 * l + 2)
                        for hk in range(8):
                            z = QZ[:, hk, :, :]
                            dst = bass.AP(z.tensor, z.offset + (hk // 2) * NT, [list(z.ap[0]), [P + 16, NB], [1, NT]])
                            pool.tensor_copy(dst, q[:, hk, SEQ:T].rearrange("p (b t) -> p b t", b=NB)).then_inc(s["q_ready"], 1)
            cpo = O["conv_p"].rearrange("a b r c -> (a b r) c")
            cso = O["conv_s"].rearrange("a b r c -> (a b r) c")
            spo = O["ssm_p"].rearrange("a b (g q r) p n -> g (a b r p) q n", g=NG, q=2)
            sso_s = O["ssm_s"].rearrange("a b (g q r) p n -> g q (r p) (a b) n", g=NG, q=2)
            pool.wait_ge(s["alb_sub"], 1)
            pool.memset(CZ[:, :, :], 0.0).then_inc(s["pz"], 1)
            pool.memset(pre[:, :, 0:CW - 1], 0.0).then_inc(s["pz"], 1)
            pool.wait_ge(s["pz"], 2)

            def group(g):
                pool.wait_ge(s["group_end"], g + 1)
                for ti in range(4):
                    b = ti % 2
                    pool.wait_ge(s["tap0"], g * 4 + ti + 1)
                    pool.sem_inc(s["passed"], 1)
                    pool.tensor_copy(cvn[:, ti, 0:3], pre[:, b, SEQ:SEQ + CW - 1])
                    pool.tensor_copy(cvn[:, ti, 3:27].rearrange("p (b r) -> p b r", b=NB), pres[:, b, :, NT:NT + CW - 1]).then_inc(s["cvn_done"], 1)
                pool.wait_ge(s["conv_done"], g * 4 + 4)
                pool.sem_inc(s["passed"], 1)
                cz = CZ[:, :, :]
                pool.tensor_copy(bass.AP(cz.tensor, cz.offset, [list(cz.ap[0]), [NS + NT, NB], [1, NT]]), xbc[:, 1, SEQ:T].rearrange("p (b t) -> p b t", b=NB)).then_inc(s["cz_ready"], 1)
                pool.wait_ge(s["small_read"], g + 1)
                pool.tensor_tensor(BZ[:, :, :], btok[0:NS, NCH, :].unsqueeze(1).to_broadcast([NS, NB, P]), own.unsqueeze(2).to_broadcast([NS, NB, P]), ALU.mult).then_inc(s["bz_ready"], 1)
                for h in range(4):
                    pool.wait_ge(s["bc_read"], g * 4 + h + 1)
                    pool.tensor_tensor(Eh[:, h % 2, :], Eh[:, h % 2, :], xbc[:, 1, 0:SEQ], ALU.mult).then_inc(s["c_ready"], 1)
                    if h == 1:
                        pool.wait_ge(s["cvo_done"], g + 1)
                        pool.sem_inc(s["passed"], 1)
                        for t, c in enumerate((D * 2 + g * P, D * 3 + g * P, g * 256)):
                            w = P if t < 2 else 256
                            src = cvo[:, t:t + 1 + (t == 2), :].rearrange("p a c -> p (a c)")
                            pool.dma_start(cpo[:, bass.ds(c, w)], src[0:3]).then_inc(s["group_out"], 16)
                            pool.dma_start(cso[:, bass.ds(c, w)], src[3:27]).then_inc(s["group_out"], 16)
                for q in range(2):
                    pool.wait_ge(s["news_read"], g * 2 + q + 1)
                    pool.sem_inc(s["passed"], 1)
                    pool.dma_start(sso_s[bass.ds(g, 1), q].rearrange("o p b n -> p (o b) n"), nst[:, :, :]).then_inc(s["news_out"], 16)
                    pool.wait_ge(s["news_out"], g * 32 + q * 16 + 16)
                    pool.sem_inc(s["nst_free"], 1)
                pool.wait_ge(s["final_read"], g + 1)
                pool.sem_inc(s["passed"], 1)
                pool.dma_start(spo[bass.ds(g, 1)].rearrange("o p q n -> p (o q) n"), sso[:, :, :]).then_inc(s["group_out"], 16)
                pool.wait_ge(s["group_out"], g * 112 + 112)
                pool.sem_inc(s["rest_out"], 1)
            step_loop(pool, NG, group)
            attention_loads(0, yT)
            kv_out()
            attention_loads(1, yT)
            pool.wait_ge(s["att_done"], 2)
            pool.dma_start(kvd[:, :, :], kvs[0:SEQ, :].rearrange("(t p) c -> p t c", p=P)).then_inc(s["dil_in"], 16)
            pool.dma_start(tab[:, :], A["c_dil"]).then_inc(s["dil_in"], 16)
            pool.dma_start(kvn[:, :], kvs[SEQ:T, :]).then_inc(s["dil_in"], 16)
            win = [A[f"cache_win_g{g + 1}"].rearrange("b e c h d -> b e c (h d)") for g in range(GD)]

            def far_rows(c):
                w = win[2]
                for r in range(NT):
                    src = bass.AP(w.tensor, w.offset + r * 512 + c * 256, [[DILS[2][1] * 512, 16], [256 * 512, NB], [1, 256]])
                    pool.dma_start(Kc[r * 16:(r + 1) * 16, :, 3, :], src).then_inc(s[("dks_in", "dv_in")[c]], 16)

            pool.dma_start(Kc[:, :, 0, :], win[0][:, :, 0, :].rearrange("b p n -> p b n")).then_inc(s["dks_in"], 16)
            for t in range(2):
                pool.dma_start(Kc[:, :, 1 + t, :], win[1][:, t * P:(t + 1) * P, 0, :].rearrange("b p n -> p b n")).then_inc(s["dks_in"], 16)
            far_rows(0)

            def sample_queries(dst, batch_step, done):
                for g in range(GD):
                    for kv in range(KVH):
                        z = dst[:, 2 * g + kv]
                        q = M1[:, 12 + g * QH + 2 * kv:12 + g * QH + 2 * kv + 2, SEQ:T]
                        for h in range(2):
                            ins = pool.tensor_copy(bass.AP(z.tensor, z.offset + (2 * kv + h) * NT, [list(z.ap[0]), [batch_step, NB], [1, NT]]),
                                                   q[:, h, :].rearrange("p (b t) -> p b t", b=NB))
                ins.then_inc(s[done], 1)

            pool.memset(QN[:, :, :], 0.0).then_inc(s["qn_zero"], 1)
            pool.wait_ge(s["qn_zero"], 1)
            sample_queries(QN, 16, "qn_done")
            pool.wait_ge(s["do_ready"], 16)
            pool.memset(QZD[:, :, :, :], 0.0).then_inc(s["qd_zero"], 1)
            pool.wait_ge(s["qd_zero"], 1)
            sample_queries(QZD, P + 16, "qd_done")
            for b in range(NB):
                pool.wait_ge(s["dks_tr"], 2 * b + 2)
                pool.dma_start(Kc[:, b, 0, :], win[0][b, :, 1, :]).then_inc(s["dv_in"], 16)
                pool.dma_start(Kc[:, b, 1:3, :], win[1][b, :, 1, :].rearrange("(t p) n -> p t n", p=P)).then_inc(s["dv_in"], 16)
            far_rows(1)


_OUTS = [("y_prompt", (1, SEQ, D)), ("y_sample", (NB, NT, D)), ("mem_kv", (DEPTH, 1, NM, 2, MH, MD)),
         ("ssm_p", (1, 1, NH, PD, P)), ("conv_p", (1, 1, CW - 1, CONV_DIM)),
         ("win_p0", (1, P, 2, KVH, HD)), ("win_p1", (1, SEQ, 2, KVH, HD)), ("win_p2", (1, SEQ, 2, KVH, HD)),
         ("ssm_s", (1, NB, NH, PD, P)), ("conv_s", (1, NB, CW - 1, CONV_DIM)),
         ("win_s0", (NB, NT, 2, KVH, HD)), ("win_s1", (NB, NT, 2, KVH, HD)), ("win_s2", (NB, NT, 2, KVH, HD))]


def kernel(**inputs):
    import numpy as _np
    import concourse.bacc as _bacc
    from concourse import mybir as _mybir
    from concourse.bass_utils import run_bass_kernel_spmd as _run

    nc = _bacc.Bacc("TRN2", target_bir_lowering=False, num_devices=1)
    given = {name: _np.ascontiguousarray(a) for name, a in inputs.items()}
    given["c_base"], given["c_dil"], given["c_reset"] = constants()
    arrays, ins, outs = {}, {}, {}
    for name, a in given.items():
        arrays[f"in_{name}"] = a
        ins[name] = nc.dram_tensor(f"in_{name}", a.shape, _mybir.dt.from_np(a.dtype), kind="ExternalInput").ap()
    for name, shape in _OUTS:
        outs[name] = nc.dram_tensor(f"out_{name}", shape, _mybir.dt.float32, kind="ExternalOutput").ap()
    build_trunk(nc, ins, outs)
    r = _run(nc, [arrays], core_ids=[0])
    return tuple(r.results[0][f"out_{name}"] for name, _ in _OUTS)
```

```python
from contextlib import ExitStack

import numpy as np

import concourse.bass as bass
from concourse import mybir

F32 = mybir.dt.float32
F32R = mybir.dt.float32r
ACT = mybir.ActivationFunctionType
ALU = mybir.AluOpType
AX_X = mybir.AxisListType.X

P = 128
D = 1024
KD = D // P
SEQ, NB, NT = 512, 8, 4
NS = NB * NT
T = SEQ + NS
HT = T // 2
HP = SEQ - HT
FF = 2816
KF = FF // P
DEPTH = 2
DI = 2048
KI = DI // P
NH, NG, RPG, PD = 32, 8, 4, 64
NCH = SEQ // P
CONV_DIM = 4096
CW = 4
XBC0 = DI
DT0 = DI + CONV_DIM
QM0 = DT0 + NH
NM, MH, MD = 256, 4, 256
GD = 3
QH, KVH, HD = 4, 2, 128
DILS = ((128, 1), (512, 4), (2048, 16))
WINS = (128, 256, 256)
EPS = 1e-6
BIG = 1e30
NEW0 = 448
U = 8 * P


def constants():
    p = np.arange(P)
    ident = np.eye(P, dtype=np.float32)
    ones = np.ones((P, P), np.float32)
    causal = (p[:, None] <= p[None, :]).astype(np.float32)
    s = np.arange(NS)
    small = np.zeros((P, NS), np.float32)
    small[:NS] = (s[:, None] <= s[None, :]) & (s[:, None] // NT == s[None, :] // NT)
    own = np.zeros((P, NB), np.float32)
    own[:NS] = s[:, None] // NT == np.arange(NB)[None, :]
    eps = np.full((P, 1), EPS, np.float32)
    slope = 2.0 ** (-8.0 * np.arange(1, GD * QH + 1) / (GD * QH)).reshape(GD, QH)
    neg = -slope[:, (p // NT) % QH].T.astype(np.float32)
    base = np.concatenate([ident, ones, causal, small, own, eps, neg], 1).astype(np.float32)
    dist = 384 + p[:, None] - np.arange(SEQ)[None, :]
    tabs = []
    for w, dil in DILS:
        ok = (dist >= 0) & (dist <= w) & (dist % dil == 0)
        tabs.append(np.where(ok, dist, BIG))
    t, b = (p % NT)[:, None], (p // (NT * QH))[:, None]
    e = np.arange(P)[None, :]
    c1 = np.where(e >= t, 128 + t - e, BIG)
    e = np.arange(256)[None, :]
    c2 = np.where((e - t) % 4 == 0, 256 + t - e, BIG)
    r, a = np.arange(64)[None, :] // 16, np.arange(64)[None, :] % 16
    c3 = np.where(r == t, 256 + t - 16 * a - r, BIG)
    bb, tt = s[None, :] // NT, s[None, :] % NT
    new = [np.where((bb == b) & (tt <= t) & ((t - tt) % dil == 0), t - tt, BIG) for _, dil in DILS]
    dilc = np.concatenate(tabs + [c1, c2, c3] + new, 1).astype(np.float32)
    reset = np.ones((NH, T), np.float32)
    reset[:, 0:SEQ:P] = 0
    reset[:, SEQ::NT] = 0
    return base, dilc, reset


NBASE = 3 * P + NS + NB + 1 + GD
NDIL = GD * SEQ + NEW0 + GD * NS
SLOPES = [[2.0 ** (-8.0 * (g * QH + h + 1) / (GD * QH)) for h in range(QH)] for g in range(GD)]


class Dense:

    def __init__(self, plan, n, tiles, nks):
        self.n, self.tiles, self.nks = n, tiles, nks
        self.k0 = [sum(nks[:q]) for q in range(len(nks))]
        self.ub = tiles * len(nks)
        self.u0 = plan["units"]
        plan["units"] += n * self.ub
        assert n == 1 or self.ub % 2 == 0


def step_loop(eng, n, body, first=0):
    with eng.Fori(first, n) as i:
        body(i)


CREDITS = (("group_end", 1), ("taps", 2), ("cvn_done", 2), ("nst_free", 1), ("news_read", 1),
           ("rest_out", 1), ("y_read", 1))

SEMS = """const_in x_in row_in cols_out x_tr mem_in mem_sq mem_rt mem_rb mem_sc mem_tr mem_ev
 w_hi w_lo w_mm evac0 evac1 evac2 evac3 mid_hi mid_lo sq_ready sq_used rt_ready rb_ready
 t_ready hi_ready lo_ready pn_t x_done blk_evac blk_out stage_free w_in0 w_in1 f_tr f_ev y_out
 warmed m_in0 m_in1 m_in2 m_in3 conv_in hist_tr dt_e dt_u dt_ln dt_v scan_done dtt_tr alb_sub de_done na_ready
 col_g hist_g tap0 taps conv_done cvn_done tok_ready cb_ready cvt_ready small_read btok_ready
 xd_ready xdd_ready cbm_ready bcs_ready bcs_read st_ready st_done bc_ready bc_read seg_ready lexp m_ready
 c_ready s0_in s0t_ready s0t_evac yoff_ready yos_ready news_ready news_read news_out cds_exp final_ready
 final_read y_ready y_read cz_ready bz_ready cvo_done group_end ve rest_out silu_done sg_ready pz hist_copied y_used nst_free group_out passed
 kv_in0 kv_in1 kv_in2 att_go kt_tr kt_ev sc_ready mx_ready p_exp p_rcp p_ready ptr_ready pt_evac pv_ready pv_evac
 q_ready ks_tr ks_ev ss_ready smx s_exp s_rcp s_p s_tr pz_ready vb_done so_ev so_tr att_done qz_zero
 dil_in dkt_tr dkt_ev ds_ready ds_ev dmx dexp drcp dp_ready dptr dpt_ev do_ready do_ev
 dks_in dv_in dks_tr dks_ev dss_ready qs_zero qn_done qd_done dil_done
""".split()


def build_trunk(nc, A, O):
    with ExitStack() as ctx:
        s = {n: ctx.enter_context(nc.semaphore(n)) for n in SEMS}
        evac = [s[f"evac{j}"] for j in range(4)]
        w_in = [s["w_in0"], s["w_in1"]]
        m_in = [s[f"m_in{j}"] for j in range(4)]

        top = [16512]

        def keep(name, shape, dt=F32):
            t = nc.alloc_sbuf_tensor_at(name, shape, dt, offset=top[0])
            size = 4
            for d in shape[1:]:
                size *= d
            top[0] += (size + 31) // 32 * 32
            return t

        con = keep("con", [P, NBASE])
        G = keep("G", [P, P])
        GH = keep("GH", [P, P])
        CWB = keep("CWB", [P, P + 48])
        CWT, CB = CWB[:, 0:P], CWB[:, P:]
        DC = keep("DC", [P, KI])
        dtb = keep("dtb", [NH, 1])
        alog = keep("alog", [NH, 1])
        rb = keep("rb", [P, T])
        xT = keep("xT", [P, KD, T])
        raw = keep("raw", [P, 2, U])
        whi = keep("whi", [P, 2, U], F32R)
        wlo = keep("wlo", [P, 2, U], F32R)
        H0 = top[0]
        hH = keep("hH", [P, KD, T], F32R)
        hL = keep("hL", [P, KD, T], F32R)
        Y0 = top[0]
        yT = keep("yT", [P, KD, T])
        M10 = top[0]
        L24 = keep("L24", [P, 24, T], F32R)
        M20 = top[0]
        H24 = keep("H24", [P, 24, T], F32R)
        E0 = top[0]
        tile_b = T * 4

        def at(name, shape, offset, dt=F32):
            return nc.alloc_sbuf_tensor_at(name, shape, dt, offset=offset)

        M1 = at("M1", [P, 24, T], M10)
        sqb = at("sqb", [P, 2, T], H0 + 8 * tile_b)
        rt = at("rt", [P, T], H0 + 10 * tile_b)
        acc = at("acc", [P, T], H0 + 11 * tile_b)
        sqf = at("sqf", [P, 2, T], M20 + 21 * tile_b)
        rtf = at("rtf", [P, T], M20 + 23 * tile_b)
        sg = at("sg", [P, 2, T], Y0)
        prod = at("prod", [P, 2, T], Y0 + 2 * tile_b)
        rows = at("rows", [P, 3, P], Y0)
        xnat = at("xnat", [P, NCH + 1, D], M10)
        memnat = at("memnat", [P, 2, D], M20)
        memT = at("memT", [P, KD, NM], M20 + 8192)
        memsq = at("memsq", [P, D], M20 + 16384)
        mst = at("mst", [P, 8], M20 + 20480)
        rawm = at("rawm", [P, 4, U], M10 + 30720)
        stage = at("stage", [P, NCH + 1, 512], M10 + 20480)

        ident, ones = con[:, 0:P], con[:, P:2 * P]
        causal = con[:, 2 * P:3 * P]
        small = con[0:NS, 3 * P:3 * P + NS]
        own = con[0:NS, 3 * P + NS:3 * P + NS + NB]
        epsc = con[:, 3 * P + NS + NB:3 * P + NS + NB + 1]
        negc = con[:, 3 * P + NS + NB + 1:NBASE]

        PS = ctx.enter_context(nc.psum_tensor("PS", [P, 8, 512], F32))
        kvs = nc.dram_tensor("kvs", (T, GD * 512), F32).ap()

        plan = {"units": 0}
        ph = {}
        for l in range(DEPTH):
            ph["mem", l] = Dense(plan, 4, 1, (2, 2, 2, 2))
        for l in range(DEPTH):
            ph["gu", l, 0] = Dense(plan, 11, 4, (8,))
            ph["down", l, 0] = Dense(plan, 4, 2, (8, 7, 7))
            if l == 0:
                ph["dt"] = Dense(plan, 1, 1, (8,))
                ph["ssd"] = Dense(plan, NG, 6, (8,))
                ph["qm", 0] = Dense(plan, 4, 2, (8,))
                ph["out", 0] = Dense(plan, 4, 2, (8, 8, 8))
            else:
                ph["in_b"] = Dense(plan, 6, 2, (8,))
                ph["qm", 1] = Dense(plan, 4, 2, (8,))
                ph["out", 1] = Dense(plan, 4, 2, (6, 6))
            ph["gu", l, 1] = Dense(plan, 11, 4, (8,))
            ph["down", l, 1] = Dense(plan, 4, 2, (8, 7, 7))
            if l == 0:
                ph["kv"] = Dense(plan, 3, 1, (2, 2, 2, 2))
        U0 = ph["gu", 0, 0].u0

        def gain(l, i):
            return lambda k: G[:, (6 * l + i) * KD + k:(6 * l + i) * KD + k + 1]

        def half_gain(l, i):
            return lambda k: GH[:, (6 * l + i) * KD + k:(6 * l + i) * KD + k + 1]

        def col(c):
            return lambda k: G[:, c + k:c + k + 1]

        x_of = lambda k: xT[:, k, :]
        y_of = lambda k: yT[:, k, :]
        hH_of = lambda k: hH[:, k, :]
        hL_of = lambda k: hL[:, k, :]

        class Place:

            def __init__(self):
                self.ev = [0, 0, 0, 0]
                self.mid = self.blk = self.out = 0
                self.sq = self.norm = self.t = self.res = self.unscaled = self.warm = 0

        class Arena:
            def __init__(self, *regions):
                self.regions = [list(r) for r in regions]

            def __call__(self, name, shape, dt=F32):
                size = 4
                for d in shape[1:]:
                    size *= d
                size = (size + 31) // 32 * 32
                for r in self.regions:
                    if r[1] - r[0] >= size:
                        r[0] += size
                        return at(name, shape, r[0] - size, dt)
                raise ValueError(name)

        A1 = Arena([M20, E0], [Y0, M10], [M10 + 16 * tile_b, M20], [E0, 229344])
        xbc = A1("xbc", [P, 4, T])
        S0 = A1("S0", [P, 2, NB, P])
        S0T = A1("S0T", [P, NB, 256])
        xd = A1("xd", [P, NCH + 1, 256])
        xdd = A1("xdd", [P, NCH + 1, 256])
        sz = A1("sz", [P, 2, T])
        Lh = A1("Lh", [P, 2, T])
        ST = A1("ST", [P, NCH, 256])
        BZ = A1("BZ", [NS, NB, P])
        nst = A1("nst", [P, NB, P])
        pre = A1("pre", [P, 2, SEQ + CW - 1])
        pres = A1("pres", [P, 2, NB, NT + CW - 1])
        bcS = A1("bcS", [P, 2, SEQ])
        Eh = A1("Eh", [P, 2, SEQ])
        hist = A1("hist", [P, 32, NB * 3])
        btok = A1("btok", [P, NCH + 1, P])
        cbm = A1("cbm", [P, T])
        cvo = A1("cvo", [27, 4, P])
        CZ = A1("CZ", [P, NB, NS])
        tmpS = A1("tmpS", [P, 256])
        cvn = A1("cvn", [P, 4, 32])
        yos = A1("yos", [NS, 256])
        sso = A1("sso", [P, 2, P])
        bcsS = A1("bcsS", [NS, QH, NS])
        cds = A1("cds", [P, 2 * NB])
        acum = A1("acum", [NH, T])
        dtx = A1("dtx", [NH, T])
        selp = A1("selp", [NH, 4, PD])
        selg = A1("selg", [NH, 4])
        tokc = A1("tokc", [P, 4, NCH + 1, NH])
        aT, dT, DE, CD = (tokc[:, k] for k in range(4))
        EAS = A1("EAS", [NS, NH])
        tokg = A1("tokg", [P, 4, NCH + 1, 4])
        aTg, dTg, DEg, CDg = (tokg[:, k] for k in range(4))
        EASg = A1("EASg", [NS, 4])
        DCg = A1("DCg", [P, 2])
        cwg = A1("cwg", [P, 4, 8])
        nA = A1("nA", [NH, 1])
        tmpL = A1("tmpL", [NH, NS])
        cvin = at("cvin", [NB * 3, CONV_DIM], M20 + 4 * tile_b)
        dts = at("dts", [NH, 6, T], M20 + 4 * tile_b + 16384 + 4096)
        reset = at("reset", [NH, T], M20 + 4 * tile_b + 16384 + 4096 + 6 * tile_b)
        A2 = Arena([M20, 229344])
        QZ = Arena([H0, Y0])("QZ", [P, 8, NB, P])
        PZ = A2("PZ", [P, 2, NB, P])
        Pb = A2("Pb", [P, NCH, NM])
        Ob = at("Ob", [P, NCH * NM], M20 + 8192)
        PT = A2("PT", [P, 2, SEQ])
        kvr = A2("kvr", [P, 3, 2, D])
        KT = [A2(f"KT{j}", [P, 4, NM]) for j in range(4)]
        am = A2("am", [P, 2, NCH])
        ar = A2("ar", [P, 2, NCH])
        ai = A2("ai", [P, 2, NCH])
        A3 = Arena([H0, M10], [M20, 229344])
        kvd = A3("kvd", [P, NCH, GD * 512])
        tab = A3("tab", [P, NDIL])
        kvn = A3("kvn", [NS, GD * 512])
        PTd = A3("PTd", [P, 2, 10 * P])
        Kc = A3("Kc", [P, NB, 4, 256])
        KTd = A3("KTd", [P, 2 * GD, SEQ])
        SS = A3("SS", [P, 2, 10 * P])
        KTn = A3("KTn", [P, 2 * GD, NS])
        QN = A3("QN", [P, 2 * GD, P])
        dm = A3("dm", [P, 2])
        dr = A3("dr", [P, 2])
        di = A3("di", [P, 2])
        ss_at = M20 + NB * 4 * 256 * 4 + 2 * GD * SEQ * 4
        QZD = at("QZD", [P, 2 * GD, NB, P], H0)
        PTn = at("PTn", [NS, GD, P], ss_at + 10 * P * 4)
        Od = at("Od", [P, 256], ss_at + 10 * P * 4 + GD * P * 4)
        KTb = at("KTb", [P, 4, NEW0], H0 + (NCH * GD * 512 + NDIL + GD * 512) * 4)
        OLD = ((0, 0, P), (1, P, 3 * P), (2, 3 * P, NEW0))

        def spans(i):
            return [(g, f, (i + 1 - f) * P) for g, f in ((0, max(0, i - 1)), (1, 0), (2, 0))]
        CT = lambda g: (16 + g, 24 + g, 2 * g, 2 * g + 1)
        POS = (0, 3, 2, 1, 0, 1)
        QPOS = (0, 3)
        VE = 37

        class Steps:

            def __init__(self, eng, sem, base):
                self.eng, self.sem, self.base, self.n = eng, sem, base, 0

            def __call__(self, ins):
                ins.then_inc(self.sem, 1)
                self.n += 1

            def wait(self):
                self.eng.wait_ge(self.sem, self.base + self.n)

        block = ctx.enter_context(nc.Block())

        @block.sync
        def _(sp):
            sp.dma_start(memnat[:, :, :], A["mem_prompt"].rearrange("a (t p) d -> p (a t) d", p=P)).then_inc(s["mem_in"], 16)
            sp.dma_start(con[:, :], A["c_base"]).then_inc(s["const_in"], 16)
            ng = A["norm_g"].rearrange("l i (k p) -> (l i k) p", p=P)
            for r0, src in ((0, ng), (96, A["kv_norm_g"].rearrange("(k p) -> k p", p=P)),
                            (104, A["mem_norm_g"].rearrange("l (k p) -> (l k) p", p=P)),
                            (120, A["final_norm_g"].rearrange("(k p) -> k p", p=P))):
                sp.dma_start(rows[r0:r0 + src.shape[0], 0, :], src).then_inc(s["const_in"], 16)
            sp.dma_start(rows[:, 1, :], A["conv_w"].rearrange("a w (k p) -> (a w k) p", p=P)).then_inc(s["const_in"], 16)
            sp.dma_start(rows[0:32, 2, :], A["conv_b"].rearrange("a (k p) -> (a k) p", p=P)).then_inc(s["const_in"], 16)
            sp.dma_start(rows[32:48, 2, :], A["ssd_norm_g"].rearrange("a (k p) -> (a k) p", p=P)).then_inc(s["const_in"], 16)

            def load(u, slot, src, nk, cols=P, passed=False):
                sp.wait_ge(s["w_lo"], u + 1)
                if passed:
                    sp.sem_inc(s["passed"], 1)
                sp.dma_start(raw[:, slot, 0:nk * cols].rearrange("p (k n) -> p k n", k=nk), src).then_inc(w_in[slot], 16)

            def kview(w):
                return w.rearrange("(k p) n -> p k n", p=P)

            def wide(d, w, deep=False):
                def body(i):
                    for q in range(4):
                        if deep:
                            if not isinstance(i, int):
                                sp.wait_ge(s["w_lo"], d.u0 + i * 4 + q - 1)
                            sp.dma_start(rawm[:, q, :].rearrange("p (k n) -> p k n", k=2), kview(w)[:, 2 * q:2 * q + 2, bass.ds(i * 512, 512)]).then_inc(m_in[q], 16)
                            continue
                        load(d.u0 + i * 4 + q, (d.u0 + q) % 2, kview(w)[:, 2 * q:2 * q + 2, bass.ds(i * 512, 512)], 2, 512)
                first = deep and d.u0 == 0
                if first:
                    body(0)
                step_loop(sp, d.n, body, first)

            for l in range(DEPTH):
                wide(ph["mem", l], A["w_mem_kv"][l], True)

            def narrow(d, w):
                def body(i):
                    for j in range(2):
                        for q, nk in enumerate(d.nks):
                            u = j * len(d.nks) + q
                            load(d.u0 + i * d.ub + u, (d.u0 + u) % 2, w[:, d.k0[q]:d.k0[q] + nk, bass.ds(i * 256 + j * P, P)], nk)
                step_loop(sp, d.n, body)

            def ffn(l, f):
                d = ph["gu", l, f]
                wg = kview(A["w_ffn_gu"][l, f])

                def gu(i):
                    for j in range(4):
                        c = i * 256 + (j // 2) * P + (j % 2) * FF
                        load(d.u0 + i * 4 + j, (d.u0 + j) % 2, wg[:, :, bass.ds(c, P)], KD)
                step_loop(sp, d.n, gu)
                dn = ph["down", l, f]
                wd = kview(A["w_ffn_down"][l, f])

                def down(i):
                    for j in range(2):
                        for q in range(3):
                            u = 3 * j + q
                            load(dn.u0 + i * 6 + u, (dn.u0 + u) % 2, wd[:, dn.k0[q]:dn.k0[q] + dn.nks[q], bass.ds(i * 256 + j * P, P)], dn.nks[q])
                step_loop(sp, dn.n, down)

            for l in range(DEPTH):
                ffn(l, 0)
                if l == 0:
                    wa = kview(A["w_in_a"][0])
                    u0 = ph["dt"].u0
                    load(u0, u0 % 2, wa[:, :, DT0:DT0 + P], KD)
                    sp.wait_ge(s["w_mm"], u0 + 2)
                    sp.dma_start(cvin[:, :], A["state_conv"].rearrange("a b r c -> (a b r) c")).then_inc(s["conv_in"], 16)
                    sp.dma_start(reset[:, :], A["c_reset"]).then_inc(s["conv_in"], 16)
                    d = ph["ssd"]
                    s0v = A["state_ssm"].rearrange("a b (g q r) p n -> g q (r p) (a b) n", g=NG, q=2)

                    def group(g):
                        for j, c in enumerate((XBC0 + DI + g * P, XBC0 + DI + D + g * P, XBC0 + g * 256, XBC0 + g * 256 + P, g * 256, g * 256 + P)):
                            load(d.u0 + g * 6 + j, (d.u0 + j) % 2, wa[:, :, bass.ds(c, P)], KD, passed=True)
                            if j == 2:
                                sp.wait_ge(s["hist_copied"], 1)
                                sp.wait_ge(s["group_end"], g + 1)
                                sp.sem_inc(s["passed"], 1)
                                for q in range(2):
                                    sp.dma_start(S0[:, q], s0v[bass.ds(g, 1), q].rearrange("o p b n -> p (o b) n")).then_inc(s["s0_in"], 16)
                    step_loop(sp, NG, group)
                    d1 = ph["qm", 0]

                    def queries(i):
                        for j in range(2):
                            load(d1.u0 + i * 2 + j, (d1.u0 + j) % 2, wa[:, :, bass.ds(i * 256 + (QM0 + j * P), P)], KD)
                    step_loop(sp, d1.n, queries)
                    narrow(ph["out", 0], kview(A["w_out_a"][0]))
                else:
                    wb = kview(A["w_in_b"][0])
                    for d, c0 in ((ph["in_b"], 0), (ph["qm", 1], GD * QH * HD)):
                        def queries(i, d=d, c0=c0):
                            for j in range(2):
                                load(d.u0 + i * 2 + j, (d.u0 + j) % 2, wb[:, :, bass.ds(i * 256 + (c0 + j * P), P)], KD)
                        step_loop(sp, d.n, queries)
                    narrow(ph["out", 1], kview(A["w_out_b"][0]))
                ffn(l, 1)
                if l == 0:
                    wide(ph["kv"], A["w_kv_shared"])
            sp.wait_ge(s["y_out"], 32)

        @block.scalar
        def _(act):
            n = Place()

            def split(u, slot, nk=8, m=None):
                if m is None:
                    src = raw[:, slot, 0:nk * P]
                    act.wait_ge(w_in[slot], u * 8 + ((16 if slot == 0 else 8) - 8 * U0))
                else:
                    src = rawm[:, m, :]
                    act.wait_ge(m_in[m], u * 4 + (16 - 4 * m))
                act.wait_ge(s["w_mm"], u + 1)
                act.activation(whi[:, slot, 0:nk * P], src, ACT.Copy).then_inc(s["w_hi"], 1)

            def folded_h(g):
                for k in range(KD):
                    x_ready(k)
                    act.wait_ge(s["sq_used"], n.sq + max(k, 1) + 1)
                    act.activation(sqf[:, k % 2, :], xT[:, k, :], ACT.Square).then_inc(s["sq_ready"], 1)
                    act.activation(hH[:, k, :], xT[:, k, :], ACT.Copy, scale=g(k)).then_inc(s["hi_ready"], 1)
                n.sq += KD
                rms(D, rtf)

            def stats(src, ready, nk, dm):
                for k in range(nk):
                    ready(k)
                    act.wait_ge(s["sq_used"], n.sq + max(k, 1) + 1)
                    act.activation(sqb[:, k % 2, :], src(k), ACT.Square).then_inc(s["sq_ready"], 1)
                n.sq += nk
                rms(dm)

            def rms(dm, rt=rt):
                act.wait_ge(s["sq_used"], n.sq + 2)
                act.activation(rt[:, :].rearrange("p (h t) -> p h t", h=2), PS[:, 4:6, 0:HT], ACT.Sqrt,
                               bias=epsc, scale=1.0 / dm).then_inc(s["rt_ready"], 1)
                n.norm += 1

            def highs(tmp, hi, nk):
                for k in range(nk):
                    act.wait_ge(s["t_ready"], n.t + k + 1)
                    act.activation(hi(k), tmp(k), ACT.Copy).then_inc(s["hi_ready"], 1)
                n.t += nk

            def x_ready(k):
                act.wait_ge(s["x_done"], n.res + k + 1)

            act.nop().then_inc(s["w_mm"], 2)
            act.nop().then_inc(s["w_lo"], 2)
            act.nop().then_inc(s["sq_used"], 2)
            act.nop().then_inc(s["mid_lo"], 2)
            act.nop().then_inc(s["blk_evac"], 1)
            act.nop().then_inc(s["stage_free"], 1)
            for j in range(4):
                act.nop().then_inc(evac[j], 1)
            for name, k in CREDITS:
                act.nop().then_inc(s[name], k)
            act.wait_ge(s["mem_in"], 16)
            act.wait_ge(s["const_in"], 8 * 16)
            for t in range(2):
                if t:
                    act.wait_ge(s["mem_sq"], 1)
                act.activation(memsq[:, :], memnat[:, t, :], ACT.Square, accum_out=mst[:, t:t + 1]).then_inc(s["mem_sq"], 1)
            act.wait_ge(s["mem_sq"], 2)
            act.activation(mst[:, 2:4], mst[:, 0:2], ACT.Sqrt, bias=epsc, scale=1.0 / D).then_inc(s["mem_rt"], 1)
            split(0, 0, m=0)
            act.dma_start(xnat[:, 0:NCH, :], A["x_prompt"].rearrange("a (t p) d -> p (a t) d", p=P)).then_inc(s["x_in"], 16)
            act.dma_start(xnat[0:NS, NCH, :], A["x_sample"].rearrange("b t d -> (b t) d")).then_inc(s["x_in"], 16)
            act.dma_start(dtb[:, :], A["dt_bias"].rearrange("a (h o) -> (a h) o", o=1)).then_inc(s["x_in"], 16)
            act.dma_start(alog[:, :], A["a_log"].rearrange("a (h o) -> (a h) o", o=1)).then_inc(s["x_in"], 16)
            for r in range(2):
                src = A["d_skip"]
                src = bass.AP(src.tensor, src.offset + r, [[0, PD], [2, KI]])
                act.dma_start(DC[r * PD:(r + 1) * PD, :], src, allow_slow_non_contiguous=True).then_inc(s["x_in"], 16)
            for k in range(KD):
                act.wait_ge(s["mem_tr"], k + 1)
                act.activation(memT[:, k, :], PS[:, k % 2, 0:NM], ACT.Copy).then_inc(s["mem_ev"], 1)

            def wide(d, deep=False):
                def body(i, last=False):
                    for q in range(4):
                        split(d.u0 + i * 4 + q + 1, (d.u0 + q + 1) % 2, m=(q + 1) % 4 if deep and not (last and q == 3) else None)
                last = deep and d.u0 > 0
                step_loop(act, d.n - last, body)
                if last:
                    body(d.n - 1, True)

            for l in range(DEPTH):
                if l:
                    act.wait_ge(s["w_mm"], ph["mem", l].u0 + 2)
                highs(lambda k: yT[:, k, 0:NM], lambda k: hH[:, k, 0:NM], KD)
                wide(ph["mem", l], True)
            for k in range(KD):
                act.wait_ge(s["x_tr"], k + 1)
                b = 2 * (k % 3) + 2
                act.activation(xT[:, k, 0:SEQ], PS[:, b, :], ACT.Copy)
                act.activation(xT[:, k, SEQ:T], PS[:, b + 1, 0:NS], ACT.Copy).then_inc(s["x_done"], 1)

            def to_h():
                stats(x_of, x_ready, KD, D)
                highs(y_of, hH_of, KD)

            def narrow(d, early=0, last=False):
                e = list(n.ev)
                act.wait_ge(s["sq_used"], n.sq + 2)
                act.activation(rt[:, 0:1], epsc, ACT.Sqrt).then_inc(s["warmed"], 1)
                n.warm += 1
                act.wait_ge(s["warmed"], n.warm)

                def square(i, j):
                    act.wait_ge(evac[j], i + e[j] + 2)
                    act.wait_ge(s["sq_used"], 2 * i + n.sq + j + 1)
                    act.activation(sqb[:, j, :], yT[:, bass.ds(2 * i + j, 1), :].rearrange("p o t -> p (o t)"), ACT.Square).then_inc(s["sq_ready"], 1)

                def body(i, early=0, last=False):
                    for u in range(d.ub):
                        if u >= early and not (last and u == d.ub - 1):
                            split(d.u0 + i * d.ub + u + 1, (d.u0 + u + 1) % 2, (d.nks * 2 + (8,))[u + 1])
                        if u == len(d.nks):
                            square(i, 0)
                    square(i, 1)
                if early:
                    body(0, early)
                step_loop(act, d.n - last, body, early > 0)
                if last:
                    body(d.n - 1, last=True)
                for j in range(2):
                    n.ev[j] += d.n
                n.sq += KD
                n.res += KD
                rms(D)

            def attention(l):
                act.wait_ge(s["kt_tr"], l + 1)
                for k in range(2):
                    act.activation(KT[k][:, :, :], PS[:, 2 * k:2 * k + 2, :].rearrange("p a (j m) -> p (a j) m", j=2), ACT.Copy).then_inc(s["kt_ev"], 1)
                for h in range(MH):
                    act.wait_ge(s["mx_ready"], MH * l + h + 1)
                    if h:
                        act.wait_ge(s["ptr_ready"], MH * l + h)
                    for r in range(NCH):
                        ins = act.activation(Pb[:, r, :], PS[:, 4 + 2 * (h % 2) + r // 2, (r % 2) * NM:(r % 2 + 1) * NM], ACT.Exp, bias=am[:, h % 2, r:r + 1], accum_out=ar[:, h % 2, r:r + 1])
                    ins.then_inc(s["p_exp"], 1)
                    act.wait_ge(s["ptr_ready"], MH * l + h + 1)
                    if h:
                        act.wait_ge(s["pv_ready"], MH * l + h)
                    act.activation(PT[:, :, :], PS[:, 0:2, :], ACT.Copy).then_inc(s["pt_evac"], 1)
                for st in range(16):
                    act.wait_ge(s["ks_tr"], 16 * l + st + 1)
                    if st >= 4:
                        act.wait_ge(s["ss_ready"], 16 * l + st - 3)
                    b = (0, 2, 6)[st % 3]
                    act.activation(KT[st % 4][:, :, :], PS[:, b:b + 2, :].rearrange("p a (j m) -> p (a j) m", j=2), ACT.Copy).then_inc(s["ks_ev"], 1)
                act.wait_ge(s["smx"], l + 1)
                act.activation(Pb[:, 0, :], PS[:, 4, 0:NM], ACT.Exp, bias=am[:, 0, 0:1], accum_out=ar[:, 0, 0:1]).then_inc(s["s_exp"], 1)
                act.wait_ge(s["vb_done"], NB * l + NB)
                act.activation(Ob[:, :].rearrange("p (a n) -> p a n", a=2), PS[:, 6:8, :], ACT.Copy).then_inc(s["so_ev"], 1)
                act.wait_ge(s["att_done"], l + 1)

            def ffn(l, f):
                folded_h(gain(l, 4 * f))
                d = ph["gu", l, f]
                e0 = list(n.ev)

                def gu(i):
                    for b in range(2):
                        u = d.u0 + i * 4 + 2 * b
                        split(u + 1, (d.u0 + 1) % 2)
                        act.wait_ge(evac[2 * b], i + e0[2 * b] + 2)
                        act.activation(sg[:, b, :], sg[:, b, :], ACT.Silu).then_inc(s["silu_done"], 1)
                        split(u + 2, d.u0 % 2)
                        act.wait_ge(evac[2 * b + 1], i + e0[2 * b + 1] + 2)
                        act.activation(H24[:, bass.ds(2 * i + b, 1), :], prod[:, b:b + 1, :], ACT.Copy).then_inc(s["mid_hi"], 1)
                step_loop(act, d.n, gu)
                for j in range(4):
                    n.ev[j] += d.n
                n.mid += 2 * d.n
                dn = ph["down", l, f]
                narrow(dn, last=(l, f) == (DEPTH - 1, 1))

            for l in range(DEPTH):
                ffn(l, 0)
                if l == 0:
                    to_h()
                    u0 = ph["dt"].u0
                    split(u0 + 1, (u0 + 1) % 2)
                    act.wait_ge(s["w_mm"], u0 + 3)
                    act.activation(dts[:, 0, :].rearrange("p (h t) -> p h t", h=2), PS[0:NH, 0:2, 0:HT], ACT.Identity, bias=dtb[:, :]).then_inc(evac[0], 1)
                    n.ev[0] += 1
                    act.wait_ge(evac[0], n.ev[0] + 1)
                    act.activation(dts[:, 1, :], dts[:, 0, :], ACT.Abs).then_inc(s["dt_e"], 1)
                    act.wait_ge(s["dt_e"], 1)
                    act.activation(dts[:, 2, :], dts[:, 1, :], ACT.Exp, scale=-1.0).then_inc(s["dt_e"], 1)
                    act.activation(nA[:, :], alog[:, :], ACT.Exp).then_inc(s["na_ready"], 1)
                    act.wait_ge(s["dt_u"], 1)
                    act.activation(dts[:, 4, :], dts[:, 3, :], ACT.Ln).then_inc(s["dt_ln"], 1)
                    act.wait_ge(s["alb_sub"], 1)
                    act.activation(DE[:, :, :], DE[:, :, :], ACT.Exp)
                    act.activation(CD[:, :, :], CD[:, :, :], ACT.Exp)
                    act.activation(EAS[:, :], aT[0:NS, NCH, :], ACT.Exp).then_inc(s["de_done"], 1)
                    act.wait_ge(s["pz"], 2)
                    act.wait_ge(s["de_done"], 1)
                    d = ph["ssd"]
                    split(d.u0 + 1, (d.u0 + 1) % 2)
                    e0 = list(n.ev)

                    def group(g):
                        def conv_in(ti):
                            act.wait_ge(s["w_mm"], d.u0 + g * 6 + ti + 3)
                            act.wait_ge(s["taps"], g * 4 + ti + 3 - 2)
                            act.wait_ge(s["cvn_done"], g * 4 + ti + 3 - 2)
                            b, bank = ti % 2, 2 * POS[ti]
                            act.activation(pre[:, b, CW - 1:CW - 1 + HT], PS[:, bank, 0:HT], ACT.Copy)
                            act.activation(pre[:, b, CW - 1 + HT:], PS[:, bank + 1, 0:HP], ACT.Copy)
                            act.activation(pres[:, b, :, CW - 1:], PS[:, bank + 1, HP:HT].rearrange("p (b t) -> p b t", b=NB), ACT.Copy).then_inc(evac[POS[ti]], 1)
                            rep = 2 if POS[ti] < 2 else 1
                            act.wait_ge(evac[POS[ti]], g * rep + e0[POS[ti]] + 2)
                            act.wait_ge(s["hist_g"], g * 4 + ti + 1)
                            act.activation(xbc[:, ti, 0:SEQ], pre[:, b, 0:SEQ], ACT.Identity, bias=cwg[:, ti, 4:5], scale=cwg[:, ti, 0:1])
                            act.activation(xbc[:, ti, SEQ:T].rearrange("p (b t) -> p b t", b=NB), pres[:, b, :, 0:NT], ACT.Identity, bias=cwg[:, ti, 4:5], scale=cwg[:, ti, 0:1]).then_inc(s["tap0"], 1)

                        def conv_silu(ti):
                            act.wait_ge(s["taps"], g * 4 + ti + 1 + 2)
                            act.activation(xbc[:, ti, :], xbc[:, ti, :], ACT.Silu).then_inc(s["conv_done"], 1)

                        for j in range(6):
                            split(d.u0 + g * 6 + j + 2, (d.u0 + j) % 2)
                            if j == 2:
                                act.wait_ge(s["group_end"], g + 1)
                            if j < 4:
                                conv_in(j)
                                if j:
                                    conv_silu(j - 1)
                            else:
                                act.wait_ge(s["w_mm"], d.u0 + g * 6 + j + 3)
                                act.activation(sz[:, j - 4, :].rearrange("p (h t) -> p h t", h=2), PS[:, 2 * (j - 4):2 * (j - 4) + 2, 0:HT], ACT.Silu).then_inc(evac[j - 4], 1)
                                if j == 4:
                                    conv_silu(3)
                        act.wait_ge(s["tok_ready"], g + 1)
                        act.activation(btok[:, 0:NCH, :], PS[:, 4, :].rearrange("p (c n) -> p c n", c=NCH), ACT.Copy).then_inc(s["btok_ready"], 1)
                        act.wait_ge(s["cvt_ready"], g + 1)
                        act.wait_ge(s["rest_out"], g + 1)
                        act.activation(cvo[:, :, :], PS[0:27, 1, :].rearrange("p (c n) -> p c n", c=4), ACT.Copy).then_inc(s["cvo_done"], 1)
                        act.wait_ge(s["small_read"], g + 1)
                        act.activation(cds[:, :], cds[:, :], ACT.Exp).then_inc(s["cds_exp"], 1)

                        def decay(h):
                            act.wait_ge(s["bc_ready"], g * 4 + h + 1)
                            if h >= 2:
                                act.wait_ge(s["seg_ready"], g * 4 + h - 1)
                            act.activation(bcS[:, h % 2, :], PS[:, h % 2, :], ACT.Copy)
                            if h >= 2:
                                act.wait_ge(s["y_used"], g * 4 + h - 1)
                            act.activation(Eh[:, h % 2, :], PS[:, h % 2, :], ACT.Exp).then_inc(s["bc_read"], 1)

                        def pair_decay(h):
                            act.wait_ge(s["seg_ready"], g * 4 + h + 1)
                            act.activation(Lh[0:NS, h % 2, SEQ:T], Lh[0:NS, h % 2, SEQ:T], ACT.Exp)
                            act.activation(Lh[:, h % 2, 0:SEQ], Lh[:, h % 2, 0:SEQ], ACT.Exp).then_inc(s["lexp"], 1)

                        def state_rows(q):
                            act.wait_ge(s["s0t_ready"], g * 2 + q + 1)
                            act.activation(S0T[:, :, q * P:(q + 1) * P], PS[:, 6:8, :].rearrange("p a (b n) -> p (a b) n", b=4), ACT.Copy).then_inc(s["s0t_evac"], 1)

                        decay(0)
                        pair_decay(0)
                        decay(1)
                        state_rows(0)
                        pair_decay(1)
                        decay(2)
                        pair_decay(2)
                        state_rows(1)
                        decay(3)
                        pair_decay(3)
                        act.wait_ge(s["final_ready"], g + 1)
                        act.activation(sso[:, :, :], PS[:, 4, 0:256].rearrange("p (q n) -> p q n", q=2), ACT.Copy).then_inc(s["final_read"], 1)
                        act.wait_ge(s["final_read"], g + 1)
                    step_loop(act, NG, group)
                    n.ev = [n.ev[0] + 2 * NG, n.ev[1] + 2 * NG, n.ev[2] + NG, n.ev[3] + NG]

                    def queries(d, dst=None, first=0, scale=MD ** -0.5, early=0, pos=(0, 1)):
                        e = list(n.ev)

                        def body(i, early=0):
                            for j in range(early, 2):
                                split(d.u0 + i * 2 + j + 1, (d.u0 + j + 1) % 2)
                            for j in range(2 if dst else 0):
                                act.wait_ge(s["w_mm"], d.u0 + i * 2 + j + 3)
                                act.activation(dst[:, bass.ds(2 * i + (j + first), 1), :].rearrange("p o (h t) -> p (o h) t", h=2), PS[:, 2 * pos[j]:2 * pos[j] + 2, 0:HT], ACT.Copy, scale=scale).then_inc(evac[pos[j]], 1)
                        if early:
                            body(0, early)
                        step_loop(act, d.n, body, early)
                        for j in pos:
                            n.ev[j] += d.n

                    act.wait_ge(s["group_end"], NG + 1)
                    act.wait_ge(s["rest_out"], NG + 1)
                    queries(ph["qm", 0], yT, early=1, pos=QPOS)
                    stats(lambda k: M1[:, k, :], lambda k: None, KI, DI)
                    attention(0)
                    d = ph["out", 0]
                    for k in range(24):
                        if k < KI:
                            act.wait_ge(s["t_ready"], n.t + k + 1)
                        act.activation(H24[:, k, :], M1[:, k, :], ACT.Copy).then_inc(s["hi_ready"], 1)
                        if k in (8, 20):
                            u = d.u0 + 1 + k // 20
                            split(u, u % 2, 8)
                    n.t += KI
                    narrow(d, 2)
                else:
                    folded_h(gain(1, 2))
                    queries(ph["in_b"])
                    queries(ph["qm", 1])
                    attention(1)
                    act.wait_ge(s["dkt_tr"], 1)
                    for k in range(3):
                        act.activation(KTd[:, 2 * k:2 * k + 2, :], PS[:, 2 * k:2 * k + 2, :], ACT.Copy)
                    act.activation(KTn[:, :, :].rearrange("p j n -> p (j n)"), PS[:, 6, 0:2 * GD * NS], ACT.Copy).then_inc(s["dkt_ev"], 1)

                    def expo(t):
                        n_ = sum(n for _, _, n in spans(t % NCH)) if t < 16 else NEW0 + GD * NS
                        act.wait_ge(s["dmx"], t + 1)
                        b = t % 2
                        act.activation(SS[:, b, 0:n_], SS[:, b, 0:n_], ACT.Exp, bias=dm[:, b:b + 1], accum_out=dr[:, b:b + 1]).then_inc(s["dexp"], 1)

                    def head_out(t):
                        act.wait_ge(s["do_ready"], t + 1)
                        act.activation(M1[:, t // NCH, (t % NCH) * P:(t % NCH + 1) * P], PS[:, 6 + t % 2, 0:P], ACT.Copy).then_inc(s["do_ev"], 1)

                    expo(0)
                    for t in range(16):
                        if t + 1 < 16:
                            expo(t + 1)
                        act.wait_ge(s["dptr"], t + 1)
                        if t >= 2:
                            act.wait_ge(s["do_ready"], t - 1)
                        n_ = sum(n for _, _, n in spans(t % NCH))
                        act.activation(PTd[:, t % 2, 0:n_], PS[:, 3:6, :].rearrange("p a n -> p (a n)")[:, 0:n_], ACT.Copy).then_inc(s["dpt_ev"], 1)
                        if t:
                            head_out(t - 1)
                    head_out(15)
                    for st in range(16):
                        act.wait_ge(s["dks_tr"], st + 1)
                        if st >= 4:
                            act.wait_ge(s["dss_ready"], st - 3)
                        act.activation(KTb[:, st % 4, :], PS[:, st % 3, 0:NEW0], ACT.Copy).then_inc(s["dks_ev"], 1)
                    expo(16)
                    act.wait_ge(s["do_ready"], 17)
                    act.activation(Od[:, :], PS[:, 2, 0:256], ACT.Copy).then_inc(s["do_ev"], 1)
                    act.wait_ge(s["dil_done"], 1)
                    d = ph["out", 1]
                    for k in range(12):
                        act.activation(H24[:, k, :], M1[:, k, :], ACT.Copy).then_inc(s["hi_ready"], 1)
                        if k == 6:
                            split(d.u0 + 1, (d.u0 + 1) % 2, 6)
                    narrow(d, 1)
                ffn(l, 1)
                if l == 0:
                    to_h()
                    wide(ph["kv"])
            stats(x_of, x_ready, KD, D)

            for t in range(NCH + 1):
                rows_ = P if t < NCH else NS
                for h in range(2):
                    act.wait_ge(s["f_tr"], 2 * t + h + 1)
                    act.activation(xnat[0:rows_, t, h * 512:(h + 1) * 512], PS[0:rows_, (2 * t + h) % 4, :], ACT.Copy).then_inc(s["f_ev"], 1)
            act.wait_ge(s["f_ev"], 2 * NCH + 2)
            act.dma_start(O["y_prompt"].rearrange("a (t p) d -> p (a t) d", p=P), xnat[:, 0:NCH, :]).then_inc(s["y_out"], 16)
            act.dma_start(O["y_sample"].rearrange("b t d -> (b t) d"), xnat[0:NS, NCH, :]).then_inc(s["y_out"], 16)
            act.wait_ge(s["y_out"], 32)

        @block.tensor
        def _(pe):
            n = Place()

            def products(slot, nk, k0, hi, lo, bank, first, final, ready=None):
                for k in range(nk):
                    if ready:
                        pe.wait_ge(*ready(k0 + k))
                    for w, x in ((whi, hi), (whi, lo), (wlo, hi)):
                        for h in range(2):
                            mm = pe.matmul(PS[:, bank + h, 0:HT], w[:, slot, k * P:(k + 1) * P],
                                           x(k0 + k)[:, h * HT:(h + 1) * HT],
                                           start=first and k == 0 and w is whi and x is hi,
                                           stop=final and k == nk - 1 and w is wlo)
                return mm

            def dense(d, hi, lo, pos=lambda j: j, ready=None, summed=False):
                e = list(n.ev)

                def body(i):
                    seen = [0] * 4
                    for j in range(d.tiles):
                        b = pos(j)
                        reps = sum(pos(jj) == b for jj in range(d.tiles))
                        pe.wait_ge(evac[b], i * reps + e[b] + seen[b] + 1)
                        seen[b] += 1
                        for q, nk in enumerate(d.nks):
                            u = j * len(d.nks) + q
                            pe.wait_ge(s["w_lo"], i * d.ub + d.u0 + u + 3)
                            products((d.u0 + u) % 2, nk, d.k0[q], hi, lo, 2 * b, q == 0, q == len(d.nks) - 1,
                                     None if j else ready).then_inc(s["w_mm"], 1)
                step_loop(pe, d.n, body)
                if summed:
                    pe.wait_ge(evac[2], n.ev[2] + 1)
                    pe.wait_ge(s["sq_used"], n.sq + KD + 1)
                    sums(acc[:, :], True, False)
                    pe.wait_ge(s["sq_ready"], n.sq + KD)
                    sums(sqb[:, 1, :], False, True).then_inc(s["sq_used"], 1)
                    n.sq += KD
                for j in range(d.tiles):
                    n.ev[pos(j)] += d.n

            def sums(sq, start, stop):
                for h in range(2):
                    mm = pe.matmul(PS[:, 4 + h, 0:HT], ones, sq[:, h * HT:(h + 1) * HT], start=start, stop=stop)
                return mm

            def wide(d, windows):
                def body(i):
                    pe.wait_ge(s["blk_evac"], n.blk + i * len(windows) + 1)
                    for q in range(4):
                        pe.wait_ge(s["w_lo"], d.u0 + i * 4 + q + 3)
                        for kk in range(2):
                            pe.wait_ge(s["lo_ready"], n.t - KD + 2 * q + kk + 1)
                            for b, t0 in enumerate(windows):
                                for x, w in ((hH, whi), (hL, whi), (hH, wlo)):
                                    mm = pe.matmul(PS[:, b, :], x[:, 2 * q + kk, t0:t0 + P], w[:, (d.u0 + q) % 2, kk * 512:(kk + 1) * 512],
                                                   start=q == 0 and kk == 0 and x is hH and w is whi,
                                                   stop=q == 3 and kk == 1 and w is wlo)
                        mm.then_inc(s["w_mm"], 1)
                step_loop(pe, d.n, body)
                n.blk += d.n * len(windows)

            def stats(nk, sqb=sqb):
                for k in range(nk):
                    pe.wait_ge(s["sq_ready"], n.sq + k + 1)
                    sums(sqb[:, k % 2, :], k == 0, k == nk - 1).then_inc(s["sq_used"], 1)
                n.sq += nk

            pe.wait_ge(s["const_in"], 8 * 16)
            for j, m in ((0, P), (1, P), (2, 48)):
                tr = pe.transpose(PS[:, 0, j * P:j * P + m], rows[0:m, j, :], ident[0:m, 0:m])
            tr.then_inc(s["row_in"], 1)
            pe.wait_ge(s["cols_out"], 1)
            for k in range(KD):
                pe.wait_ge(s["mem_sc"], 2)
                if k >= 2:
                    pe.wait_ge(s["mem_ev"], k - 1)
                for t in range(2):
                    tr = pe.transpose(PS[:, k % 2, t * P:(t + 1) * P], memnat[:, t, k * P:(k + 1) * P], ident)
                tr.then_inc(s["mem_tr"], 1)
            for l in range(DEPTH):
                n.t += KD
                wide(ph["mem", l], (0, P))
            pe.wait_ge(s["x_in"], 6 * 16)
            for k in range(KD):
                if k >= 3:
                    pe.wait_ge(s["x_done"], k - 2)
                b = 2 * (k % 3) + 2
                for t in range(NCH):
                    pe.transpose(PS[:, b, t * P:(t + 1) * P], xnat[:, t, k * P:(k + 1) * P], ident)
                pe.transpose(PS[:, b + 1, 0:NS], xnat[0:NS, NCH, k * P:(k + 1) * P], ident[0:NS, 0:NS]).then_inc(s["x_tr"], 1)

            def to_h():
                stats(KD)
                n.t += KD

            def folded_stats():
                stats(KD, sqf)
                n.t += KD
                n.unscaled += KD

            def h_ready(k, nk=KD):
                return s["lo_ready"], n.t - nk + k + 1

            kv_in = [s["kv_in0"], s["kv_in1"], s["kv_in2"]]

            def attention(l):
                q = yT
                land = lambda idx: pe.wait_ge(kv_in[idx % 3], 16 * (6 * l + idx // 3 + 1))
                pe.wait_ge(s["att_go"], l + 1)
                land(0)
                for hk in range(8):
                    for t in range(2):
                        tr = pe.transpose(PS[:, hk // 2, (hk % 2) * 256 + t * P:(hk % 2) * 256 + (t + 1) * P], kvr[:, 0, t, hk * P:(hk + 1) * P], ident)
                tr.then_inc(s["kt_tr"], 1)

                def scores(h):
                    for r in range(NCH):
                        for k in range(2):
                            mm = pe.matmul(PS[:, 4 + 2 * (h % 2) + r // 2, (r % 2) * NM:(r % 2 + 1) * NM], q[:, 2 * h + k, r * P:(r + 1) * P], KT[(2 * h + k) // 4][:, (2 * h + k) % 4, :], start=k == 0, stop=k == 1)
                    mm.then_inc(s["sc_ready"], 1)

                pe.wait_ge(s["kt_ev"], 2 * l + 2)
                scores(0)
                scores(1)
                land(1)
                for h in range(MH):
                    pe.wait_ge(s["p_ready"], MH * l + h + 1)
                    if h:
                        pe.wait_ge(s["pt_evac"], MH * l + h)
                    for t in range(2):
                        for r in range(NCH):
                            tr = pe.transpose(PS[:, t, r * P:(r + 1) * P], Pb[:, r, t * P:(t + 1) * P], ident)
                    tr.then_inc(s["ptr_ready"], 1)
                    if h + 2 < MH:
                        scores(h + 2)
                    pe.wait_ge(s["pt_evac"], MH * l + h + 1)
                    if h:
                        pe.wait_ge(s["pv_evac"], MH * l + h)
                    for k in range(2):
                        for t in range(2):
                            mm = pe.matmul(PS[:, 2 + k, :], kvr[:, 1, t, (2 * h + k) * P:(2 * h + k + 1) * P], PT[:, t, :], start=t == 0, stop=t == 1)
                    mm.then_inc(s["pv_ready"], 1)
                pe.wait_ge(s["q_ready"], 8 * l + 8)
                pe.wait_ge(s["pt_evac"], MH * l + MH)
                pe.wait_ge(s["pv_evac"], MH * l + MH)
                pairs = (0, 2, 6)

                def rows_of(st):
                    b, half = st // 2, st % 2
                    idx = 2 + b
                    if half == 0:
                        land(idx)
                    if st >= 3:
                        pe.wait_ge(s["ks_ev"], 16 * l + st - 2)
                    for j in range(4):
                        for t in range(2):
                            tr = pe.transpose(PS[:, pairs[st % 3] + j // 2, (j % 2) * 256 + t * P:(j % 2) * 256 + (t + 1) * P], kvr[:, idx % 3, t, (4 * half + j) * P:(4 * half + j + 1) * P], ident)
                    tr.then_inc(s["ks_tr"], 1)

                rows_of(0)
                rows_of(1)
                for st in range(16):
                    if st + 2 < 16:
                        rows_of(st + 2)
                    pe.wait_ge(s["ks_ev"], 16 * l + st + 1)
                    for j in range(4):
                        mm = pe.matmul(PS[:, 4, 0:NM], QZ[:, 4 * (st % 2) + j, st // 2, :], KT[st % 4][:, j, :], start=st == 0 and j == 0, stop=st == 15 and j == 3)
                    mm.then_inc(s["ss_ready"], 1)
                pe.wait_ge(s["s_p"], l + 1)
                for t in range(2):
                    tr = pe.transpose(PS[:, 5, t * P:(t + 1) * P], Pb[:, 0, t * P:(t + 1) * P], ident)
                tr.then_inc(s["s_tr"], 1)
                pe.wait_ge(s["pz_ready"], l + 1)
                pe.wait_ge(s["ks_ev"], 16 * l + 16)
                for b in range(NB):
                    land(10 + b)
                    for t in range(2):
                        for k in range(2):
                            mm = pe.matmul(PS[:, 6 + k, :], PZ[:, t, b, :], kvr[:, (10 + b) % 3, t, k * 512:(k + 1) * 512], start=b == 0 and t == 0, stop=b == NB - 1 and t == 1)
                    mm.then_inc(s["vb_done"], 1)
                pe.wait_ge(s["so_ev"], l + 1)
                for hk in range(8):
                    tr = pe.transpose(PS[:, hk // 4, (hk % 4) * P:(hk % 4 + 1) * P], Ob[:, hk * P:(hk + 1) * P], ident)
                tr.then_inc(s["so_tr"], 1)
                pe.wait_ge(s["att_done"], l + 1)

            def ffn(l, f):
                folded_stats()
                dense(ph["gu", l, f], hH_of, hL_of, ready=h_ready)
                dense(ph["down", l, f], lambda k: H24[:, k, :], lambda k: L24[:, k, :], ready=lambda k: (s["mid_lo"], n.mid + k + 3), summed=True)
                n.mid += KF

            for l in range(DEPTH):
                ffn(l, 0)
                if l == 0:
                    to_h()
                    dense(ph["dt"], hH_of, hL_of, ready=h_ready)
                    pe.wait_ge(s["conv_in"], 32)
                    for c in range(32):
                        tr = pe.transpose(PS[:, 2 + c // 16, (c % 16) * 24:(c % 16 + 1) * 24], cvin[:, c * P:(c + 1) * P], ident[0:24, 0:24])
                    tr.then_inc(s["hist_tr"], 1)
                    pe.wait_ge(s["scan_done"], 1)
                    for c in range(NCH + 1):
                        m = P if c < NCH else NS
                        last = acum[:, c * P + P - 1:c * P + P].to_broadcast([NH, P]) if c < NCH else None
                        pe.transpose(PS[0:m, 0, c * NH:(c + 1) * NH], acum[:, c * P:c * P + m], ident[0:NH, 0:NH])
                        pe.transpose(PS[0:m, 0, 160 + c * NH:160 + (c + 1) * NH], dtx[:, c * P:c * P + m], ident[0:NH, 0:NH])
                        if c < NCH:
                            pe.matmul(PS[:, 0, 320 + c * NH:320 + (c + 1) * NH], last, ident[0:NH, 0:NH], start=True, stop=True)
                        else:
                            pe.matmul(PS[0:NS, 0, 320 + c * NH:320 + (c + 1) * NH], tmpL[:, :], ident[0:NH, 0:NH], start=True, stop=True).then_inc(s["dtt_tr"], 1)
                    pe.wait_ge(s["hist_copied"], 1)
                    d = ph["ssd"]
                    e0 = list(n.ev)

                    def group(g):
                        def spread(h):
                            if h == 0:
                                pe.wait_ge(s["cbm_ready"], g + 1)
                            elif h == 1:
                                pe.wait_ge(s["cvo_done"], g + 1)
                            else:
                                pe.wait_ge(s["bc_read"], g * 4 + h - 1)
                            pe.matmul(PS[:, h % 2, :], selg[:, h:h + 1].to_broadcast([NH, P]), acum[:, 0:SEQ], start=True, stop=True).then_inc(s["bc_ready"], 1)

                        def state_rows(q):
                            if q == 0:
                                pe.wait_ge(s["s0_in"], g * 32 + 32)
                                pe.wait_ge(s["xd_ready"], g + 1)
                            else:
                                pe.wait_ge(s["s0t_evac"], g * 2 + 1)
                            for b in range(NB):
                                tr = pe.transpose(PS[:, 6 + b // 4, (b % 4) * P:(b % 4 + 1) * P], S0[:, q, b, :], ident)
                            tr.then_inc(s["s0t_ready"], 1)

                        for j in range(6):
                            if j == 1:
                                pe.wait_ge(s["news_read"], 2 * g + 1)
                            elif j == 2:
                                pe.wait_ge(s["y_read"], g + 1)
                            rep = 2 if POS[j] < 2 else 1
                            pe.wait_ge(evac[POS[j]], g * rep + e0[POS[j]] + 1 + (j >= 4))
                            pe.wait_ge(s["w_lo"], g * 6 + d.u0 + j + 3)
                            products((d.u0 + j) % 2, KD, 0, hH_of, hL_of, 2 * POS[j], True, True).then_inc(s["w_mm"], 1)
                        pe.wait_ge(s["conv_done"], g * 4 + 4)
                        pe.wait_ge(s["col_g"], g + 1)
                        for c in range(NCH):
                            pe.transpose(PS[:, 4, c * P:(c + 1) * P], xbc[:, 0, c * P:(c + 1) * P], ident)
                            for q in range(2):
                                pe.transpose(PS[:, 6 + c // 2, (c % 2) * 256 + q * P:(c % 2) * 256 + (q + 1) * P], xbc[:, 2 + q, c * P:(c + 1) * P], ident)
                        for q, t in enumerate((0, 2, 3)):
                            pe.transpose(PS[0:NS, 5, q * P:(q + 1) * P], xbc[:, t, SEQ:T], ident)
                        pe.matmul(PS[0:NS, 5, 384:384 + NS], xbc[:, 0, SEQ:T], xbc[:, 1, SEQ:T], start=True, stop=True)
                        for q in range(2):
                            mm = pe.matmul(PS[:, 5, 416 + q * NB:416 + (q + 1) * NB], selp[:, 2 * q:2 * q + 2, :].rearrange("p a b -> p (a b)"), acum[:, SEQ + NT - 1:T:NT], start=True, stop=True)
                        mm.then_inc(s["tok_ready"], 1)
                        pe.wait_ge(evac[0], 2 * g + e0[0] + 3)
                        for c in range(NCH):
                            mm = pe.matmul(PS[:, 0, c * P:(c + 1) * P], xbc[:, 0, c * P:(c + 1) * P], xbc[:, 1, c * P:(c + 1) * P], start=True, stop=True)
                        mm.then_inc(s["cb_ready"], 1)
                        pe.wait_ge(s["cvn_done"], g * 4 + 4 + 2)
                        for q in range(4):
                            tr = pe.transpose(PS[0:27, 1, q * P:(q + 1) * P], cvn[:, q, 0:27], ident)
                        tr.then_inc(s["cvt_ready"], 1)
                        pe.wait_ge(s["small_read"], g + 1)
                        for h in range(4):
                            mm = pe.matmul(PS[:, 5, h * NS:(h + 1) * NS], selg[:, h:h + 1].to_broadcast([NH, P]), acum[:, SEQ:T], start=True, stop=True)
                        mm.then_inc(s["bcs_ready"], 1)
                        pe.wait_ge(evac[1], 2 * g + e0[1] + 3)
                        pe.wait_ge(s["xdd_ready"], g + 1)
                        pe.wait_ge(s["btok_ready"], g + 1)
                        for c in range(NCH):
                            mm = pe.matmul(PS[:, 2 + c // 2, (c % 2) * 256:(c % 2 + 1) * 256], btok[:, c, :], xdd[:, c, :], start=True, stop=True)
                        mm.then_inc(s["st_ready"], 1)
                        spread(0)
                        spread(1)
                        state_rows(0)
                        def head(h):
                            pe.wait_ge(s["m_ready"], g * 4 + h + 1)
                            pe.wait_ge(s["c_ready"], g * 4 + h + 1)
                            if h == 0:
                                pe.wait_ge(s["st_done"], g + 1)
                                pe.wait_ge(s["bcs_read"], g + 1)
                            r, w = (h % 2) * PD, slice(h * PD, (h + 1) * PD)
                            for c in range(NCH):
                                pe.matmul(PS[r:r + PD, 2 + h // 2, c * P:(c + 1) * P], xd[:, c, w], Lh[:, h % 2, c * P:(c + 1) * P], start=True, stop=c == 0)
                                if c:
                                    pe.matmul(PS[r:r + PD, 2 + h // 2, c * P:(c + 1) * P], ST[:, c - 1, w], Eh[:, h % 2, c * P:(c + 1) * P], start=False, stop=True)
                            pe.matmul(PS[r:r + PD, 5, 128 + (h // 2) * NS:128 + (h // 2 + 1) * NS], xd[0:NS, NCH, w], Lh[0:NS, h % 2, SEQ:T], start=True, stop=True).then_inc(s["y_used"], 1)

                        def new_states(q):
                            if q == 0:
                                pe.wait_ge(s["s0t_evac"], g * 2 + 2)
                                pe.wait_ge(s["bz_ready"], g + 1)
                            else:
                                pe.wait_ge(s["news_read"], g * 2 + 2)
                            for k in range(2):
                                mm = pe.matmul(PS[:, 6 + k, :], xdd[0:NS, NCH, q * P:(q + 1) * P], BZ[:, 4 * k:4 * k + 4, :].rearrange("p b n -> p (b n)"), start=True, stop=True)
                            mm.then_inc(s["news_ready"], 1)

                        spread(2)
                        head(0)
                        spread(3)
                        head(1)
                        state_rows(1)
                        pe.wait_ge(s["s0t_evac"], g * 2 + 2)
                        pe.wait_ge(s["cz_ready"], g + 1)
                        for b in range(NB):
                            mm = pe.matmul(PS[0:NS, 4, 0:256], CZ[:, b, :], S0T[:, b, :], start=b == 0, stop=b == NB - 1)
                        mm.then_inc(s["yoff_ready"], 1)
                        new_states(0)
                        head(2)
                        new_states(1)
                        head(3)
                        pe.wait_ge(s["yos_ready"], g + 1)
                        for q in range(2):
                            tr = pe.transpose(PS[:, 4, q * P:(q + 1) * P], ST[:, NCH - 1, q * P:(q + 1) * P], ident)
                        tr.then_inc(s["final_ready"], 1)
                        for q in range(2):
                            tr = pe.transpose(PS[:, 5, 192 + q * NS:192 + (q + 1) * NS], yos[:, q * P:(q + 1) * P], ident[0:NS, 0:NS])
                        tr.then_inc(s["y_ready"], 1)
                    step_loop(pe, NG, group)
                    n.ev = [n.ev[0] + 2 * NG, n.ev[1] + 2 * NG, n.ev[2] + NG, n.ev[3] + NG]
                    pe.wait_ge(s["news_read"], 2 * NG + 1)
                    dense(ph["qm", 0], hH_of, hL_of, pos=lambda j: QPOS[j])
                    stats(KI)
                    attention(0)
                    n.t += 24
                    n.unscaled += 8
                    dense(ph["out", 0], lambda k: H24[:, k, :], lambda k: L24[:, k, :], ready=lambda k: h_ready(k, 24), summed=True)
                else:
                    folded_stats()
                    dense(ph["in_b"], hH_of, hL_of, ready=h_ready)
                    dense(ph["qm", 1], hH_of, hL_of)
                    attention(1)
                    pe.wait_ge(s["dil_in"], 48)
                    for j in range(2 * GD):
                        for t in range(NCH):
                            pe.transpose(PS[:, j, t * P:(t + 1) * P], kvd[:, t, (j // 2) * 512 + (j % 2) * P:(j // 2) * 512 + (j % 2 + 1) * P], ident)
                    for j in range(2 * GD):
                        tr = pe.transpose(PS[:, 6, j * NS:(j + 1) * NS], kvn[:, (j // 2) * 512 + (j % 2) * P:(j // 2) * 512 + (j % 2 + 1) * P], ident[0:NS, 0:NS])
                    tr.then_inc(s["dkt_tr"], 1)

                    def scores(t):
                        h, i = t // NCH, t % NCH
                        if t:
                            pe.wait_ge(s["ds_ev"], t)
                        for g, first, n_ in spans(i):
                            mm = pe.matmul(PS[:, g, 0:n_], M1[:, 12 + g * QH + h, i * P:(i + 1) * P], KTd[:, 2 * g + h // 2, first * P:(i + 1) * P], start=True, stop=True)
                        mm.then_inc(s["ds_ready"], 1)

                    def values(t):
                        h, i = t // NCH, t % NCH
                        if t >= 2:
                            pe.wait_ge(s["do_ev"], t - 1)
                        tiles = [(g, kt) for g, first, _ in spans(i) for kt in range(first, i + 1)]
                        for x, (g, kt) in enumerate(tiles):
                            c = g * 512 + 256 + (h // 2) * P
                            mm = pe.matmul(PS[:, 6 + t % 2, 0:P], kvd[:, kt, c:c + P], PTd[:, t % 2, x * P:(x + 1) * P], start=x == 0, stop=x == len(tiles) - 1)
                        mm.then_inc(s["do_ready"], 1)

                    pe.wait_ge(s["dkt_ev"], 1)
                    scores(0)
                    scores(1)
                    for t in range(16):
                        if t + 2 < 16:
                            scores(t + 2)
                        pe.wait_ge(s["dp_ready"], t + 1)
                        if t:
                            pe.wait_ge(s["dpt_ev"], t)
                        for x in range(sum(n for _, _, n in spans(t % NCH)) // P):
                            tr = pe.transpose(PS[:, 3 + x // 4, (x % 4) * P:(x % 4 + 1) * P], SS[:, t % 2, x * P:(x + 1) * P], ident)
                        tr.then_inc(s["dptr"], 1)
                        if t:
                            values(t - 1)
                    pe.wait_ge(s["dpt_ev"], 16)
                    values(15)
                    pe.wait_ge(s["dks_in"], 7 * 16)
                    pe.wait_ge(s["ds_ev"], 16)

                    def rows_of(st):
                        b, kv = st // 2, st % 2
                        if st >= 3:
                            pe.wait_ge(s["dks_ev"], st - 2)
                        for sl in range(4):
                            m = P if sl < 3 else 64
                            tr = pe.transpose(PS[:, st % 3, sl * P:sl * P + m], Kc[0:m, b, sl, kv * P:(kv + 1) * P], ident[0:m, 0:m])
                        tr.then_inc(s["dks_tr"], 1)

                    rows_of(0)
                    rows_of(1)
                    pe.wait_ge(s["qd_done"], 1)
                    for st in range(16):
                        if st + 2 < 16:
                            rows_of(st + 2)
                        pe.wait_ge(s["dks_ev"], st + 1)
                        for g, c0, c1 in OLD:
                            mm = pe.matmul(PS[:, 3 + g, 0:c1 - c0], QZD[:, 2 * g + st % 2, st // 2, :], KTb[:, st % 4, c0:c1], start=st == 0, stop=st == 15)
                        mm.then_inc(s["dss_ready"], 1)
                    pe.wait_ge(s["do_ev"], 16)
                    pe.wait_ge(s["qn_done"], 1)
                    for g in range(GD):
                        for kv in range(KVH):
                            mm = pe.matmul(PS[:, 6, g * NS:(g + 1) * NS], QN[:, 2 * g + kv, :], KTn[:, 2 * g + kv, :], start=kv == 0, stop=kv == 1)
                    mm.then_inc(s["ds_ready"], 1)
                    pe.wait_ge(s["dp_ready"], 17)
                    for sl in range(4):
                        m = P if sl < 3 else 64
                        pe.transpose(PS[0:m, 0, sl * P:(sl + 1) * P], SS[:, 0, sl * P:sl * P + m], ident)
                    for g in range(GD):
                        tr = pe.transpose(PS[0:NS, 1, g * P:(g + 1) * P], SS[:, 0, NEW0 + g * NS:NEW0 + (g + 1) * NS], ident)
                    tr.then_inc(s["dptr"], 1)
                    pe.wait_ge(s["dpt_ev"], 17)
                    pe.wait_ge(s["dv_in"], (2 * NB + NT) * 16)
                    for b in range(NB):
                        for sl in range(4):
                            m = P if sl < 3 else 64
                            pe.matmul(PS[:, 2, 0:256], QZD[0:m, sl, b, :], Kc[0:m, b, sl, :], start=b == 0 and sl == 0, stop=False)
                    for g in range(GD):
                        mm = pe.matmul(PS[:, 2, 0:256], PTn[:, g, :], kvn[:, g * 512 + 256:(g + 1) * 512], start=False, stop=g == GD - 1)
                    mm.then_inc(s["do_ready"], 1)
                    pe.wait_ge(s["do_ev"], 17)
                    for kv in range(KVH):
                        tr = pe.transpose(PS[:, 3, kv * P:(kv + 1) * P], Od[:, kv * P:(kv + 1) * P], ident)
                    tr.then_inc(s["dptr"], 1)
                    pe.wait_ge(s["dil_done"], 1)
                    n.t += 12
                    n.unscaled += 12
                    dense(ph["out", 1], lambda k: H24[:, k, :], lambda k: L24[:, k, :], ready=lambda k: h_ready(k, 12), summed=True)
                ffn(l, 1)
                if l == 0:
                    to_h()
                    wide(ph["kv"], (0, P, 2 * P, 3 * P, T - P))
                    pe.wait_ge(s["blk_evac"], n.blk + 1)
            stats(KD)
            pe.wait_ge(s["t_ready"], n.t - n.unscaled + KD)
            for t in range(NCH + 1):
                rows_ = P if t < NCH else NS
                for h in range(2):
                    m = 2 * t + h
                    if m >= 4:
                        pe.wait_ge(s["f_ev"], m - 3)
                    for k in range(4):
                        tr = pe.transpose(PS[0:rows_, m % 4, k * P:(k + 1) * P], yT[:, 4 * h + k, t * P:t * P + rows_], ident)
                    tr.then_inc(s["f_tr"], 1)

        @block.vector
        def _(dve):
            n = Place()

            def split(u, slot, nk=8, m=None):
                dve.wait_ge(s["w_hi"], u + 1)
                src = raw[:, slot, 0:nk * P] if m is None else rawm[:, m, :]
                dve.tensor_tensor(wlo[:, slot, 0:nk * P], src, whi[:, slot, 0:nk * P].bitcast(F32), ALU.subtract).then_inc(s["w_lo"], 1)

            def inverse(rt=rt):
                dve.wait_ge(s["rt_ready"], n.norm + 1)
                dve.reciprocal(rb[:, :], rt[:, :]).then_inc(s["rb_ready"], 1)
                n.norm += 1
                dve.wait_ge(s["rb_ready"], n.norm)

            def lows(tmp, hi, lo, nk, make):
                for k in range(nk + 2):
                    if k < nk:
                        make(k).then_inc(s["t_ready"], 1)
                    if k >= 2:
                        dve.wait_ge(s["hi_ready"], n.t + k - 1)
                        dve.tensor_tensor(lo(k - 2), tmp(k - 2), hi(k - 2).bitcast(F32), ALU.subtract).then_inc(s["lo_ready"], 1)
                n.t += nk

            def scaled(out, src, g):
                return lambda k: dve.scalar_tensor_tensor(out=out(k), in0=src(k), scalar=g(k), in1=rb[:, :], op0=ALU.mult, op1=ALU.mult)

            def folded_low(k, g):
                dve.wait_ge(s["hi_ready"], n.t + k + 1)
                dve.scalar_tensor_tensor(out=hL[:, k, :], in0=xT[:, k, :], scalar=g(k), in1=hH[:, k, :].bitcast(F32), op0=ALU.mult, op1=ALU.subtract).then_inc(s["lo_ready"], 1)

            def residual(g, g_next=None):
                inverse()
                for k in range(KD + 2):
                    if k < KD:
                        scaled(y_of, y_of, g)(k).then_inc(s["pn_t"], 1)
                    if 1 <= k <= KD:
                        dve.wait_ge(s["pn_t"], n.res + k)
                        dve.tensor_tensor(xT[:, k - 1, :], xT[:, k - 1, :], yT[:, k - 1, :], ALU.add).then_inc(s["x_done"], 1)
                    if k >= 2 and g_next:
                        folded_low(k - 2, g_next)
                n.res += KD
                if g_next:
                    n.t += KD

            dve.wait_ge(s["row_in"], 1)
            dve.tensor_copy(G[:, :], PS[:, 0, 0:P])
            dve.tensor_scalar(GH[:, :], PS[:, 0, 0:P], 0.5, None, ALU.mult)
            dve.tensor_copy(CWT[:, :], PS[:, 0, P:2 * P])
            dve.tensor_copy(CB[:, :], PS[:, 0, 2 * P:2 * P + 48]).then_inc(s["cols_out"], 1)
            dve.wait_ge(s["mem_rt"], 1)
            dve.reciprocal(mst[:, 4:6], mst[:, 2:4]).then_inc(s["mem_rb"], 1)
            dve.wait_ge(s["mem_rb"], 1)
            for t in range(2):
                dve.tensor_scalar(memnat[:, t, :], memnat[:, t, :], mst[:, 4 + t:5 + t], None, ALU.mult).then_inc(s["mem_sc"], 1)
            split(0, 0, m=0)
            dve.wait_ge(s["mem_ev"], KD)
            dve.wait_ge(s["cols_out"], 1)

            def wide(d, nt, deep=False):
                def body(i, last=False):
                    for q in range(4):
                        split(d.u0 + i * 4 + q + 1, (d.u0 + q + 1) % 2, m=(q + 1) % 4 if deep and not (last and q == 3) else None)
                    dve.wait_ge(s["w_mm"], d.u0 + i * 4 + 6)
                    dve.wait_ge(s["stage_free"], i + n.out + 1)
                    for b in range(nt):
                        dve.tensor_copy(stage[:, b, :], PS[:, b, :]).then_inc(s["blk_evac"], 1)
                return body

            for l in range(DEPTH):
                if l:
                    dve.wait_ge(s["w_mm"], ph["mem", l].u0 + 2)
                g = col(104 + KD * l)
                lows(lambda k: yT[:, k, 0:NM], lambda k: hH[:, k, 0:NM], lambda k: hL[:, k, 0:NM], KD,
                     lambda k: dve.tensor_scalar(yT[:, k, 0:NM], memT[:, k, :], g(k), None, ALU.mult))
                body = wide(ph["mem", l], 2, True)
                step_loop(dve, 4 - l, body)
                if l:
                    body(3, True)
                n.out += 4

            def to_h(g):
                inverse()
                lows(y_of, hH_of, hL_of, KD, scaled(y_of, x_of, g))

            def narrow(d, early=0):
                def body(i, early=0):
                    for j in range(2):
                        for q in range(len(d.nks)):
                            u = j * len(d.nks) + q
                            if u >= early:
                                split(d.u0 + i * d.ub + u + 1, (d.u0 + u + 1) % 2, (d.nks * 2 + (8,))[u + 1])
                        dve.wait_ge(s["w_mm"], d.u0 + i * d.ub + (j + 1) * len(d.nks) + 2)
                        dve.tensor_copy(yT[:, bass.ds(2 * i + j, 1), :].rearrange("p o (h t) -> p (o h) t", h=2), PS[:, 2 * j:2 * j + 2, 0:HT]).then_inc(evac[j], 1)
                if early:
                    body(0, early)
                step_loop(dve, d.n, body, early > 0)
                for j in range(2):
                    n.ev[j] += d.n

            def attention(l, meanwhile=None):
                o0 = (16, 4)[l]

                def maxima(h):
                    dve.wait_ge(s["sc_ready"], MH * l + h + 1)
                    b = 4 + 2 * (h % 2)
                    dve.tensor_reduce(am[:, h % 2, :], PS[:, b:b + 2, :].rearrange("p a (r m) -> p (a r) m", r=2), AX_X, ALU.max, negate=True).then_inc(s["mx_ready"], 1)

                maxima(0)
                for h in range(MH):
                    if h + 1 < MH:
                        maxima(h + 1)
                    dve.wait_ge(s["p_exp"], MH * l + h + 1)
                    dve.reciprocal(ai[:, 0, :], ar[:, h % 2, :]).then_inc(s["p_rcp"], 1)
                    dve.wait_ge(s["p_rcp"], MH * l + h + 1)
                    dve.tensor_tensor(Pb[:, :, :], Pb[:, :, :], ai[:, 0, :].unsqueeze(2).to_broadcast([P, NCH, NM]), ALU.mult).then_inc(s["p_ready"], 1)
                    dve.wait_ge(s["pv_ready"], MH * l + h + 1)
                    dve.tensor_copy(M1[:, o0 + 2 * h:o0 + 2 * h + 2, 0:SEQ], PS[:, 2:4, :]).then_inc(s["pv_evac"], 1)
                if meanwhile:
                    meanwhile()
                dve.wait_ge(s["ss_ready"], 16 * l + 16)
                dve.tensor_reduce(am[:, 0, 0:1], PS[:, 4, 0:NM], AX_X, ALU.max, negate=True).then_inc(s["smx"], 1)
                dve.wait_ge(s["s_exp"], l + 1)
                dve.reciprocal(ai[:, 1, 0:1], ar[:, 0, 0:1]).then_inc(s["s_rcp"], 1)
                dve.wait_ge(s["s_rcp"], l + 1)
                dve.tensor_scalar(Pb[:, 0, :], Pb[:, 0, :], ai[:, 1, 0:1], None, ALU.mult).then_inc(s["s_p"], 1)
                dve.wait_ge(s["s_tr"], l + 1)
                dve.wait_ge(s["qz_zero"], 2 * l + 2)
                for t in range(2):
                    z = PZ[:, t, :, :]
                    ins = dve.tensor_copy(bass.AP(z.tensor, z.offset, [list(z.ap[0]), [P + 16, NB], [1, 16]]), PS[:, 5, t * P:(t + 1) * P].rearrange("p (b r) -> p b r", b=NB))
                ins.then_inc(s["pz_ready"], 1)
                dve.wait_ge(s["so_tr"], l + 1)
                for hk in range(8):
                    src = PS[:, hk // 4, (hk % 4) * P:(hk % 4 + 1) * P].rearrange("p (b h t) -> p b h t", b=NB, h=MH)[:, :, hk // 2, :]
                    ins = dve.tensor_copy(M1[:, o0 + hk, SEQ:T].rearrange("p (b t) -> p b t", b=NB), src)
                ins.then_inc(s["att_done"], 1)

            n.res = 0

            def ffn(l, f):
                if f == 0:
                    for k in range(KD):
                        folded_low(k, gain(l, 0))
                    n.t += KD
                inverse(rtf)
                if f == 0:
                    dve.wait_ge(s["stage_free"], 2 * 4 + GD * l + 1)
                d = ph["gu", l, f]
                e0 = list(n.ev)

                def gu(i):
                    for b in range(2):
                        u = d.u0 + i * 4 + 2 * b
                        split(u + 1, (d.u0 + 1) % 2)
                        halves = lambda ap: ap.rearrange("p (h t) -> p h t", h=2)
                        dve.wait_ge(s["w_mm"], u + 3)
                        dve.tensor_tensor(halves(sg[:, b, :]), PS[:, 4 * b:4 * b + 2, 0:HT], halves(rb[:, :]), ALU.mult).then_inc(evac[2 * b], 1)
                        split(u + 2, d.u0 % 2)
                        dve.wait_ge(s["silu_done"], 2 * i + b + n.mid + 1)
                        dve.tensor_tensor(sg[:, b, :], sg[:, b, :], rb[:, :], ALU.mult).then_inc(s["sg_ready"], 1)
                        dve.wait_ge(s["w_mm"], u + 4)
                        dve.wait_ge(s["sg_ready"], 2 * i + b + n.mid + 1)
                        dve.wait_ge(s["mid_lo"], 2 * i + b + n.mid + 1)
                        dve.tensor_tensor(halves(prod[:, b, :]), PS[:, 4 * b + 2:4 * b + 4, 0:HT], halves(sg[:, b, :]), ALU.mult).then_inc(evac[2 * b + 1], 1)
                        dve.wait_ge(s["mid_hi"], 2 * i + b + n.mid + 1)
                        dve.tensor_tensor(L24[:, bass.ds(2 * i + b, 1), :], prod[:, b:b + 1, :], H24[:, bass.ds(2 * i + b, 1), :].bitcast(F32), ALU.subtract).then_inc(s["mid_lo"], 1)
                step_loop(dve, d.n, gu)
                for j in range(4):
                    n.ev[j] += d.n
                n.mid += 2 * d.n
                dn = ph["down", l, f]
                dve.wait_ge(s["mid_lo"], n.mid + 2)

                def down(i, final=False):
                    for j in range(2):
                        for q in range(3):
                            u = 3 * j + q
                            if not (final and u == 5):
                                split(dn.u0 + i * 6 + u + 1, (dn.u0 + u + 1) % 2, (dn.nks * 2 + (8,))[u + 1])
                        dve.wait_ge(s["w_mm"], dn.u0 + i * 6 + 3 * j + 5)
                        dve.tensor_copy(yT[:, bass.ds(2 * i + j, 1), :].rearrange("p o (h t) -> p (o h) t", h=2), PS[:, 2 * j:2 * j + 2, 0:HT]).then_inc(evac[j], 1)
                if (l, f) == (DEPTH - 1, 1):
                    step_loop(dve, dn.n - 1, down)
                    down(dn.n - 1, True)
                else:
                    step_loop(dve, dn.n, down)
                for j in range(2):
                    n.ev[j] += dn.n
                residual(half_gain(l, 4 * f + 1), gain(1, 2) if (l, f) == (1, 0) else None)

            for l in range(DEPTH):
                ffn(l, 0)
                if l == 0:
                    to_h(gain(0, 2))
                    u0 = ph["dt"].u0
                    split(u0 + 1, (u0 + 1) % 2)
                    n.ev[0] += 1
                    st = Steps(dve, s["dt_v"], 0)
                    dve.wait_ge(s["dt_e"], 2)
                    dve.tensor_scalar(dts[:, 3, :], dts[:, 2, :], 1.0, None, ALU.add).then_inc(s["dt_u"], 1)
                    dve.wait_ge(s["dt_u"], 1)
                    st(dve.tensor_scalar(dts[:, 1, :], dts[:, 3, :], -1.0, None, ALU.add))
                    st(dve.reciprocal(dts[:, 5, :], dts[:, 3, :]))
                    st.wait()
                    st(dve.tensor_tensor(dts[:, 1, :], dts[:, 2, :], dts[:, 1, :], ALU.subtract))
                    st.wait()
                    st(dve.tensor_tensor(dts[:, 1, :], dts[:, 1, :], dts[:, 5, :], ALU.mult))
                    dve.wait_ge(s["dt_ln"], 1)
                    st.wait()
                    st(dve.tensor_tensor(dts[:, 1, :], dts[:, 1, :], dts[:, 4, :], ALU.add))
                    st.wait()
                    st(dve.scalar_tensor_tensor(out=dtx[:, :], in0=dts[:, 0, :], scalar=0.0, in1=dts[:, 1, :], op0=ALU.max, op1=ALU.add))
                    dve.wait_ge(s["na_ready"], 1)
                    st(dve.tensor_scalar(nA[:, :], nA[:, :], -1.0, None, ALU.mult))
                    st.wait()
                    st(dve.tensor_scalar(dts[:, 2, :], dtx[:, :], nA[:, 0:1], None, ALU.mult))
                    st.wait()
                    dve.wait_ge(s["conv_in"], 32)
                    st(dve.tensor_tensor_scan(acum[:, :], reset[:, :], dts[:, 2, :], 0.0, ALU.mult, ALU.add))
                    st.wait()
                    dve.tensor_copy(tmpL[:, :].rearrange("p (b t) -> p b t", b=NB), acum[:, SEQ + NT - 1:T:NT].unsqueeze(2).to_broadcast([NH, NB, NT])).then_inc(s["scan_done"], 1)
                    for t in (aT, dT, CD):
                        st(dve.memset(t[:, NCH, :], 0.0))
                    dve.wait_ge(s["dtt_tr"], 1)
                    st.wait()
                    for m, c0, c1 in ((P, 0, NCH), (NS, NCH, NCH + 1)):
                        w = slice(c0 * NH, c1 * NH)
                        for q, dst in enumerate((aT, dT, CD)):
                            st(dve.tensor_copy(dst[0:m, c0:c1, :].rearrange("p c h -> p (c h)"), PS[0:m, 0, q * 160 + w.start:q * 160 + w.stop]))
                    st.wait()
                    dve.tensor_tensor(DE[:, :, :], CD[:, :, :], aT[:, :, :], ALU.subtract).then_inc(s["alb_sub"], 1)
                    dve.wait_ge(s["hist_tr"], 1)
                    dve.tensor_copy(hist[:, :, :].rearrange("p (a c) k -> p a (c k)", a=2), PS[:, 2:4, 0:16 * 24]).then_inc(s["hist_copied"], 1)
                    dve.wait_ge(s["hist_copied"], 1)
                    dve.wait_ge(s["de_done"], 1)
                    d = ph["ssd"]
                    split(d.u0 + 1, (d.u0 + 1) % 2)
                    cw5 = CWB[:, 0:(CW + 1) * 32].rearrange("p (w c) -> p w c", w=CW + 1)

                    def group(g):
                        st = Steps(dve, s["ve"], g * VE)
                        dve.wait_ge(s["group_end"], g + 1)
                        split(d.u0 + g * 6 + 2, d.u0 % 2)
                        for ti, nt in ((0, 1), (1, 1), (2, 2)):
                            dve.tensor_copy(cwg[:, ti:ti + nt, 0:CW + 1], cw5[:, :, bass.ds(CT(g)[ti], nt)].rearrange("p w t -> p t w"))
                        hs = bass.ds(g * 4, 4)
                        dve.tensor_copy(tokg[:, :, :, :], tokc[:, :, :, hs])
                        dve.tensor_copy(EASg[:, :], EAS[:, hs])
                        dve.tensor_copy(DCg[:, :], DC[:, bass.ds(g * 2, 2)])
                        dve.tensor_copy(selg[:, :], con[0:NH, hs])
                        dve.tensor_copy(selp[:, :, :], con[0:NH, hs].unsqueeze(2).to_broadcast([NH, 4, PD])).then_inc(s["col_g"], 1)
                        dve.wait_ge(s["col_g"], g + 1)

                        def history(ti, ct):
                            if ti >= 2:
                                dve.wait_ge(s["taps"], g * 4 + ti - 2 + 1 + 2)
                                dve.wait_ge(s["cvn_done"], g * 4 + ti - 2 + 1 + 2)
                            dve.tensor_copy(pres[:, ti % 2, :, 0:CW - 1], hist[:, bass.ds(ct, 1), :].rearrange("p o (b r) -> p (o b) r", b=NB)).then_inc(s["hist_g"], 1)

                        cts = CT(g)
                        history(0, cts[0])
                        history(1, cts[1])
                        for j in range(6):
                            if j:
                                split(d.u0 + g * 6 + j + 2, (d.u0 + j) % 2)
                            if j >= 4:
                                continue
                            b = j % 2
                            dve.wait_ge(s["tap0"], g * 4 + j + 1)
                            for w in range(1, CW):
                                st(dve.scalar_tensor_tensor(out=xbc[:, j, 0:SEQ], in0=pre[:, b, w:w + SEQ], scalar=cwg[:, j, w:w + 1], in1=xbc[:, j, 0:SEQ], op0=ALU.mult, op1=ALU.add))
                                xs = xbc[:, j, SEQ:T].rearrange("p (b t) -> p b t", b=NB)
                                ins = dve.scalar_tensor_tensor(out=xs, in0=pres[:, b, :, w:w + NT], scalar=cwg[:, j, w:w + 1], in1=xs, op0=ALU.mult, op1=ALU.add)
                                if w < CW - 1:
                                    st(ins)
                                    st.wait()
                                else:
                                    ins.then_inc(s["taps"], 1)
                            if j < 2:
                                history(j + 2, cts[j + 2])
                        dve.wait_ge(s["tok_ready"], g + 1)
                        st(dve.tensor_copy(btok[0:NS, NCH, :], PS[0:NS, 5, 0:P]))
                        heads = lambda t, m, c0, c1: t[0:m, c0:c1, :].unsqueeze(3).to_broadcast([m, c1 - c0, 4, PD])
                        four = lambda ap: ap.rearrange("p c (h w) -> p c h w", h=4)
                        st(dve.tensor_tensor(xd[0:NS, NCH, :].rearrange("p (h w) -> p h w", h=4), PS[0:NS, 5, P:P + 256].rearrange("p (h w) -> p h w", h=4), dTg[0:NS, NCH, :].unsqueeze(2).to_broadcast([NS, 4, PD]), ALU.mult))
                        st(dve.tensor_tensor(cbm[0:NS, SEQ:T], PS[0:NS, 5, 384:384 + NS], small, ALU.mult))
                        dve.tensor_copy(cds[:, :], PS[:, 5, 416:432]).then_inc(s["small_read"], 1)
                        for k in range(2):
                            ins = dve.tensor_tensor(four(xd[:, 2 * k:2 * k + 2, :]), PS[:, 6 + k, :].rearrange("p (c h w) -> p c h w", c=2, h=4), heads(dTg, P, 2 * k, 2 * k + 2), ALU.mult)
                        ins.then_inc(s["xd_ready"], 1)
                        dve.wait_ge(s["xd_ready"], g + 1)
                        st.wait()
                        dve.tensor_tensor(xdd[0:NS, NCH, :].rearrange("p (h w) -> p h w", h=4), xd[0:NS, NCH, :].rearrange("p (h w) -> p h w", h=4), DEg[0:NS, NCH, :].unsqueeze(2).to_broadcast([NS, 4, PD]), ALU.mult)
                        dve.tensor_tensor(four(xdd[:, 0:NCH, :]), four(xd[:, 0:NCH, :]), heads(DEg, P, 0, NCH), ALU.mult).then_inc(s["xdd_ready"], 1)
                        dve.wait_ge(s["cb_ready"], g + 1)
                        dve.tensor_tensor(cbm[:, 0:SEQ].rearrange("p (c t) -> p c t", c=NCH), PS[:, 0, :].rearrange("p (c t) -> p c t", c=NCH), causal.unsqueeze(1).to_broadcast([P, NCH, P]), ALU.mult).then_inc(s["cbm_ready"], 1)
                        dve.wait_ge(s["bcs_ready"], g + 1)
                        dve.tensor_copy(bcsS[:, :, :].rearrange("p h t -> p (h t)"), PS[0:NS, 5, 0:QH * NS]).then_inc(s["bcs_read"], 1)
                        dve.wait_ge(s["bcs_read"], g + 1)

                        def seg(h):
                            dve.wait_ge(s["bc_read"], g * 4 + h + 1)
                            if h >= 2:
                                dve.wait_ge(s["y_used"], g * 4 + h - 1)
                            dve.tensor_scalar(Lh[0:NS, h % 2, SEQ:T], bcsS[:, h, :], aTg[0:NS, NCH, h:h + 1], 0.0, ALU.subtract, ALU.min)
                            for c in range(NCH):
                                ins = dve.tensor_scalar(Lh[:, h % 2, c * P:(c + 1) * P], bcS[:, h % 2, c * P:(c + 1) * P], aTg[:, c, h:h + 1], 0.0, ALU.subtract, ALU.min)
                            ins.then_inc(s["seg_ready"], 1)

                        def masked(h):
                            dve.wait_ge(s["lexp"], g * 4 + h + 1)
                            dve.tensor_tensor(Lh[0:NS, h % 2, SEQ:T], Lh[0:NS, h % 2, SEQ:T], cbm[0:NS, SEQ:T], ALU.mult)
                            dve.tensor_tensor(Lh[:, h % 2, 0:SEQ], Lh[:, h % 2, 0:SEQ], cbm[:, 0:SEQ], ALU.mult).then_inc(s["m_ready"], 1)

                        seg(0)
                        dve.wait_ge(s["st_ready"], g + 1)
                        st(dve.tensor_copy(ST[:, 0, :], PS[:, 2, 0:256]))
                        st.wait()
                        for c in range(1, NCH):
                            st(dve.tensor_tensor(tmpS[:, :].rearrange("p (h w) -> p h w", h=4), ST[:, c - 1, :].rearrange("p (h w) -> p h w", h=4), CDg[:, c, :].unsqueeze(2).to_broadcast([P, 4, PD]), ALU.mult))
                            st.wait()
                            ins = dve.tensor_tensor(ST[:, c, :], tmpS[:, :], PS[:, 2 + c // 2, (c % 2) * 256:(c % 2 + 1) * 256], ALU.add)
                            if c < NCH - 1:
                                st(ins)
                                st.wait()
                            else:
                                ins.then_inc(s["st_done"], 1)
                        masked(0)
                        seg(1)
                        masked(1)
                        seg(2)
                        masked(2)
                        seg(3)
                        masked(3)
                        dve.wait_ge(s["yoff_ready"], g + 1)
                        dve.tensor_tensor(yos[:, :].rearrange("p (h w) -> p h w", h=4), PS[0:NS, 4, 0:256].rearrange("p (h w) -> p h w", h=4), EASg[:, :].unsqueeze(2).to_broadcast([NS, 4, PD]), ALU.mult).then_inc(s["yos_ready"], 1)

                        def new_states(q):
                            if q == 0:
                                dve.wait_ge(s["cds_exp"], g + 1)
                            dve.wait_ge(s["nst_free"], g * 2 + q + 1)
                            st(dve.tensor_tensor(nst[:, :, :], S0[:, q], cds[:, q * NB:(q + 1) * NB].unsqueeze(2).to_broadcast([P, NB, P]), ALU.mult))
                            st.wait()
                            dve.wait_ge(s["news_ready"], g * 2 + q + 1)
                            flat = nst[:, :, :].rearrange("p (a b) n -> p a (b n)", a=2)
                            dve.tensor_tensor(flat, flat, PS[:, 6:8, :], ALU.add).then_inc(s["news_read"], 1)

                        new_states(0)
                        new_states(1)
                        dve.wait_ge(s["y_ready"], g + 1)
                        dve.wait_ge(s["y_used"], g * 4 + 4)
                        for q in range(2):
                            st(dve.scalar_tensor_tensor(out=xbc[:, 2 + q, SEQ:T], in0=xbc[:, 2 + q, SEQ:T], scalar=DCg[:, q:q + 1], in1=PS[:, 5, 128 + q * NS:128 + (q + 1) * NS], op0=ALU.mult, op1=ALU.add))
                            st(dve.scalar_tensor_tensor(out=xbc[:, 2 + q, 0:SEQ], in0=xbc[:, 2 + q, 0:SEQ], scalar=DCg[:, q:q + 1], in1=PS[:, 2 + q, :], op0=ALU.mult, op1=ALU.add))
                        st.wait()
                        for q in range(2):
                            ins = dve.tensor_tensor(xbc[:, 2 + q, SEQ:T], xbc[:, 2 + q, SEQ:T], PS[:, 5, 192 + q * NS:192 + (q + 1) * NS], ALU.add)
                        ins.then_inc(s["y_read"], 1)
                        dve.wait_ge(s["y_read"], g + 2)
                        for q in range(2):
                            st(dve.tensor_tensor(M1[:, bass.ds(g * 2 + q, 1), :].rearrange("p o t -> p (o t)"), xbc[:, 2 + q, :], sz[:, q, :], ALU.mult))
                        st.wait()
                        dve.sem_inc(s["group_end"], 1)
                        assert st.n == VE, st.n
                    step_loop(dve, NG, group)
                    n.ev = [n.ev[0] + 2 * NG, n.ev[1] + 2 * NG, n.ev[2] + NG, n.ev[3] + NG]
                    d = ph["qm", 0]

                    def queries(d, early=0, dst=None, first=0, scale=MD ** -0.5, pos=(0, 1)):
                        def body(i, early=0):
                            for j in range(early, 2):
                                split(d.u0 + i * 2 + j + 1, (d.u0 + j + 1) % 2)
                            for j in range(2 if dst else 0):
                                dve.wait_ge(s["w_mm"], d.u0 + i * 2 + j + 3)
                                dve.scalar_tensor_tensor(out=dst[:, bass.ds(2 * i + (j + first), 1), :].rearrange("p o (h t) -> p (o h) t", h=2), in0=PS[:, 2 * j:2 * j + 2, 0:HT],
                                                         scalar=scale, in1=rb[:, :].rearrange("p (h t) -> p h t", h=2), op0=ALU.mult, op1=ALU.mult).then_inc(evac[j], 1)
                        if early:
                            body(0, early)
                        step_loop(dve, d.n, body, early)
                        for j in pos:
                            n.ev[j] += d.n
                    queries(d, 1, pos=QPOS)
                    dve.wait_ge(s["rt_ready"], n.norm + 1)
                    dve.sem_inc(s["att_go"], 1)
                    inverse()

                    def gated_norm():
                        for k in range(KI):
                            dve.scalar_tensor_tensor(out=M1[:, k, :], in0=M1[:, k, :], scalar=CB[:, 32 + k:33 + k], in1=rb[:, :], op0=ALU.mult, op1=ALU.mult).then_inc(s["t_ready"], 1)
                    attention(0, gated_norm)
                    d = ph["out", 0]
                    for k in range(24):
                        dve.wait_ge(s["hi_ready"], n.t + k + 1)
                        dve.tensor_tensor(L24[:, k, :], M1[:, k, :], H24[:, k, :].bitcast(F32), ALU.subtract).then_inc(s["lo_ready"], 1)
                        if k in (8, 20):
                            u = d.u0 + 1 + k // 20
                            split(u, u % 2, 8)
                    n.t += 24
                    narrow(d, 2)
                    residual(gain(0, 3), gain(0, 4))
                else:
                    inverse(rtf)
                    queries(ph["in_b"], dst=M1, first=12, scale=HD ** -0.5)
                    queries(ph["qm", 1], dst=yT)
                    for j in range(2):
                        dve.wait_ge(evac[j], n.ev[j] + 1)
                    dve.sem_inc(s["att_go"], 1)
                    attention(1)

                    def soften(t):
                        dve.wait_ge(s["ds_ev"], t + 1)
                        n_ = sum(n for _, _, n in spans(t % NCH)) if t < 16 else NEW0 + GD * NS
                        dve.tensor_reduce(dm[:, t % 2:t % 2 + 1], SS[:, t % 2, 0:n_], AX_X, ALU.max, negate=True).then_inc(s["dmx"], 1)

                    def biased(t):
                        h, i = t // NCH, t % NCH
                        dve.wait_ge(s["ds_ready"], t + 1)
                        if t >= 2:
                            dve.wait_ge(s["dptr"], t - 1)
                        c = 0
                        for g, first, n_ in spans(i):
                            ins = dve.scalar_tensor_tensor(out=SS[:, t % 2, c:c + n_], in0=tab[:, (g + 1) * SEQ - n_:(g + 1) * SEQ], scalar=-SLOPES[g][h], in1=PS[:, g, 0:n_], op0=ALU.mult, op1=ALU.add)
                            c += n_
                        ins.then_inc(s["ds_ev"], 1)
                        soften(t)

                    def divided(t):
                        n_ = sum(n for _, _, n in spans(t % NCH)) if t < 16 else NEW0 + GD * NS
                        b = t % 2
                        dve.wait_ge(s["dexp"], t + 1)
                        dve.reciprocal(di[:, b:b + 1], dr[:, b:b + 1]).then_inc(s["drcp"], 1)
                        dve.wait_ge(s["drcp"], t + 1)
                        dve.tensor_scalar(SS[:, b, 0:n_], SS[:, b, 0:n_], di[:, b:b + 1], None, ALU.mult).then_inc(s["dp_ready"], 1)

                    biased(0)
                    for t in range(16):
                        if t + 1 < 16:
                            biased(t + 1)
                        divided(t)
                    dve.wait_ge(s["do_ready"], 16)
                    dve.wait_ge(s["qs_zero"], 1)
                    dve.memset(QZD[:, GD:, :, :], 0.0).then_inc(s["qs_zero"], 1)
                    dve.wait_ge(s["ds_ready"], 17)
                    dve.wait_ge(s["dptr"], 16)
                    for g, c0, c1 in OLD:
                        dve.scalar_tensor_tensor(out=SS[:, 0, c0:c1], in0=tab[:, GD * SEQ + c0:GD * SEQ + c1], scalar=negc[:, g:g + 1], in1=PS[:, 3 + g, 0:c1 - c0], op0=ALU.mult, op1=ALU.add)
                    for g in range(GD):
                        c0 = NEW0 + g * NS
                        ins = dve.scalar_tensor_tensor(out=SS[:, 0, c0:c0 + NS], in0=tab[:, GD * SEQ + c0:GD * SEQ + c0 + NS], scalar=negc[:, g:g + 1], in1=PS[:, 6, g * NS:(g + 1) * NS], op0=ALU.mult, op1=ALU.add)
                    ins.then_inc(s["ds_ev"], 1)
                    soften(16)
                    divided(16)
                    dve.wait_ge(s["dptr"], 17)
                    for sl in range(4):
                        m = P if sl < 3 else 64
                        z = QZD[0:m, sl]
                        dve.tensor_copy(bass.AP(z.tensor, z.offset, [list(z.ap[0]), [P + 16, NB], [1, 16]]), PS[0:m, 0, sl * P:(sl + 1) * P].rearrange("p (b r) -> p b r", b=NB))
                    dve.tensor_copy(PTn[:, :, :].rearrange("p g r -> p (g r)"), PS[0:NS, 1, 0:GD * P]).then_inc(s["dpt_ev"], 1)
                    dve.wait_ge(s["dptr"], 18)
                    for h in range(QH):
                        src = PS[:, 3, (h // 2) * P:(h // 2 + 1) * P].rearrange("p (b h t) -> p b h t", b=NB, h=QH)[:, :, h, :]
                        ins = dve.tensor_copy(M1[:, h, SEQ:T].rearrange("p (b t) -> p b t", b=NB), src)
                    ins.then_inc(s["dil_done"], 1)
                    for k in range(12):
                        dve.wait_ge(s["hi_ready"], n.t + k + 1)
                        dve.tensor_tensor(L24[:, k, :], M1[:, k, :], H24[:, k, :].bitcast(F32), ALU.subtract).then_inc(s["lo_ready"], 1)
                        if k == 6:
                            split(ph["out", 1].u0 + 1, (ph["out", 1].u0 + 1) % 2, 6)
                    n.t += 12
                    narrow(ph["out", 1], 1)
                    residual(gain(1, 3), gain(1, 4))
                ffn(l, 1)
                if l == 0:
                    to_h(col(96))
                    body = wide(ph["kv"], NCH + 1)
                    for i in range(GD):
                        n.out = 8
                        body(i)
            inverse()
            for k in range(KD):
                scaled(y_of, x_of, col(120))(k).then_inc(s["t_ready"], 1)

        @block.gpsimd
        def _(pool):
            n = Place()
            mk = O["mem_kv"].rearrange("l a (t p) c h d -> l p (a t) (c h d)", p=P)
            blocks = stores = 0

            def stored(k):
                nonlocal stores
                stores += k
                pool.wait_ge(s["blk_out"], 16 * stores)
                pool.nop().then_inc(s["stage_free"], 1)

            for l in range(DEPTH):
                for i in range(4):
                    blocks += 2
                    pool.wait_ge(s["blk_evac"], blocks + 1)
                    pool.dma_start(mk[l, :, :, i * 512:(i + 1) * 512], stage[:, 0:2, :]).then_inc(s["blk_out"], 16)
                    stored(1)

            def kv_out():
                nonlocal blocks
                for g in range(GD):
                    blocks += NCH + 1
                    pool.wait_ge(s["blk_evac"], blocks + 1)
                    c = slice(g * 512, (g + 1) * 512)
                    w = O[f"win_p{g}"].rearrange("a r c h d -> (a r) (c h d)")
                    pool.dma_start(kvs[0:SEQ, c].rearrange("(t p) c -> p t c", p=P), stage[:, 0:NCH, :]).then_inc(s["blk_out"], 16)
                    pool.dma_start(kvs[SEQ:T, c], stage[P - NS:P, NCH, :]).then_inc(s["blk_out"], 16)
                    pool.dma_start(O[f"win_s{g}"].rearrange("b t c h d -> (b t) (c h d)"), stage[P - NS:P, NCH, :]).then_inc(s["blk_out"], 16)
                    if g == 0:
                        pool.dma_start(w, stage[:, NCH - 1, :]).then_inc(s["blk_out"], 16)
                    else:
                        pool.dma_start(w.rearrange("(t p) c -> p t c", p=P), stage[:, 0:NCH, :]).then_inc(s["blk_out"], 16)
                    stored(4)
            def y_sums():
                def add(t, slot):
                    pool.wait_ge(s["sq_ready"], t + 1)
                    pool.wait_ge(s["sq_used"], t + 2)
                    pool.tensor_tensor(acc[:, :], acc[:, :], sqb[:, slot, :], ALU.add).then_inc(s["sq_used"], 1)

                pool.wait_ge(s["sq_ready"], n.sq + 1)
                pool.wait_ge(s["sq_used"], n.sq + 2)
                pool.tensor_copy(acc[:, :], sqb[:, 0, :]).then_inc(s["sq_used"], 1)

                def body(i):
                    add(2 * i + n.sq + 1, 1)
                    add(2 * i + n.sq + 2, 0)
                step_loop(pool, KD // 2 - 1, body)
                n.sq += KD

            mkc = A["cache_mem_kv"].rearrange("l b (t p) c h d -> l b p t c (h d)", p=P)
            kv_in = [s["kv_in0"], s["kv_in1"], s["kv_in2"]]

            def attention_loads(l, q, norms=0):
                order = [(None, 0), (None, 1)] + [(b, c) for c in range(2) for b in range(NB)]
                for idx, (b, c) in enumerate(order):
                    if idx >= 3:
                        what, last = [("kt_tr", l + 1), ("pv_ready", MH * (l + 1))][idx - 3] if idx < 5 else \
                            ("ks_tr", 16 * l + 2 * (idx - 4)) if idx < 13 else ("vb_done", NB * l + idx - 12)
                        pool.wait_ge(s[what], last)
                    src = mk[l].rearrange("p t (c n) -> p t c n", c=2)[:, :, c, :] if b is None else mkc[l, b][:, :, c, :]
                    pool.dma_start(kvr[:, idx % 3], src).then_inc(kv_in[idx % 3], 16)
                    if idx == 2:
                        pool.wait_ge(s["att_go"], l + 1)
                        if norms:
                            pool.wait_ge(s["rb_ready"], norms)
                        pool.memset(QZ[:, :, :, :], 0.0).then_inc(s["qz_zero"], 1)
                        pool.memset(PZ[:, :, :, :], 0.0).then_inc(s["qz_zero"], 1)
                        pool.wait_ge(s["qz_zero"], 2 * l + 2)
                        for hk in range(8):
                            z = QZ[:, hk, :, :]
                            dst = bass.AP(z.tensor, z.offset + (hk // 2) * NT, [list(z.ap[0]), [P + 16, NB], [1, NT]])
                            pool.tensor_copy(dst, q[:, hk, SEQ:T].rearrange("p (b t) -> p b t", b=NB)).then_inc(s["q_ready"], 1)

            def ffn():
                n.sq += KD
                y_sums()

            ffn()
            n.sq += KD
            cpo = O["conv_p"].rearrange("a b r c -> (a b r) c")
            cso = O["conv_s"].rearrange("a b r c -> (a b r) c")
            spo = O["ssm_p"].rearrange("a b (g q r) p n -> g (a b r p) q n", g=NG, q=2)
            sso_s = O["ssm_s"].rearrange("a b (g q r) p n -> g q (r p) (a b) n", g=NG, q=2)
            pool.wait_ge(s["alb_sub"], 1)
            pool.memset(CZ[:, :, :], 0.0).then_inc(s["pz"], 1)
            pool.memset(pre[:, :, 0:CW - 1], 0.0).then_inc(s["pz"], 1)
            pool.wait_ge(s["pz"], 2)

            def group(g):
                pool.wait_ge(s["group_end"], g + 1)
                for ti in range(4):
                    b = ti % 2
                    pool.wait_ge(s["tap0"], g * 4 + ti + 1)
                    pool.sem_inc(s["passed"], 1)
                    pool.tensor_copy(cvn[:, ti, 0:3], pre[:, b, SEQ:SEQ + CW - 1])
                    pool.tensor_copy(cvn[:, ti, 3:27].rearrange("p (b r) -> p b r", b=NB), pres[:, b, :, NT:NT + CW - 1]).then_inc(s["cvn_done"], 1)
                pool.wait_ge(s["conv_done"], g * 4 + 4)
                pool.sem_inc(s["passed"], 1)
                cz = CZ[:, :, :]
                pool.tensor_copy(bass.AP(cz.tensor, cz.offset, [list(cz.ap[0]), [NS + NT, NB], [1, NT]]), xbc[:, 1, SEQ:T].rearrange("p (b t) -> p b t", b=NB)).then_inc(s["cz_ready"], 1)
                pool.wait_ge(s["small_read"], g + 1)
                pool.tensor_tensor(BZ[:, :, :], btok[0:NS, NCH, :].unsqueeze(1).to_broadcast([NS, NB, P]), own.unsqueeze(2).to_broadcast([NS, NB, P]), ALU.mult).then_inc(s["bz_ready"], 1)
                for h in range(4):
                    pool.wait_ge(s["bc_read"], g * 4 + h + 1)
                    pool.tensor_tensor(Eh[:, h % 2, :], Eh[:, h % 2, :], xbc[:, 1, 0:SEQ], ALU.mult).then_inc(s["c_ready"], 1)
                    if h == 1:
                        pool.wait_ge(s["cvo_done"], g + 1)
                        pool.sem_inc(s["passed"], 1)
                        for t, c in enumerate((D * 2 + g * P, D * 3 + g * P, g * 256)):
                            w = P if t < 2 else 256
                            src = cvo[:, t:t + 1 + (t == 2), :].rearrange("p a c -> p (a c)")
                            pool.dma_start(cpo[:, bass.ds(c, w)], src[0:3]).then_inc(s["group_out"], 16)
                            pool.dma_start(cso[:, bass.ds(c, w)], src[3:27]).then_inc(s["group_out"], 16)
                for q in range(2):
                    pool.wait_ge(s["news_read"], g * 2 + q + 2)
                    pool.sem_inc(s["passed"], 1)
                    pool.dma_start(sso_s[bass.ds(g, 1), q].rearrange("o p b n -> p (o b) n"), nst[:, :, :]).then_inc(s["news_out"], 16)
                    pool.wait_ge(s["news_out"], g * 32 + q * 16 + 16)
                    pool.sem_inc(s["nst_free"], 1)
                pool.wait_ge(s["final_read"], g + 1)
                pool.sem_inc(s["passed"], 1)
                pool.dma_start(spo[bass.ds(g, 1)].rearrange("o p q n -> p (o q) n"), sso[:, :, :]).then_inc(s["group_out"], 16)
                pool.wait_ge(s["group_out"], g * 112 + 112)
                pool.sem_inc(s["rest_out"], 1)
            step_loop(pool, NG, group)
            pool.wait_ge(s["group_end"], NG + 1)
            attention_loads(0, yT, 4)
            n.sq += KI
            y_sums()
            ffn()
            n.sq += KD
            kv_out()
            ffn()
            n.sq += KD
            pool.wait_ge(s["w_mm"], ph["in_b"].u0 + 2)
            attention_loads(1, yT)
            pool.wait_ge(s["ss_ready"], 32)
            pool.dma_start(kvd[:, :, :], kvs[0:SEQ, :].rearrange("(t p) c -> p t c", p=P)).then_inc(s["dil_in"], 16)
            pool.dma_start(tab[:, :], A["c_dil"]).then_inc(s["dil_in"], 16)
            pool.dma_start(kvn[:, :], kvs[SEQ:T, :]).then_inc(s["dil_in"], 16)
            pool.wait_ge(s["att_done"], 2)
            win = [A[f"cache_win_g{g + 1}"].rearrange("b e c h d -> b e c (h d)") for g in range(GD)]

            def far_rows(c):
                w = win[2]
                for r in range(NT):
                    src = bass.AP(w.tensor, w.offset + r * 512 + c * 256, [[DILS[2][1] * 512, 16], [256 * 512, NB], [1, 256]])
                    pool.dma_start(Kc[r * 16:(r + 1) * 16, :, 3, :], src).then_inc(s[("dks_in", "dv_in")[c]], 16)

            pool.dma_start(Kc[:, :, 0, :], win[0][:, :, 0, :].rearrange("b p n -> p b n")).then_inc(s["dks_in"], 16)
            for t in range(2):
                pool.dma_start(Kc[:, :, 1 + t, :], win[1][:, t * P:(t + 1) * P, 0, :].rearrange("b p n -> p b n")).then_inc(s["dks_in"], 16)
            far_rows(0)

            def sample_queries(dst, batch_step, done):
                for g in range(GD):
                    for kv in range(KVH):
                        z = dst[:, 2 * g + kv]
                        q = M1[:, 12 + g * QH + 2 * kv:12 + g * QH + 2 * kv + 2, SEQ:T]
                        for h in range(2):
                            ins = pool.tensor_copy(bass.AP(z.tensor, z.offset + (2 * kv + h) * NT, [list(z.ap[0]), [batch_step, NB], [1, NT]]),
                                                   q[:, h, :].rearrange("p (b t) -> p b t", b=NB))
                ins.then_inc(s[done], 1)

            pool.memset(QN[:, :, :], 0.0).then_inc(s["qs_zero"], 1)
            pool.wait_ge(s["qs_zero"], 1)
            sample_queries(QN, 16, "qn_done")
            pool.wait_ge(s["do_ready"], 16)
            pool.memset(QZD[:, 0:GD, :, :], 0.0).then_inc(s["qs_zero"], 1)
            pool.wait_ge(s["qs_zero"], 3)
            sample_queries(QZD, P + 16, "qd_done")
            for b in range(NB):
                pool.wait_ge(s["dks_tr"], 2 * b + 2)
                pool.dma_start(Kc[:, b, 0, :], win[0][b, :, 1, :]).then_inc(s["dv_in"], 16)
                pool.dma_start(Kc[:, b, 1:3, :], win[1][b, :, 1, :].rearrange("(t p) n -> p t n", p=P)).then_inc(s["dv_in"], 16)
            far_rows(1)
            y_sums()
            ffn()


_OUTS = [("y_prompt", (1, SEQ, D)), ("y_sample", (NB, NT, D)), ("mem_kv", (DEPTH, 1, NM, 2, MH, MD)),
         ("ssm_p", (1, 1, NH, PD, P)), ("conv_p", (1, 1, CW - 1, CONV_DIM)),
         ("win_p0", (1, P, 2, KVH, HD)), ("win_p1", (1, SEQ, 2, KVH, HD)), ("win_p2", (1, SEQ, 2, KVH, HD)),
         ("ssm_s", (1, NB, NH, PD, P)), ("conv_s", (1, NB, CW - 1, CONV_DIM)),
         ("win_s0", (NB, NT, 2, KVH, HD)), ("win_s1", (NB, NT, 2, KVH, HD)), ("win_s2", (NB, NT, 2, KVH, HD))]


def kernel(**inputs):
    import numpy as _np
    import concourse.bacc as _bacc
    from concourse import mybir as _mybir
    from concourse.bass_utils import run_bass_kernel_spmd as _run

    nc = _bacc.Bacc("TRN2", target_bir_lowering=False, num_devices=1)
    given = {name: _np.ascontiguousarray(a) for name, a in inputs.items()}
    given["c_base"], given["c_dil"], given["c_reset"] = constants()
    arrays, ins, outs = {}, {}, {}
    for name, a in given.items():
        arrays[f"in_{name}"] = a
        ins[name] = nc.dram_tensor(f"in_{name}", a.shape, _mybir.dt.from_np(a.dtype), kind="ExternalInput").ap()
    for name, shape in _OUTS:
        outs[name] = nc.dram_tensor(f"out_{name}", shape, _mybir.dt.float32, kind="ExternalOutput").ap()
    build_trunk(nc, ins, outs)
    r = _run(nc, [arrays], core_ids=[0])
    return tuple(r.results[0][f"out_{name}"] for name, _ in _OUTS)
```
